# Optimizing a Trainium2 kernel written in Bass

```python
import jax, jax.numpy as jnp
from jax import lax
import numpy as np

D_MODEL = 1024
BATCH = 1
SEQ = 256
DEPTH = 2

HEAD_DIM = 64
ROPE_THETA = 10000.0
EPS = 1e-6
Q_BLOCK = 128

A_HEADS = 4
MOBA_BLOCK = 256
MOBA_TOPK = 3
B_HEADS = 8
B_KV_HEADS = 2
WINDOW = 128
C_HEADS = 4
C_HALF = HEAD_DIM // 2

N_BRANCH = 3
D_FF = 2816
CONV_W = 3

A_W = A_HEADS * HEAD_DIM
B_QW = B_HEADS * HEAD_DIM
B_KVW = B_KV_HEADS * HEAD_DIM
C_W = C_HEADS * HEAD_DIM
IN_SIZES = (A_W, A_W, A_W, B_QW, B_KVW, B_KVW, C_W, C_W, C_W, N_BRANCH * D_MODEL)
IN_COLS = sum(IN_SIZES)
SPLIT_POINTS = tuple(np.cumsum(IN_SIZES)[:-1].tolist())


def rms_norm(x, g):
    x32 = x.astype(jnp.float32)
    y = x32 * lax.rsqrt(jnp.mean(x32 * x32, axis=-1, keepdims=True) + EPS)
    return (y * g.astype(jnp.float32)).astype(x.dtype)

def rope_tables(seq, dim):
    inv = 1.0 / (ROPE_THETA ** (jnp.arange(0, dim, 2, dtype=jnp.float32) / dim))
    ang = jnp.arange(seq, dtype=jnp.float32)[:, None] * inv[None, :]
    return jnp.cos(ang), jnp.sin(ang)

def apply_rope(x, cos, sin):
    half = x.shape[-1] // 2
    shape = (1, x.shape[1]) + (1,) * (x.ndim - 3) + (half,)
    c = cos.reshape(shape).astype(x.dtype)
    s = sin.reshape(shape).astype(x.dtype)
    x1, x2 = x[..., :half], x[..., half:]
    return jnp.concatenate([x1 * c - x2 * s, x2 * c + x1 * s], axis=-1)

def moba_attention(q, k, v):
    B, S, H, d = q.shape
    n_blk = -(-S // MOBA_BLOCK)
    pad = n_blk * MOBA_BLOCK - S
    padw = ((0, 0), (0, pad), (0, 0), (0, 0))
    kb = jnp.pad(k, padw).reshape(B, n_blk, MOBA_BLOCK, H, d).transpose(0, 3, 1, 2, 4)
    vb = jnp.pad(v, padw).reshape(B, n_blk, MOBA_BLOCK, H, d).transpose(0, 3, 1, 2, 4)
    k_mean = kb.mean(axis=3)
    topk = min(MOBA_TOPK, n_blk)
    n_chunks = S // Q_BLOCK
    qc = q.reshape(B, n_chunks, Q_BLOCK, H, d).transpose(1, 0, 3, 2, 4)
    b_idx = jnp.arange(B)[:, None, None, None]
    h_idx = jnp.arange(H)[None, :, None, None]
    scale = d ** -0.5
    n_sel = topk * MOBA_BLOCK

    def one_chunk(args):
        c, qh = args
        q_pos = c * Q_BLOCK + jnp.arange(Q_BLOCK)
        own = (c * Q_BLOCK) // MOBA_BLOCK
        gate = jnp.einsum('bhqd,bhnd->bhqn', qh, k_mean).astype(jnp.float32)
        gate = jnp.where(jnp.arange(n_blk) < own, gate, -jnp.inf)
        _, idx = lax.top_k(gate, topk)
        valid = jnp.arange(topk) < own
        k_sel = kb[b_idx, h_idx, idx]
        v_sel = vb[b_idx, h_idx, idx]
        s_sel = jnp.einsum('bhqd,bhqjld->bhqjl', qh, k_sel).astype(jnp.float32) * scale
        s_sel = jnp.where(valid[:, None], s_sel, -jnp.inf).reshape(B, H, Q_BLOCK, n_sel)
        k_own = lax.dynamic_index_in_dim(kb, own, axis=2, keepdims=False)
        v_own = lax.dynamic_index_in_dim(vb, own, axis=2, keepdims=False)
        s_own = jnp.einsum('bhqd,bhld->bhql', qh, k_own).astype(jnp.float32) * scale
        k_pos = own * MOBA_BLOCK + jnp.arange(MOBA_BLOCK)
        s_own = jnp.where(k_pos[None, :] <= q_pos[:, None], s_own, -jnp.inf)
        p = jax.nn.softmax(jnp.concatenate([s_sel, s_own], axis=-1), axis=-1).astype(v.dtype)
        p_sel = p[..., :n_sel].reshape(B, H, Q_BLOCK, topk, MOBA_BLOCK)
        p_own = p[..., n_sel:]
        return (jnp.einsum('bhqjl,bhqjld->bhqd', p_sel, v_sel)
                + jnp.einsum('bhql,bhld->bhqd', p_own, v_own))

    o = lax.map(one_chunk, (jnp.arange(n_chunks), qc))
    return o.transpose(1, 0, 3, 2, 4).reshape(B, S, H * d)

def sliding_window_sink_attention(q, k, v, sinks):
    B, S, Hq, d = q.shape
    Hkv = k.shape[2]
    G = Hq // Hkv
    nb = S // WINDOW
    qb = q.reshape(B, nb, WINDOW, Hkv, G, d)

    def band(t):
        tb = t.reshape(B, nb, WINDOW, Hkv, d)
        prev = jnp.concatenate([jnp.zeros_like(tb[:, :1]), tb[:, :-1]], axis=1)
        return jnp.concatenate([prev, tb], axis=2)

    kband, vband = band(k), band(v)
    s = jnp.einsum('bnqkgd,bnjkd->bnkgqj', qb, kband).astype(jnp.float32) * (d ** -0.5)
    rel = jnp.arange(WINDOW)[:, None] + WINDOW - jnp.arange(2 * WINDOW)[None, :]
    in_win = (rel >= 0) & (rel < WINDOW)
    k_abs = jnp.arange(nb)[:, None] * WINDOW - WINDOW + jnp.arange(2 * WINDOW)[None, :]
    mask = in_win[None, :, :] & (k_abs >= 0)[:, None, :]
    s = jnp.where(mask[None, :, None, None], s, -jnp.inf)
    sink = sinks.astype(jnp.float32).reshape(1, 1, Hkv, G, 1, 1)
    m = jnp.maximum(s.max(axis=-1, keepdims=True), sink)
    p = jnp.exp(s - m)
    denom = p.sum(axis=-1, keepdims=True) + jnp.exp(sink - m)
    o = jnp.einsum('bnkgqj,bnjkd->bnqkgd', (p / denom).astype(v.dtype), vband)
    return o.reshape(B, S, Hq * d)

def differential_attention(q, k, v, lam, subln_g, lam_init):
    B, S, H, _, dh = q.shape
    n_chunks = S // Q_BLOCK
    qc = q.reshape(B, n_chunks, Q_BLOCK, H, 2, dh).transpose(1, 0, 2, 3, 4, 5)
    scale = dh ** -0.5
    k_pos = jnp.arange(S)

    def one_chunk(args):
        c, qq = args
        q_pos = c * Q_BLOCK + jnp.arange(Q_BLOCK)
        s = jnp.einsum('bqhcd,bkhcd->bhcqk', qq, k).astype(jnp.float32) * scale
        s = jnp.where(k_pos[None, :] <= q_pos[:, None], s, -jnp.inf)
        p = jax.nn.softmax(s, axis=-1)
        a = (p[:, :, 0] - lam * p[:, :, 1]).astype(v.dtype)
        return jnp.einsum('bhqk,bkhd->bqhd', a, v)

    o = lax.map(one_chunk, (jnp.arange(n_chunks), qc))
    o = o.transpose(1, 0, 2, 3, 4).reshape(B, S, H, 2 * dh)
    o = rms_norm(o, subln_g) * (1.0 - lam_init)
    return o.reshape(B, S, H * 2 * dh)

def causal_depthwise_conv(u, w, b):
    S = u.shape[1]
    up = jnp.pad(u, ((0, 0), (CONV_W - 1, 0), (0, 0)))
    y = b.astype(u.dtype)
    for j in range(CONV_W):
        y = y + up[:, j:j + S] * w[j]
    return y

def first_inputs(seed: int = 0) -> dict:
    key = jax.random.key(seed)
    ks = jax.random.split(key, 24)
    n = jax.random.normal
    f32 = jnp.float32

    def gain(k, shape):
        return 1.0 + 0.02 * n(k, shape, f32)

    return {
        "x": n(ks[0], (BATCH, SEQ, D_MODEL), f32),
        "attn_norm": gain(ks[1], (DEPTH, D_MODEL)),
        "w_in": n(ks[2], (DEPTH, D_MODEL, IN_COLS), f32) * D_MODEL ** -0.5,
        "qn_a": gain(ks[3], (DEPTH, HEAD_DIM)),
        "kn_a": gain(ks[4], (DEPTH, HEAD_DIM)),
        "qn_b": gain(ks[5], (DEPTH, HEAD_DIM)),
        "kn_b": gain(ks[6], (DEPTH, HEAD_DIM)),
        "sinks": 0.5 * n(ks[7], (DEPTH, B_HEADS), f32),
        "qn_c": gain(ks[8], (DEPTH, C_HALF)),
        "kn_c": gain(ks[9], (DEPTH, C_HALF)),
        "lam_q1": 0.1 * n(ks[10], (DEPTH, C_HALF), f32),
        "lam_k1": 0.1 * n(ks[11], (DEPTH, C_HALF), f32),
        "lam_q2": 0.1 * n(ks[12], (DEPTH, C_HALF), f32),
        "lam_k2": 0.1 * n(ks[13], (DEPTH, C_HALF), f32),
        "subln": gain(ks[14], (DEPTH, HEAD_DIM)),
        "w_pa": n(ks[15], (DEPTH, A_W, D_MODEL), f32) * A_W ** -0.5,
        "w_pb": n(ks[16], (DEPTH, B_QW, D_MODEL), f32) * B_QW ** -0.5,
        "w_pc": n(ks[17], (DEPTH, C_W, D_MODEL), f32) * C_W ** -0.5,
        "w_out": n(ks[18], (DEPTH, D_MODEL, D_MODEL), f32) * D_MODEL ** -0.5,
        "mlp_norm": gain(ks[19], (DEPTH, D_MODEL)),
        "w_up": n(ks[20], (DEPTH, D_MODEL, 2 * D_FF), f32) * D_MODEL ** -0.5,
        "conv_w": 0.5 * n(ks[21], (DEPTH, CONV_W, 2 * D_FF), f32),
        "conv_b": 0.01 * n(ks[22], (DEPTH, 2 * D_FF), f32),
        "w_down": n(ks[23], (DEPTH, D_FF, D_MODEL), f32) * D_FF ** -0.5,
    }

def first_block(x, attn_norm, w_in, qn_a, kn_a, qn_b, kn_b, sinks, qn_c, kn_c,
              lam_q1, lam_k1, lam_q2, lam_k2, subln, w_pa, w_pb, w_pc, w_out,
              mlp_norm, w_up, conv_w, conv_b, w_down):
    B, S, D = x.shape
    cos64, sin64 = rope_tables(S, HEAD_DIM)
    cos32, sin32 = rope_tables(S, C_HALF)
    for i in range(DEPTH):
        lam_init = 0.8 - 0.6 * float(np.exp(-0.3 * i))
        h = rms_norm(x, attn_norm[i])
        proj = h @ w_in[i]
        qa, ka, va, qb, kb, vb, qc, kc, vc, gates = jnp.split(proj, SPLIT_POINTS, axis=-1)

        qa = apply_rope(rms_norm(qa.reshape(B, S, A_HEADS, HEAD_DIM), qn_a[i]), cos64, sin64)
        ka = apply_rope(rms_norm(ka.reshape(B, S, A_HEADS, HEAD_DIM), kn_a[i]), cos64, sin64)
        ya = moba_attention(qa, ka, va.reshape(B, S, A_HEADS, HEAD_DIM))

        qb = apply_rope(rms_norm(qb.reshape(B, S, B_HEADS, HEAD_DIM), qn_b[i]), cos64, sin64)
        kb = apply_rope(rms_norm(kb.reshape(B, S, B_KV_HEADS, HEAD_DIM), kn_b[i]), cos64, sin64)
        yb = sliding_window_sink_attention(qb, kb, vb.reshape(B, S, B_KV_HEADS, HEAD_DIM), sinks[i])

        qc = apply_rope(rms_norm(qc.reshape(B, S, C_HEADS, 2, C_HALF), qn_c[i]), cos32, sin32)
        kc = apply_rope(rms_norm(kc.reshape(B, S, C_HEADS, 2, C_HALF), kn_c[i]), cos32, sin32)
        lam = (jnp.exp(jnp.sum(lam_q1[i].astype(jnp.float32) * lam_k1[i].astype(jnp.float32)))
               - jnp.exp(jnp.sum(lam_q2[i].astype(jnp.float32) * lam_k2[i].astype(jnp.float32)))
               + lam_init)
        yc = differential_attention(qc, kc, vc.reshape(B, S, C_HEADS, HEAD_DIM), lam, subln[i], lam_init)

        g = jax.nn.sigmoid(gates.reshape(B, S, N_BRANCH, D))
        merged = g[:, :, 0] * (ya @ w_pa[i]) + g[:, :, 1] * (yb @ w_pb[i]) + g[:, :, 2] * (yc @ w_pc[i])
        x = x + merged @ w_out[i]

        h = rms_norm(x, mlp_norm[i])
        u = causal_depthwise_conv(h @ w_up[i], conv_w[i], conv_b[i])
        gate_u, val_u = jnp.split(u, 2, axis=-1)
        x = x + (jax.nn.silu(gate_u) * val_u) @ w_down[i]
    return x


RWKV_HEADS = 8
RWKV_HEAD_DIM = 64
RWKV_WIDTH = RWKV_HEADS * RWKV_HEAD_DIM
DECAY_LORA = 64
AAA_LORA = 64
GATE_LORA = 128
RWKV_GN_EPS = 64e-5
RWKV_COLS = 3 * RWKV_WIDTH + DECAY_LORA + AAA_LORA + GATE_LORA
CONF_WIDTH = 256
CONF_CONV_WIDTH = 31
CONF_COLS = 2 * CONF_WIDTH
SHORT_WIDTH = 256
SHORT_CONV_WIDTH = 3
SHORT_COLS = 3 * SHORT_WIDTH
N_BRANCHES = 3
GATE_COLS = N_BRANCHES * D_MODEL
IN_COLS_2 = RWKV_COLS + CONF_COLS + SHORT_COLS + GATE_COLS
N_EXPERTS = 8
TOP_K = 2
EXPERT_FF = 2816
MOE_BLOCK = 256
LN_EPS = 1e-5


def _layernorm(x, g, b, eps=LN_EPS):
    xf = x.astype(jnp.float32)
    mu = jnp.mean(xf, axis=-1, keepdims=True)
    var = jnp.mean(jnp.square(xf - mu), axis=-1, keepdims=True)
    return ((xf - mu) * lax.rsqrt(var + eps) * g + b).astype(x.dtype)

def _causal_depthwise_conv(x, w):
    width, ch = w.shape
    return lax.conv_general_dilated(
        x, w[:, None, :].astype(x.dtype), window_strides=(1,), padding=[(width - 1, 0)],
        dimension_numbers=("NWC", "WIO", "NWC"), feature_group_count=ch)

def _rwkv7_scan(r, decay, k, v, kk, a):
    bn, _, h, n = r.shape

    def step(state, inp):
        r_t, w_t, k_t, v_t, kk_t, a_t = inp
        sa = jnp.einsum("bhvk,bhk->bhv", state, -kk_t)
        state = (state * w_t[:, :, None, :]
                 + sa[..., None] * (kk_t * a_t)[:, :, None, :]
                 + v_t[..., None] * k_t[:, :, None, :])
        out = jnp.einsum("bhvk,bhk->bhv", state, r_t)
        return state, out

    xs = tuple(jnp.moveaxis(t, 1, 0) for t in (r, decay, k, v, kk, a))
    s0 = jnp.zeros((bn, h, n, n), jnp.float32)
    _, out = lax.scan(step, s0, xs)
    return jnp.moveaxis(out, 0, 1)

def _rwkv7_branch(p, mu, w0, w2, a0, a2, g2, k_k, k_a, r_k, ln_g, ln_b, w_o):
    bn, s, _ = p.shape
    H, N, W = RWKV_HEADS, RWKV_HEAD_DIM, RWKV_WIDTH
    f32 = jnp.float32
    p_prev = jnp.pad(p, ((0, 0), (1, 0), (0, 0)))[:, :-1]
    p = p + (p_prev - p) * mu
    cuts = [W, 2 * W, 3 * W, 3 * W + DECAY_LORA, 3 * W + DECAY_LORA + AAA_LORA]
    r, k, v, pw, pa, pg = jnp.split(p, cuts, axis=-1)
    w = -jax.nn.softplus(-(w0 + jnp.tanh(pw) @ w2).astype(f32)) - 0.5
    decay = jnp.exp(-jnp.exp(w))
    a = jax.nn.sigmoid((a0 + pa @ a2).astype(f32))
    g = jax.nn.sigmoid(pg) @ g2
    heads = lambda t: t.reshape(bn, s, H, N)
    k = k.astype(f32)
    kk = heads(k * k_k)
    kk = kk / jnp.maximum(jnp.sqrt(jnp.sum(kk * kk, axis=-1, keepdims=True)), 1e-12)
    k = k * (1.0 + (a - 1.0) * k_a)
    r4, k4, v4 = heads(r.astype(f32)), heads(k), heads(v.astype(f32))
    o = _rwkv7_scan(r4, heads(decay), k4, v4, kk, heads(a))
    mean = jnp.mean(o, axis=-1, keepdims=True)
    var = jnp.mean(jnp.square(o - mean), axis=-1, keepdims=True)
    o = (o - mean) * lax.rsqrt(var + RWKV_GN_EPS) * ln_g.reshape(H, N) + ln_b.reshape(H, N)
    o = o + jnp.sum(r4 * k4 * r_k, axis=-1, keepdims=True) * v4
    o = (o.reshape(bn, s, W) * g).astype(p.dtype)
    return o @ w_o

def _conformer_conv_branch(p, dw, dw_b, ln_g, ln_b, w_o):
    u = p[..., :CONF_WIDTH] * jax.nn.sigmoid(p[..., CONF_WIDTH:])
    u = _causal_depthwise_conv(u, dw) + dw_b
    u = jax.nn.silu(_layernorm(u, ln_g, ln_b))
    return u @ w_o

def _short_conv_branch(p, dw, w_o):
    gb, gc, h = jnp.split(p, 3, axis=-1)
    return (gb * _causal_depthwise_conv(gc * h, dw)) @ w_o

def _hybrid_mixer(x, w_in, rwkv_mu, rwkv_w0, rwkv_w2, rwkv_a0, rwkv_a2, rwkv_g2, rwkv_k_k,
                  rwkv_k_a, rwkv_r_k, rwkv_ln_g, rwkv_ln_b, rwkv_w_o, conf_dw, conf_dw_b,
                  conf_ln_g, conf_ln_b, conf_w_o, short_dw, short_w_o, w_out):
    p = x @ w_in
    c1 = RWKV_COLS
    c2 = c1 + CONF_COLS
    c3 = c2 + SHORT_COLS
    p_rwkv, p_conf, p_short, p_gate = jnp.split(p, [c1, c2, c3], axis=-1)
    y_a = _rwkv7_branch(p_rwkv, rwkv_mu, rwkv_w0, rwkv_w2, rwkv_a0, rwkv_a2, rwkv_g2,
                        rwkv_k_k, rwkv_k_a, rwkv_r_k, rwkv_ln_g, rwkv_ln_b, rwkv_w_o)
    y_b = _conformer_conv_branch(p_conf, conf_dw, conf_dw_b, conf_ln_g, conf_ln_b, conf_w_o)
    y_c = _short_conv_branch(p_short, short_dw, short_w_o)
    g_a, g_b, g_c = jnp.split(jax.nn.sigmoid(p_gate), N_BRANCHES, axis=-1)
    return (g_a * y_a.astype(x.dtype) + g_b * y_b + g_c * y_c) @ w_out

def _swiglu(x, w_gate, w_up, w_down):
    return (jax.nn.silu(x @ w_gate) * (x @ w_up)) @ w_down

def _moe_swiglu(x, w_router, w_gate, w_up, w_down):
    bn, s, d = x.shape
    xf = x.reshape(-1, d)
    n_tok = xf.shape[0]
    logits = (xf @ w_router).astype(jnp.float32)
    top_logit, top_idx = lax.top_k(logits, TOP_K)
    top_w = jax.nn.softmax(top_logit, axis=-1)
    n_assign = n_tok * TOP_K
    expert = top_idx.reshape(-1).astype(jnp.int32)
    token = jnp.repeat(jnp.arange(n_tok, dtype=jnp.int32), TOP_K)
    weight = top_w.reshape(-1)
    order = jnp.argsort(expert)
    s_expert, s_token, s_weight = expert[order], token[order], weight[order]
    counts = jnp.bincount(expert, length=N_EXPERTS).astype(jnp.int32)
    starts = jnp.cumsum(counts) - counts
    padded = ((counts + MOE_BLOCK - 1) // MOE_BLOCK) * MOE_BLOCK
    pad_ends = jnp.cumsum(padded)
    pad_starts = pad_ends - padded
    rank = jnp.arange(n_assign, dtype=jnp.int32) - starts[s_expert]
    dest = pad_starts[s_expert] + rank
    n_rows = (-(-n_assign // MOE_BLOCK) + N_EXPERTS) * MOE_BLOCK
    n_blocks = n_rows // MOE_BLOCK
    row_token = jnp.zeros((n_rows,), jnp.int32).at[dest].set(s_token)
    row_weight = jnp.zeros((n_rows,), jnp.float32).at[dest].set(s_weight)
    block_start = jnp.arange(n_blocks, dtype=jnp.int32) * MOE_BLOCK
    block_expert = jnp.minimum(jnp.searchsorted(pad_ends, block_start, side="right"),
                               N_EXPERTS - 1)
    xb = xf[row_token].reshape(n_blocks, MOE_BLOCK, d)

    def expert_block(args):
        xs, e = args
        return (jax.nn.silu(xs @ w_gate[e]) * (xs @ w_up[e])) @ w_down[e]

    yb = lax.map(expert_block, (xb, block_expert))
    y_rows = yb.reshape(n_rows, d) * row_weight[:, None].astype(x.dtype)
    out = jnp.zeros_like(xf).at[row_token].add(y_rows)
    return out.reshape(bn, s, d)

def second_inputs(seed: int = 0) -> dict:
    key = jax.random.key(seed)
    ks = jax.random.split(key, 40)
    L = DEPTH
    n_dense = (DEPTH + 1) // 2
    n_moe = DEPTH // 2
    beta = (8.0 * DEPTH) ** -0.25
    D, W = D_MODEL, RWKV_WIDTH

    def nrm(k, shape, scale):
        return jax.random.normal(k, shape, jnp.float32) * scale

    w0_base = -6.0 + 5.0 * (jnp.arange(W, dtype=jnp.float32) / (W - 1)) ** 0.9
    return {
        "x": nrm(ks[0], (BATCH, SEQ, D), 1.0),
        "w_in": nrm(ks[1], (L, D, IN_COLS_2), D ** -0.5),
        "rwkv_mu": jax.random.uniform(ks[2], (L, RWKV_COLS), jnp.float32),
        "rwkv_w0": w0_base + nrm(ks[3], (L, W), 0.1),
        "rwkv_w2": nrm(ks[4], (L, DECAY_LORA, W), 0.1 * DECAY_LORA ** -0.5),
        "rwkv_a0": nrm(ks[5], (L, W), 0.1),
        "rwkv_a2": nrm(ks[6], (L, AAA_LORA, W), AAA_LORA ** -0.5),
        "rwkv_g2": nrm(ks[7], (L, GATE_LORA, W), GATE_LORA ** -0.5),
        "rwkv_k_k": 0.85 + nrm(ks[8], (L, W), 0.02),
        "rwkv_k_a": 1.0 + nrm(ks[9], (L, W), 0.02),
        "rwkv_r_k": nrm(ks[10], (L, RWKV_HEADS, RWKV_HEAD_DIM), 0.1),
        "rwkv_ln_g": 1.0 + nrm(ks[11], (L, W), 0.02),
        "rwkv_ln_b": nrm(ks[12], (L, W), 0.02),
        "rwkv_w_o": nrm(ks[13], (L, W, D), W ** -0.5),
        "conf_dw": nrm(ks[14], (L, CONF_CONV_WIDTH, CONF_WIDTH), CONF_CONV_WIDTH ** -0.5),
        "conf_dw_b": nrm(ks[15], (L, CONF_WIDTH), 0.02),
        "conf_ln_g": 1.0 + nrm(ks[16], (L, CONF_WIDTH), 0.02),
        "conf_ln_b": nrm(ks[17], (L, CONF_WIDTH), 0.02),
        "conf_w_o": nrm(ks[18], (L, CONF_WIDTH, D), CONF_WIDTH ** -0.5),
        "short_dw": nrm(ks[19], (L, SHORT_CONV_WIDTH, SHORT_WIDTH), SHORT_CONV_WIDTH ** -0.5),
        "short_w_o": nrm(ks[20], (L, SHORT_WIDTH, D), SHORT_WIDTH ** -0.5),
        "w_out": nrm(ks[21], (L, D, D), beta * D ** -0.5),
        "ln1_g": 1.0 + nrm(ks[22], (L, D), 0.02),
        "ln1_b": nrm(ks[23], (L, D), 0.02),
        "ffn_w_gate": nrm(ks[24], (n_dense, D, D_FF), D ** -0.5),
        "ffn_w_up": nrm(ks[25], (n_dense, D, D_FF), D ** -0.5),
        "ffn_w_down": nrm(ks[26], (n_dense, D_FF, D), beta * D_FF ** -0.5),
        "moe_router": nrm(ks[27], (n_moe, D, N_EXPERTS), D ** -0.5),
        "moe_w_gate": nrm(ks[28], (n_moe, N_EXPERTS, D, EXPERT_FF), D ** -0.5),
        "moe_w_up": nrm(ks[29], (n_moe, N_EXPERTS, D, EXPERT_FF), D ** -0.5),
        "moe_w_down": nrm(ks[30], (n_moe, N_EXPERTS, EXPERT_FF, D), beta * EXPERT_FF ** -0.5),
        "ln2_g": 1.0 + nrm(ks[31], (L, D), 0.02),
        "ln2_b": nrm(ks[32], (L, D), 0.02),
    }

def second_block(x, w_in, rwkv_mu, rwkv_w0, rwkv_w2, rwkv_a0, rwkv_a2, rwkv_g2, rwkv_k_k,
              rwkv_k_a, rwkv_r_k, rwkv_ln_g, rwkv_ln_b, rwkv_w_o, conf_dw, conf_dw_b,
              conf_ln_g, conf_ln_b, conf_w_o, short_dw, short_w_o, w_out, ln1_g, ln1_b,
              ffn_w_gate, ffn_w_up, ffn_w_down, moe_router, moe_w_gate, moe_w_up,
              moe_w_down, ln2_g, ln2_b):
    alpha = (2.0 * DEPTH) ** 0.25
    for i in range(DEPTH):
        mix = _hybrid_mixer(x, w_in[i], rwkv_mu[i], rwkv_w0[i], rwkv_w2[i], rwkv_a0[i],
                            rwkv_a2[i], rwkv_g2[i], rwkv_k_k[i], rwkv_k_a[i], rwkv_r_k[i],
                            rwkv_ln_g[i], rwkv_ln_b[i], rwkv_w_o[i], conf_dw[i], conf_dw_b[i],
                            conf_ln_g[i], conf_ln_b[i], conf_w_o[i], short_dw[i],
                            short_w_o[i], w_out[i])
        x = _layernorm(alpha * x + mix, ln1_g[i], ln1_b[i])
        j = i // 2
        if i % 2 == 0:
            f = _swiglu(x, ffn_w_gate[j], ffn_w_up[j], ffn_w_down[j])
        else:
            f = _moe_swiglu(x, moe_router[j], moe_w_gate[j], moe_w_up[j], moe_w_down[j])
        x = _layernorm(alpha * x + f, ln2_g[i], ln2_b[i])
    return x


def setup_inputs(seed=0):
    out = dict(first_inputs(seed))
    for name, value in second_inputs(seed + 1).items():
        if name != "x":
            out[name + "_2"] = value
    return out


def reference(
    x, attn_norm, w_in, qn_a, kn_a, qn_b, kn_b, sinks, qn_c, kn_c, lam_q1, lam_k1, lam_q2,
    lam_k2, subln, w_pa, w_pb, w_pc, w_out, mlp_norm, w_up, conv_w, conv_b, w_down, w_in_2,
    rwkv_mu_2, rwkv_w0_2, rwkv_w2_2, rwkv_a0_2, rwkv_a2_2, rwkv_g2_2, rwkv_k_k_2, rwkv_k_a_2,
    rwkv_r_k_2, rwkv_ln_g_2, rwkv_ln_b_2, rwkv_w_o_2, conf_dw_2, conf_dw_b_2, conf_ln_g_2,
    conf_ln_b_2, conf_w_o_2, short_dw_2, short_w_o_2, w_out_2, ln1_g_2, ln1_b_2, ffn_w_gate_2,
    ffn_w_up_2, ffn_w_down_2, moe_router_2, moe_w_gate_2, moe_w_up_2, moe_w_down_2, ln2_g_2,
    ln2_b_2,
):
    x = first_block(
        x, attn_norm, w_in, qn_a, kn_a, qn_b, kn_b, sinks, qn_c, kn_c, lam_q1, lam_k1, lam_q2,
        lam_k2, subln, w_pa, w_pb, w_pc, w_out, mlp_norm, w_up, conv_w, conv_b, w_down,
    )
    return second_block(
        x, w_in_2, rwkv_mu_2, rwkv_w0_2, rwkv_w2_2, rwkv_a0_2, rwkv_a2_2, rwkv_g2_2, rwkv_k_k_2,
        rwkv_k_a_2, rwkv_r_k_2, rwkv_ln_g_2, rwkv_ln_b_2, rwkv_w_o_2, conf_dw_2, conf_dw_b_2,
        conf_ln_g_2, conf_ln_b_2, conf_w_o_2, short_dw_2, short_w_o_2, w_out_2, ln1_g_2,
        ln1_b_2, ffn_w_gate_2, ffn_w_up_2, ffn_w_down_2, moe_router_2, moe_w_gate_2, moe_w_up_2,
        moe_w_down_2, ln2_g_2, ln2_b_2,
    )


_drawn_inputs = setup_inputs


def setup_inputs(seed=0):
    import zlib

    import numpy as np

    out = dict(_drawn_inputs(seed))
    spreads = {}
    factors = {'qn_a': 7.883,
     'kn_a': 8.0,
     'qn_b': 8.0,
     'kn_b': 8.0,
     'sinks': 7.046,
     'qn_c': 3.396,
     'kn_c': 3.256,
     'subln': 3.274,
     'conv_b': 4.725,
     'rwkv_w2_2': 8.0,
     'rwkv_a0_2': 5.546,
     'rwkv_k_k_2': 43.535,
     'rwkv_k_a_2': 7.489,
     'rwkv_ln_g_2': 30.483,
     'rwkv_ln_b_2': 29.517,
     'conf_dw_b_2': 5.206,
     'conf_ln_g_2': 21.696,
     'conf_ln_b_2': 23.408}
    for name, (base, spread) in spreads.items():
        noise = np.random.default_rng([zlib.crc32(name.encode()), seed]).standard_normal(out[name].shape)
        drawn = base * np.exp(spread * noise) if base else spread * noise
        out[name] = __import__('jax').numpy.asarray(drawn.astype(out[name].dtype))
    for name, factor in factors.items():
        out[name] = (out[name] * factor).astype(out[name].dtype)
    return out
```

```python
from contextlib import ExitStack

import numpy as np

import concourse.bass as bass
from concourse import mybir

F32 = mybir.dt.float32
ALU = mybir.AluOpType
ACT = mybir.ActivationFunctionType
AX = mybir.AxisListType

P = 128
SEQ = 256
TB = SEQ // P
D = 1024
KT = D // P
DEPTH = 2
FF = 2816
FJ = FF // 256
N_EXP = 8
UNIT = 2048
HD = 64
N_QK = 13
CHUNK = 64
KAPPA = float(np.exp(-0.5))
ALPHA = (2.0 * DEPTH) ** 0.25
RMS_EPS = 1e-6
LN_EPS = 1e-5
GN_EPS = 64e-5
BIG = 1e30
CONF_TAPS = 31

N_IN1 = 21
N_PROJ = 4
N_OUT = 4
LAYER1 = N_IN1 + N_PROJ + N_OUT + 3 * FJ
N_IN2 = 24
MIX2 = N_IN2 + N_PROJ + N_OUT
FFN = 3 * FJ
MIX2_0 = DEPTH * LAYER1
FFN_0 = MIX2_0 + MIX2
MIX2_1 = FFN_0 + FFN
MOE_0 = MIX2_1 + MIX2
N_UNITS = MOE_0 + N_EXP * FFN
RING = 4
MOE_RING = 11


def ffn_order():
    order = []
    for j in range(FJ):
        order += [("gate", j), ("up", j)]
        if j:
            order.append(("down", j - 1))
    return order + [("down", FJ - 1)]


FFN_UNIT = {key: n for n, key in enumerate(ffn_order())}


class Names:

    def __init__(self):
        self.at, self.size = {}, 0

    def add(self, name, width):
        self.at[name] = (self.size, width)
        self.size += width


def param_names():
    n = Names()
    for l in range(DEPTH):
        for name, w in (("attn_norm", 8), ("mlp_norm", 8), ("q_gain", N_QK), ("subln", 1), ("sinks", 8), ("lam", 128),
                        ("conv_w", 3 * 44), ("conv_b", 44)):
            n.add(f"{name}{l}", w)
        for name, w in (("mu", 14), ("w0", 4), ("a0", 4), ("k_k", 4), ("k_a", 4), ("r_k", 4), ("conf_dw", 62),
                        ("conf_b", 2), ("conf_g", 2), ("conf_lb", 2), ("short_dw", 6), ("lora", 512), ("g2", 512)):
            n.add(f"{name}{l}", w)
    n.add("router", KT * N_EXP)
    return n


def const_names():
    n = Names()
    for name, w in (("ident", 128), ("ones64", 128), ("ones32", 128), ("rot64", 128), ("rot32", 128), ("mean256", 128),
                    ("causal", 384), ("window", 384), ("cos64", 256), ("sin64", 256), ("cos32", 256), ("sin32", 256),
                    ("chunk4", 512), ("first", 128), ("levels", 6 * 128), ("heads2", 2), ("reset", 256), ("tie", 64)):
        n.add(name, w)
    return n


PAR = param_names()
CST = const_names()


class Steps:

    def __init__(self, sem, known, where):
        self.sem, self.known, self.where = sem, known, where
        self.now, self.steps, self.loop = 0, {}, False

    def done(self, *key):
        self.now += 1
        self.steps[key] = ("expert", self.now - self.base) if self.loop else ("once", self.now)
        return self.sem, 1

    def _value(self, where, index, lag=0):
        base, per = self.known.get("base", 1), self.known.get("per", 1)
        return where * per + (base - lag * per + index)

    def of(self, *key):
        kind, n = self.steps.get(key) or self.known.get(key, ("once", 1))
        if kind == "once":
            return self.sem, n
        e = self.where["expert"]
        return self.sem, self._value(N_EXP - 1 if e is None else e, n)

    def before(self, *key):
        kind, n = self.known.get(key, ("expert", 1))
        return self.sem, self._value(self.where["expert"], n, lag=1)

    def last(self):
        if self.loop:
            return self.sem, self._value(self.where["expert"], self.now - self.base)
        return self.sem, self.now

    def enter(self):
        self.loop, self.base = True, self.now
        self.steps["base"] = self.now

    def again(self):
        self.steps["per"] = self.now - self.base
        self.now = self.base

    def leave(self):
        self.now = self.base + N_EXP * (self.now - self.base)
        self.loop = False


def emit(nc, known, stream, par_d, cst_d, rows_d, x_d, out_d, n_stages):
    ctx = ExitStack()
    with ctx:
        def sb(name, width):
            return ctx.enter_context(nc.sbuf_tensor(name, [P, width], F32))[:, :]

        where = {"expert": None}

        def steps(name):
            return Steps(ctx.enter_context(nc.semaphore(name)), known.get(name, {}), where)

        ring = sb("ring", RING * UNIT)
        par = sb("par", PAR.size)
        cst = sb("cst", CST.size)
        norm_rows = sb("norm_rows", 2 * D)
        group_rows = sb("group_rows", 2 * 512)
        xres = sb("xres", TB * D)
        xT = sb("xT", KT * SEQ)
        gates = sb("gates", 24 * SEQ)
        yT = sb("yT", KT * SEQ)
        small = sb("small", 512)
        mh = sb("minus_half", 1)
        Z = sb("Z", 21504)
        banks = [ctx.enter_context(nc.psum_tensor(f"bank{i}", [P, 512], F32))[:, :] for i in range(8)]

        def pr(name, i=0, n=1):
            a, _ = PAR.at[name]
            return par[:, a + i:a + i + n]

        def ct(name, i=0, n=None):
            a, w = CST.at[name]
            return cst[:, a + i:a + (w if n is None else i + n)]

        small_at = {}

        def sm(name, width):
            if name not in small_at:
                used = sum(w for _, w in small_at.values())
                assert used + width <= 512
                small_at[name] = (used, width)
            a, w = small_at[name]
            return small[:, a:a + w]

        T = steps("matmul_done")
        A = steps("scalar_done")
        V = steps("vector_done")
        G = steps("pool_done")
        s_const = ctx.enter_context(nc.semaphore("const_loaded"))
        s_par = ctx.enter_context(nc.semaphore("par_loaded"))
        s_x = ctx.enter_context(nc.semaphore("x_loaded"))
        s_norm_rows = ctx.enter_context(nc.semaphore("norm_rows_loaded"))
        s_group_rows = ctx.enter_context(nc.semaphore("group_rows_loaded"))
        s_out = ctx.enter_context(nc.semaphore("out_stored"))
        s_slot = [ctx.enter_context(nc.semaphore(f"slot{i}_loaded")) for i in range(RING)]
        s_moe_slot = [ctx.enter_context(nc.semaphore(f"moe_slot{i}_loaded")) for i in range(MOE_RING)]
        block = ctx.enter_context(nc.Block())

        def slot(u):
            return ring[:, (u % RING) * UNIT:(u % RING + 1) * UNIT]

        def loaded(u):
            return s_slot[u % RING], 16 * (u // RING + 1)

        def moe_slot(i):
            s = i % MOE_RING
            return ring[:, s * UNIT:(s + 1) * UNIT] if s < RING else Z[:, (s - RING) * UNIT:(s - RING + 1) * UNIT]

        def moe_loaded(i, e):
            per = FFN // MOE_RING
            return s_moe_slot[i % MOE_RING], e * (16 * per) + 16 * (i // MOE_RING + 1)

        def cols3(i):
            return slice(i * P, (i + 1) * P)

        QK_TILES = {0: 0, 1: 1, 2: 2, 3: 3, 6: 4, 7: 5, 8: 6, 9: 7, 10: 8, 12: 9, 13: 10, 14: 11, 15: 12}
        QK_PAIRS = [(0, 2), (2, 2), (4, 2), (6, 2), (8, 1), (9, 2), (11, 2)]

        JOBS = []
        for h in range(4):
            JOBS.append(("a", h, h // 2, 64 * (h % 2), h // 2, 2 + h // 2, 64 * (h % 2), 64, h * 64))
        for h in range(8):
            JOBS.append(("b", (h // 2) + 4 * (h % 2), 2 + h // 2, 64 * (h % 2), 4 + h // 2, 8, 64 * (h % 2), 64,
                         256 + 64 * (h % 2)))
        for h in range(4):
            for c in range(2):
                JOBS.append((f"c{c}", h, 6 + h // 2, 64 * (h % 2), 9 + h // 2, 11 + h // 2, 64 * (h % 2) + 32 * c, 32,
                             384 + h * 64))

        def attention_schedule():
            out, gate = [], 0
            for t in range(len(JOBS) + 3):
                if t < len(JOBS):
                    out.append(("score", t))
                if 1 <= t <= len(JOBS):
                    out.append(("norm", t - 1))
                if 2 <= t <= len(JOBS) + 1:
                    out.append(("turn", t - 2))
                if 3 <= t:
                    out.append(("value", t - 3))
                if t % 2 == 1 and gate < 7:
                    out.append(("gate", 5 + gate))
                    gate += 1
            while gate < 7:
                out.append(("gate", 5 + gate))
                gate += 1
            return out

        SCHED = attention_schedule()

        qk = Z[:, 0:N_QK * SEQ]
        vtm = Z[:, 3328:3328 + TB * 640].rearrange("p (b n) -> p b n", b=TB)
        o = 3328 + TB * 640
        sq = Z[:, o:o + 1024].rearrange("p (b n) -> p b n", b=2)
        rs = Z[:, o + 1024:o + 2048].rearrange("p (b n) -> p b n", b=2)
        rot = Z[:, o + 2048:o + 3072].rearrange("p (b n) -> p b n", b=2)
        msk = Z[:, o + 3072:o + 3072 + 2 * 384].rearrange("p (b n) -> p b n", b=2)
        prob = Z[:, o + 3840:o + 3840 + 3 * 384].rearrange("p (b n) -> p b n", b=3)
        probT = Z[:, o + 4992:o + 4992 + 2 * 384].rearrange("p (b n) -> p b n", b=2)
        wide = Z[:, o + 5760:o + 5760 + 2 * D].rearrange("p (b n) -> p b n", b=TB)
        junk = Z[:, o + 5760 + 2 * D:o + 5760 + 3 * D]
        squares = Z[:, o + 5760 + 3 * D:o + 5760 + 3 * D + N_QK * SEQ]
        xr = xres.rearrange("p (b n) -> p b n", b=TB)
        xk = xT.rearrange("p (k n) -> p k n", k=KT)
        yk = yT.rearrange("p (k n) -> p k n", k=KT)
        gk = gates.rearrange("p (k n) -> p k n", k=24)

        hid = gates[:, 0:1024].rearrange("p (b c n) -> p b c n", b=2, c=2)
        act = gates[:, 1024:2048].rearrange("p (b n) -> p b n", b=2)
        cg = gates[:, 2048:3072].rearrange("p (b c n) -> p b c n", b=2, c=2)
        cv = gates[:, 3072:4096].rearrange("p (b c n) -> p b c n", b=2, c=2)
        moe_acc = gates[:, 4096:6144].rearrange("p (b n) -> p b n", b=TB)

        rkv = Z[:, 0:3584].rearrange("p (t n) -> p t n", n=SEQ)
        r_, k_, v_ = rkv[:, 0:4, :], rkv[:, 4:8, :], rkv[:, 8:12, :]
        wa, pg = rkv[:, 12, :], rkv[:, 13, :]
        conf = Z[:, 3584:4608].rearrange("p (t n) -> p t n", n=SEQ)
        short = Z[:, 4608:6144].rearrange("p (t n) -> p t n", n=SEQ)
        a_ = Z[:, 6144:7168].rearrange("p (t n) -> p t n", n=SEQ)
        b_ = Z[:, 7168:8192].rearrange("p (t n) -> p t n", n=SEQ)
        tm = Z[:, 8192:11264].rearrange("p (x b n) -> p x b n", x=3, b=TB)
        rwo = Z[:, 11264:12288].rearrange("p (b n) -> p b n", b=TB)
        gram = Z[:, 12288:16384].rearrange("p (h n) -> p h n", h=8)
        inv = Z[:, 16384:17408].rearrange("p (h n) -> p h n", h=8)
        tri = v_.rearrange("p t n -> p (t n)").rearrange("p (h n) -> p h n", h=8)
        off = Z[:, 17408:18432].rearrange("p (h n) -> p h n", h=8)
        lev = Z[:, 18432:19456].rearrange("p (h n) -> p h n", h=8)
        xs = Z[:, 19456:19968]
        us = Z[:, 19968:20480]
        state = Z[:, 20480:20992].rearrange("p (t n) -> p t n", n=P)
        stmp = Z[:, 20992:21504]
        ctmp = yk[:, 4:6, :]
        t0 = Z[:, 12288:13312].rearrange("p (t n) -> p t n", n=SEQ)
        t1 = Z[:, 13312:14336].rearrange("p (t n) -> p t n", n=SEQ)
        t2 = Z[:, 14336:15360].rearrange("p (t n) -> p t n", n=SEQ)
        t3 = Z[:, 15360:16384].rearrange("p (t n) -> p t n", n=SEQ)
        kk = Z[:, 16384:17408].rearrange("p (t n) -> p t n", n=SEQ)
        aa = Z[:, 17408:18432].rearrange("p (t n) -> p t n", n=SEQ)
        ep = Z[:, 18432:19456].rearrange("p (t n) -> p t n", n=SEQ)

        def flat(v):
            return v.rearrange("p a b -> p (a b)")

        def halves(v):
            return v.rearrange("p (b n) -> p b n", n=SEQ)

        def grow(v, shape, axis):
            return v.unsqueeze(axis).broadcast_to(shape)

        @block.sync
        def _(sp):
            sp.dma_start(xr, x_d.rearrange("(b p) n -> p b n", p=P)).then_inc(s_x, 16)
            sp.dma_start(cst, cst_d).then_inc(s_const, 16)
            sp.dma_start(par, par_d).then_inc(s_par, 16)
            n_main = {1: LAYER1, 2: 2 * LAYER1, 3: FFN_0 + FFN, 4: MOE_0}[n_stages]
            for u in range(n_main):
                if u >= RING:
                    sp.wait_ge(*T.of("unit", u - RING))
                sp.dma_start(slot(u), stream[u]).then_inc(s_slot[u % RING], 16)
            if n_stages == 4:
                def expert(e, peeled):
                    where["expert"] = e
                    for i in range(FFN):
                        s = i % MOE_RING
                        if i >= MOE_RING:
                            sp.wait_ge(*T.of("moe_unit", i - MOE_RING))
                        elif not peeled:
                            sp.wait_ge(*T.before("moe_unit", i + FFN - MOE_RING))
                        elif s < RING:
                            sp.wait_ge(*T.of("unit", max(u for u in range(MOE_0) if u % RING == s)))
                        else:
                            sp.wait_ge(*V.of("mixed", 1))
                        sp.dma_start(moe_slot(i), stream[e * FFN + (MOE_0 + i)]).then_inc(s_moe_slot[s], 16)
                expert(0, True)
                with sp.Fori(1, N_EXP) as e:
                    expert(e, False)
                where["expert"] = None
            sp.wait_ge(*V.of("final"))
            if n_stages >= 3:
                sp.wait_ge(*G.of("final"))
            sp.dma_start(out_d.rearrange("(b p) n -> p b n", p=P), xr).then_inc(s_out, 16)
            sp.wait_ge(s_out, 16)

        @block.tensor
        def _(pe):
            mm = nc.tensor.matmul

            def turn_wide(src, tag, l, ready):
                for k in range(KT):
                    for tb in range(TB):
                        if k == 0:
                            pe.wait_ge(*ready[tb])
                        t = nc.tensor.transpose(banks[k // 2][:, (k % 2) * SEQ + tb * P:(k % 2) * SEQ + (tb + 1) * P],
                                                src[:, tb, k * P:(k + 1) * P], ct("ident"))
                    t.then_inc(*T.done("turned", tag, l, k))

            def features(bank, w, l):
                wv = w.rearrange("p (k n) -> p k n", k=KT)
                for c in range(2):
                    for k in range(KT):
                        r = mm(bank[:, c * SEQ:(c + 1) * SEQ], wv[:, k, c * P:(c + 1) * P], xk[:, k, :],
                               start=(k == 0), stop=(k == KT - 1))
                return r

            def tokens(bank, at, w, c0, width):
                wv = w.rearrange("p (k n) -> p k n", k=KT)
                for tb in range(TB):
                    for k in range(KT):
                        r = mm(bank[:, at + tb * width:at + (tb + 1) * width], xk[:, k, tb * P:(tb + 1) * P],
                               wv[:, k, c0:c0 + width], start=(k == 0), stop=(k == KT - 1))
                return r

            def rows(src, w, first, last):
                wv = w.rearrange("p (c n) -> p c n", c=2)
                for c in range(2):
                    for tb in range(TB):
                        for half in range(2):
                            r = mm(banks[2 * tb + half], src(c)[:, tb * P:(tb + 1) * P],
                                   wv[:, c, half * 512:(half + 1) * 512], start=(first and c == 0),
                                   stop=(last and c == 1))
                return r

            def project(l, blk, splits, u0):
                for n in range(N_PROJ):
                    pe.wait_ge(*loaded(u0 + n))
                k_at = [0, splits[0], splits[0] + splits[1]]
                for c in range(4):
                    for b in range(3):
                        bank = banks[4 + (3 * c + b) % 4]
                        if 3 * c + b >= 4:
                            pe.wait_ge(*V.of("merged", blk, l, 3 * c + b - 4))
                        for half in range(2):
                            for k in range(k_at[b], k_at[b] + splits[b]):
                                wv = slot(u0 + k // 2).rearrange("p (c n) -> p c n", c=2)
                                col = (2 * c + half) * P
                                r = mm(bank[:, half * SEQ:(half + 1) * SEQ], wv[:, k % 2, col:col + P], yk[:, k, :],
                                       start=(k == k_at[b]), stop=(k == k_at[b] + splits[b] - 1))
                        r.then_inc(*T.done("branch", blk, l, 3 * c + b))
                for n in range(N_PROJ):
                    T.steps[("unit", u0 + n)] = T.steps[("branch", blk, l, 11)]

            def project_out(l, blk, u0):
                for n in range(N_OUT):
                    u = u0 + n
                    pe.wait_ge(*loaded(u))
                    pe.wait_ge(*V.of("merged", blk, l, 11))
                    rows(lambda c: gk[:, 2 * n + c, :], slot(u), n == 0, n == N_OUT - 1).then_inc(*T.done("unit", u))

            def block1(l):
                u0 = l * LAYER1
                if l == 0:
                    pe.wait_ge(s_const, 16)
                turn_wide(wide, "b1", l, [V.of("normed", "b1", l, tb) for tb in range(TB)])

                def unit(n):
                    u = u0 + n
                    pe.wait_ge(*loaded(u))
                    if n == 0:
                        pe.wait_ge(*A.of("xT", "b1", l))
                        pe.wait_ge(*V.of("xT", "b1", l))
                    if n >= 4:
                        pe.wait_ge(*A.of("in1", l, n - 4))
                    bank = banks[4 + n % 4]
                    if n in (2, 8):
                        r = tokens(bank, 0, slot(u), 0, 256)
                    elif n == 5:
                        wv = slot(u).rearrange("p (k n) -> p k n", k=KT)
                        for k in range(KT):
                            mm(bank[:, 0:SEQ], wv[:, k, 0:P], xk[:, k, :], start=(k == 0), stop=(k == KT - 1))
                        r = tokens(bank, SEQ, slot(u), P, P)
                    else:
                        r = features(bank, slot(u), l)
                    r.then_inc(*T.done("unit", u))

                for n in range(9):
                    unit(n)
                for i, (c, m) in enumerate(QK_PAIRS):
                    w = m * SEQ
                    ones = "ones64" if c < 9 else "ones32"
                    if i < 5:
                        unit(9 + i)
                    pe.wait_ge(*A.of("square", l, c + m - 1))
                    if i >= 2:
                        pe.wait_ge(*A.of("qrms", l, i - 2))
                    mm(banks[i % 2][:, 0:w], ct(ones), squares[:, c * SEQ:(c + m) * SEQ], start=True, stop=True)\
                        .then_inc(*T.done("sumsq", l, i))
                    if i >= 1:
                        rotate(l, i - 1)
                rotate(l, len(QK_PAIRS) - 1)

                for kind, n in SCHED:
                    if kind == "gate":
                        unit(9 + n)
                    elif kind == "score":
                        br, h, ot, ob, qt, kt, base, kk_, vc = JOBS[n]
                        if n == 0:
                            pe.wait_ge(*G.of("roped", l, len(QK_PAIRS) - 1))
                            pe.wait_ge(*V.of("qn", l, len(QK_PAIRS) - 1))
                            pe.wait_ge(*V.of("rotsin", l, len(QK_PAIRS) - 1))
                        if n >= 2:
                            pe.wait_ge(*V.of("masked", l, n - 2))
                        q = qk[base:base + kk_, qt * SEQ:(qt + 1) * SEQ]
                        k = qk[base:base + kk_, kt * SEQ:(kt + 1) * SEQ]
                        mm(banks[n % 2][:, 0:128], q[:, 0:128], k[:, 0:128], start=True, stop=True)
                        mm(banks[n % 2][:, 128:384], q[:, 128:256], k, start=True, stop=True)\
                            .then_inc(*T.done("score", l, n))
                    elif kind == "turn" and JOBS[n][0] != "c0":
                        pe.wait_ge(*V.of("prob", l, n))
                        if n >= 1:
                            m = n - 1 if JOBS[n - 1][0] != "c0" else n - 2
                            pe.wait_ge(*A.of("probT", l, m))
                        for i in range(3):
                            r = nc.tensor.transpose(banks[2][:, i * P:(i + 1) * P], prob[:, n % 3, cols3(i)], ct("ident"))
                        r.then_inc(*T.done("turnp", l, n))
                    elif kind == "value" and JOBS[n][0] != "c0":
                        br, h, ot, ob, qt, kt, base, kk_, vc = JOBS[n]
                        pe.wait_ge(*A.of("probT", l, n))
                        if ob == 0 and ot >= 1:
                            pe.wait_ge(*A.of("y", l, ot - 1))
                        dst = banks[3][ob:ob + HD, 0:SEQ]
                        mm(dst, vtm[:, 0, vc:vc + HD], probT[:, n % 2, 0:256], start=True, stop=False)
                        mm(dst[:, 128:256], vtm[:, 1, vc:vc + HD], probT[:, n % 2, 256:384], start=False, stop=True)\
                            .then_inc(*T.done("value", l, n))
                for i in range(2):
                    pe.wait_ge(*A.of("csquare", l, i))
                    if i == 0:
                        pe.wait_ge(*V.of("masked", l, len(JOBS) - 1))
                    r = mm(banks[0][:, i * SEQ:(i + 1) * SEQ], ct("ones64"), sq[:, 0, i * SEQ:(i + 1) * SEQ],
                           start=True, stop=True)
                r.then_inc(*T.done("csum", l))
                pe.wait_ge(*V.of("cnormed", l))
                pe.wait_ge(*A.of("in1", l, N_IN1 - 1))
                project(l, "b1", (2, 4, 2), u0 + N_IN1)
                project_out(l, "b1", u0 + N_IN1 + N_PROJ)
                turn_wide(wide, "f1", l, [V.of("normed", "f1", l, tb) for tb in range(TB)])
                f0 = u0 + N_IN1 + N_PROJ + N_OUT
                for (kind, j), n in FFN_UNIT.items():
                    u = f0 + n
                    pe.wait_ge(*loaded(u))
                    if n == 0:
                        pe.wait_ge(*A.of("xT", "f1", l))
                        pe.wait_ge(*V.of("xT", "f1", l))
                    if kind == "down":
                        pe.wait_ge(*V.of("hidden1", l, j))
                        r = rows(lambda c: hid[:, j % 2, c, :], slot(u), j == 0, j == FJ - 1)
                    else:
                        if j >= 2:
                            pe.wait_ge(*V.of("conv", kind, l, j - 2))
                        r = features(banks[4 + 2 * (j % 2) + (kind == "up")], slot(u), l)
                    r.then_inc(*T.done("unit", u))
                    T.steps[(kind, l, j)] = T.steps[("unit", u)]

            def rotate(l, i):
                c, m = QK_PAIRS[i]
                pe.wait_ge(*V.of("qn", l, i))
                if i >= 2:
                    pe.wait_ge(*V.of("rotsin", l, i - 2))
                mm(banks[2 + i % 2][:, 0:m * SEQ], ct("rot64" if c < 9 else "rot32"), qk[:, c * SEQ:(c + m) * SEQ],
                   start=True, stop=True).then_inc(*T.done("rotated", l, i))

            def swiglu(pre, w_of, loaded_of, wait_first, wait_acc):
                for (kind, j), n in FFN_UNIT.items():
                    pe.wait_ge(*loaded_of(n))
                    if n == 0:
                        wait_first()
                    if kind == "down":
                        pe.wait_ge(*V.of(pre + "hidden", j))
                        if j == 0:
                            wait_acc()
                        r = rows(lambda c: hid[:, j % 2, c, :], w_of(n), j == 0, j == FJ - 1)
                    else:
                        if j >= 2:
                            pe.wait_ge(*V.of(pre + "hidden", j - 2))
                        r = features(banks[4 + 2 * (j % 2) + (kind == "up")], w_of(n), 0)
                    r.then_inc(*T.done(pre + "unit", n))
                    T.steps[(pre + kind, j)] = T.steps[(pre + "unit", n)]

            def rwkv(l, inject):
                tc = nc.tensor
                pe.wait_ge(*A.of("tanh", l))
                for x in range(2):
                    for t in range(4):
                        r = mm(banks[2 * x + t // 2][:, (t % 2) * SEQ:(t % 2 + 1) * SEQ],
                               pr(f"lora{l}", t * P, P)[64 * x:64 * x + 64, :], wa[64 * x:64 * x + 64, :],
                               start=True, stop=True)
                    r.then_inc(*T.done("lora", l, x))
                inject()
                pe.wait_ge(*A.of("kksq", l))
                pe.wait_ge(*A.of("aa", l))
                for i in range(2):
                    mm(banks[i], ct("ones64"), flat(t3)[:, i * 512:(i + 1) * 512], start=True, stop=True)\
                        .then_inc(*T.done("kksum", l, i))
                inject()
                n = 0
                for x, src, ready in ((2, v_, V.of("shift", l, 5)), (0, b_, V.of("bn", l)), (1, k_, V.of("kt", l))):
                    pe.wait_ge(*ready)
                    for tb in range(TB):
                        if n >= 2:
                            pe.wait_ge(*A.of("tm", l, n - 2))
                        elif n == 0:
                            pe.wait_ge(*V.of("kkms", l))
                        for t in range(4):
                            r = tc.transpose(banks[2 + n % 2][:, t * P:(t + 1) * P], src[:, t, tb * P:(tb + 1) * P],
                                             ct("ident"))
                        r.then_inc(*T.done("tm", l, n))
                        n += 1
                inject()
                pe.wait_ge(*V.of("rk", l))
                for tb in range(TB):
                    for t in range(4):
                        r = mm(banks[0][:, tb * 8 + 2 * t:tb * 8 + 2 * t + 2], t0[:, t, tb * P:(tb + 1) * P],
                               ct("heads2"), start=True, stop=True)
                r.then_inc(*T.done("bonus", l))
                pe.wait_ge(*V.of("bonus", l))
                pe.wait_ge(*V.of("rt", l))
                pe.wait_ge(*V.of("at", l))
                pe.wait_ge(*A.of("tm", l, 5))
                for p in range(TB):
                    cols = slice(p * P, (p + 1) * P)
                    for h in range(8):
                        bs, t = slice(64 * (h % 2), 64 * (h % 2) + 64), h // 2
                        if h >= 2:
                            pe.wait_ge(*V.of("gram", l, p, h - 2))
                        elif p:
                            pe.wait_ge(*A.of("o", l, 1) if h == 0 else V.of("state", l, 1))
                            pe.wait_ge(*V.of("us", l, 1))
                        bank = banks[h % 2]
                        mm(bank[:, 0:128], b_[bs, t, cols], a_[bs, t, cols], start=True, stop=True)
                        mm(bank[:, 128:256], b_[bs, t, cols], r_[bs, t, cols], start=True, stop=True)
                        mm(bank[:, 256:384], k_[bs, t, cols], a_[bs, t, cols], start=True, stop=True)
                        mm(bank[:, 384:512], k_[bs, t, cols], r_[bs, t, cols], start=True, stop=True)\
                            .then_inc(*T.done("gram", l, p, h))
                        r = mm(banks[2 + h % 2][:, t * P:(t + 1) * P], a_[bs, t, cols], b_[bs, t, cols],
                               start=True, stop=True)
                        if h >= 6:
                            r.then_inc(*T.done("m", l, p, h % 2))
                    inject()
                    for lv in range(5):
                        for g in range(2):
                            hs = range(4 * g, 4 * g + 4)
                            if lv == 0:
                                pe.wait_ge(*G.of("first", l, p, g))
                                pe.wait_ge(*V.of("gram", l, p, 7))
                            else:
                                pe.wait_ge(*V.of("inv", l, p, lv - 1, g))
                            pe.wait_ge(*G.of("off", l, p, lv, g))
                            for h in hs:
                                r = mm(banks[2 * g][:, (h % 4) * P:(h % 4 + 1) * P], off[:, h, :], tri[:, h, :],
                                       start=True, stop=True)
                            r.then_inc(*T.done("lev", l, p, lv, g))
                        for g in range(2):
                            hs = range(4 * g, 4 * g + 4)
                            pe.wait_ge(*A.of("lev", l, p, lv, g))
                            if lv < 4:
                                for h in hs:
                                    mm(banks[2 * g + 1][:, (h % 4) * P:(h % 4 + 1) * P], inv[:, h, :], lev[:, h, :],
                                       start=True, stop=True)
                            for h in hs:
                                r = mm(banks[2 * g][:, (h % 4) * P:(h % 4 + 1) * P], lev[:, h, :], inv[:, h, :],
                                       start=True, stop=True)
                            r.then_inc(*T.done("inv", l, p, lv, g))
                        if lv % 2 == 1:
                            inject()
                    for cc in range(2):
                        c = 2 * p + cc
                        ch = slice(64 * cc, 64 * cc + 64)
                        tc_ = slice(c * 64, c * 64 + 64)
                        if c == 0 or cc == 0:
                            pe.wait_ge(*V.of("inv", l, p, 4, 0))
                            pe.wait_ge(*V.of("inv", l, p, 4, 1))
                        if c:
                            pe.wait_ge(*V.of("state", l, c - 1))
                            pe.wait_ge(*A.of("o", l, c - 1))
                        for t in range(4):
                            dst = banks[0][ch, t * P:(t + 1) * P]
                            if c:
                                mm(dst, a_[:, t, tc_], state[:, t, :], start=True, stop=False)
                            for x in range(2):
                                r = mm(dst[:, x * HD:(x + 1) * HD], gram[:, 4 * x + t, 256 + 64 * cc:320 + 64 * cc],
                                       tm[:, 2, p, t * P + x * HD:t * P + (x + 1) * HD], start=(c == 0), stop=(c == 0 or x == 1))
                        r.then_inc(*T.done("x", l, c))
                        pe.wait_ge(*A.of("xs", l, c))
                        for h in range(8):
                            r = mm(banks[1][ch, h * 64:h * 64 + 64], inv[:, 4 * (h % 2) + h // 2, ch],
                                   xs[:, h * 64:h * 64 + 64], start=True, stop=True)
                        r.then_inc(*T.done("u", l, c))
                        pe.wait_ge(*V.of("us", l, c))
                        for t in range(4):
                            dst, two = banks[3][:, t * P:(t + 1) * P], slice(t * P, (t + 1) * P)
                            mm(dst, tm[ch, 0, p, two], us[ch, two], start=True, stop=False)
                            r = mm(dst, tm[ch, 1, p, two], tm[ch, 2, p, two], start=False, stop=True)
                        r.then_inc(*T.done("s", l, c))
                        for t in range(4):
                            dst = banks[2][ch, t * P:(t + 1) * P]
                            if c:
                                mm(dst, r_[:, t, tc_], state[:, t, :], start=True, stop=False)
                            for x in range(2):
                                d, hv = dst[:, x * HD:(x + 1) * HD], slice(t * P + x * HD, t * P + (x + 1) * HD)
                                mm(d, gram[:, 4 * x + t, 128 + 64 * cc:192 + 64 * cc], us[:, hv], start=(c == 0), stop=False)
                                r = mm(d, gram[:, 4 * x + t, 384 + 64 * cc:448 + 64 * cc], tm[:, 2, p, hv],
                                       start=False, stop=(c == 0 or x == 1))
                        r.then_inc(*T.done("o", l, c))
                    inject()
                for tb in range(TB):
                    pe.wait_ge(*V.of("state", l, 3))
                    pe.wait_ge(*A.of("o", l, 3))
                    r = mm(banks[tb], pg[:, tb * P:(tb + 1) * P], pr(f"g2{l}", 0, 512), start=True, stop=True)
                r.then_inc(*T.done("outgate", l))

            def mixer(l, u0):
                ready = [V.of("final_x", DEPTH - 1) if l == 0 else V.of("x2", 0, tb) for tb in range(TB)]
                if l:
                    pe.wait_ge(*G.of("x2", 0))
                turn_wide(xr, "b2", l, ready)

                def unit(n):
                    u = u0 + n
                    pe.wait_ge(*loaded(u))
                    if n == 0:
                        pe.wait_ge(*A.of("xT", "b2", l))
                        pe.wait_ge(*V.of("xT", "b2", l))
                    if n >= 4:
                        pe.wait_ge(*(V.of("shift", l, n - 4) if n - 4 < 7 else A.of("in2", l, n - 4)))
                    features(banks[4 + n % 4], slot(u), l).then_inc(*T.done("unit", u))
                for n in range(7):
                    unit(n)
                left = list(range(7, N_IN2))

                def inject():
                    if left:
                        unit(left.pop(0))
                    if left and len(left) % 2:
                        unit(left.pop(0))
                rwkv(l, inject)
                while left:
                    unit(left.pop(0))
                pe.wait_ge(*V.of("confconv", l))
                pe.wait_ge(*V.of("gated", l))
                for i in range(2):
                    r = mm(banks[2][:, 0:SEQ], ct("mean256"), ctmp[:, i, :], start=(i == 0), stop=(i == 1))
                r.then_inc(*T.done("confmean", l))
                pe.wait_ge(*A.of("confsq", l))
                for i in range(2):
                    r = mm(banks[3][:, 0:SEQ], ct("mean256"), conf[:, i, :], start=(i == 0), stop=(i == 1))
                r.then_inc(*T.done("confvar", l))
                for t in range(4):
                    for tb in range(TB):
                        r = nc.tensor.transpose(banks[t // 2][:, (t % 2) * SEQ + tb * P:(t % 2) * SEQ + (tb + 1) * P],
                                                rwo[:, tb, t * P:(t + 1) * P], ct("ident"))
                r.then_inc(*T.done("rwoT", l))
                pe.wait_ge(*A.of("rwoT", l))
                pe.wait_ge(*A.of("confy", l))
                pe.wait_ge(*V.of("shorty", l))
                for n in range(N_IN2 - 4, N_IN2):
                    pe.wait_ge(*A.of("in2", l, n))
                project(l, "b2", (4, 2, 2), u0 + N_IN2)
                project_out(l, "b2", u0 + N_IN2 + N_PROJ)
                pe.wait_ge(*G.of("x1", l))
                turn_wide(xr, "f2", l, [V.of("x1", l, tb) for tb in range(TB)])

            for l in range(min(DEPTH, n_stages)):
                block1(l)
            if n_stages >= 3:
                mixer(0, MIX2_0)

                def first0():
                    pe.wait_ge(*A.of("xT", "f2", 0))
                    pe.wait_ge(*V.of("xT", "f2", 0))
                swiglu("dense_", lambda n: slot(FFN_0 + n), lambda n: loaded(FFN_0 + n), first0, lambda: None)
                for n in range(FFN):
                    T.steps[("unit", FFN_0 + n)] = T.steps[("dense_unit", n)]
            if n_stages == 4:
                mixer(1, MIX2_1)
                pe.wait_ge(*A.of("xT", "f2", 1))
                pe.wait_ge(*V.of("xT", "f2", 1))
                for tb in range(TB):
                    for k in range(KT):
                        r = mm(banks[0][:, tb * 8:tb * 8 + 8], xk[:, k, tb * P:(tb + 1) * P],
                               pr("router", k * N_EXP, N_EXP), start=(k == 0), stop=(k == KT - 1))
                r.then_inc(*T.done("router"))
                pe.wait_ge(*V.of("routed"))

                def expert(e, peeled):
                    where["expert"] = e

                    def wait_acc():
                        if not peeled:
                            pe.wait_ge(*V.before("acc"))

                    def wait_up():
                        if not peeled:
                            pe.wait_ge(*V.before("moe_hidden", FJ - 1))
                    swiglu("moe_", moe_slot, lambda n: moe_loaded(n, e), wait_up, wait_acc)
                T.enter()
                expert(0, True)
                T.again()
                with pe.Fori(1, N_EXP) as e:
                    expert(e, False)
                T.leave()
                where["expert"] = None

        @block.scalar
        def _(sc):
            act_ = nc.scalar.activation

            def xT_out(tag, l, gain):
                for k in (0, 1, 4, 5):
                    sc.wait_ge(*T.of("turned", tag, l, k | 1))
                    src = banks[k // 2][:, (k % 2) * SEQ:(k % 2 + 1) * SEQ]
                    act_(xk[:, k, :], src, ACT.Copy, scale=pr(gain, k) if gain else 1.0)\
                        .then_inc(*A.done("xT", tag, l))

            def rms_sums(tag, l, ready):
                for tb in range(TB):
                    for s in ready:
                        sc.wait_ge(*s)
                    act_(junk, xr[:, tb, :], ACT.Square, accum_out=sm(f"ss{tag}", 2)[:, tb:tb + 1])\
                        .then_inc(*A.done("ss", tag, l, tb))
                    sc.wait_ge(*A.last())

            def block1(l):
                u0 = l * LAYER1
                if l == 0:
                    sc.wait_ge(s_x, 16)
                    sc.wait_ge(s_par, 16)
                rms_sums("b1", l, [] if l == 0 else [V.of("x_out", "f1", l - 1)])
                sc.wait_ge(*V.of("lamsum", l))
                act_(sm("lamexp", 2), sm("lamsum", 2), ACT.Exp).then_inc(*A.done("lamexp", l))
                xT_out("b1", l, f"attn_norm{l}")

                def unit(n):
                    u = u0 + n
                    bank = banks[4 + n % 4]
                    sc.wait_ge(*T.of("unit", u))
                    if n == 0 and l:
                        sc.wait_ge(*V.of("merged", "b1", l - 1, 11))
                    if n in (2, 8):
                        c = 0 if n == 2 else 384
                        act_(vtm[:, :, c:c + 256], bank.rearrange("p (b n) -> p b n", b=TB), ACT.Copy)\
                            .then_inc(*A.done("in1", l, n))
                    elif n == 5:
                        act_(qk[:, 8 * SEQ:9 * SEQ], bank[:, 0:SEQ], ACT.Copy).then_inc(*A.done("q8", l))
                        act_(squares[:, 8 * SEQ:9 * SEQ], bank[:, 0:SEQ], ACT.Square).then_inc(*A.done("square", l, 8))
                        act_(vtm[:, :, 256:384], bank[:, SEQ:2 * SEQ].rearrange("p (b n) -> p b n", b=TB), ACT.Copy)\
                            .then_inc(*A.done("in1", l, n))
                    elif n < 9:
                        c = QK_TILES[2 * n]
                        act_(squares[:, c * SEQ:(c + 2) * SEQ], bank, ACT.Square).then_inc(*A.done("square", l, c + 1))
                        act_(qk[:, c * SEQ:(c + 2) * SEQ], bank, ACT.Copy).then_inc(*A.done("in1", l, n))
                    else:
                        act_(gk[:, 2 * (n - 9):2 * (n - 9) + 2, :], bank.rearrange("p (b n) -> p b n", b=2), ACT.Exp,
                             scale=-1.0).then_inc(*A.done("in1", l, n))

                for n in range(9):
                    unit(n)
                for i, (c, m) in enumerate(QK_PAIRS):
                    if i < 5:
                        unit(9 + i)
                    if i >= 2:
                        sc.wait_ge(*V.of("qn", l, i - 2))
                    sc.wait_ge(*T.of("sumsq", l, i))
                    act_(rs[:, i % 2, 0:m * SEQ], banks[i % 2][:, 0:m * SEQ], ACT.Sqrt, bias=sm("rms_eps", 1),
                         scale=1.0 / (HD if c < 9 else 32)).then_inc(*A.done("qrms", l, i))
                for kind, n in SCHED:
                    if kind == "gate":
                        unit(9 + n)
                        continue
                    br = JOBS[n][0]
                    scale = 32 ** -0.5 if br[0] == "c" else HD ** -0.5
                    if kind == "score":
                        sc.wait_ge(*V.of("negmax", l, n))
                        if n >= 3:
                            if JOBS[n - 3][0] != "c0":
                                sc.wait_ge(*T.of("turnp", l, n - 3))
                            else:
                                sc.wait_ge(*V.of("prob", l, n - 2))
                        for i, s in enumerate((slice(0, 128), slice(128, 384))):
                            act_(prob[:, n % 3, s], msk[:, n % 2, s], ACT.Exp, bias=sm(f"negmax{n % 2}", 2)[:, i:i + 1],
                                 scale=scale, accum_out=sm(f"rowsum{n % 2}", 2)[:, i:i + 1])\
                                .then_inc(*A.done("exp", l, n))
                        if br == "b":
                            act_(sm(f"sinkexp{n % 2}", 2), sm(f"negmax{n % 2}", 2), ACT.Exp,
                                 bias=pr(f"sinks{l}", JOBS[n][1])).then_inc(*A.done("exp", l, n))
                    elif kind == "turn" and br != "c0":
                        sc.wait_ge(*T.of("turnp", l, n))
                        m = [i for i in range(n - 1) if JOBS[i][0] != "c0" and i % 2 == n % 2]
                        if m:
                            sc.wait_ge(*T.of("value", l, m[-1]))
                        act_(probT[:, n % 2, :], banks[2][:, 0:384], ACT.Copy).then_inc(*A.done("probT", l, n))
                    elif kind == "value" and br != "c0" and JOBS[n][3] == 64:
                        ot = JOBS[n][2]
                        sc.wait_ge(*T.of("value", l, n))
                        if ot == 0:
                            sc.wait_ge(*T.of("rotated", l, len(QK_PAIRS) - 1))
                            sc.wait_ge(*T.of("sumsq", l, len(QK_PAIRS) - 1))
                        act_(yk[:, ot, :], banks[3][:, 0:SEQ], ACT.Copy).then_inc(*A.done("y", l, ot))
                for i in range(2):
                    sc.wait_ge(*A.of("y", l, 6 + i))
                    act_(sq[:, 0, i * SEQ:(i + 1) * SEQ], yk[:, 6 + i, :], ACT.Square).then_inc(*A.done("csquare", l, i))
                sc.wait_ge(*T.of("csum", l))
                act_(rs[:, 0, :], banks[0], ACT.Sqrt, bias=sm("rms_eps", 1), scale=1.0 / HD).then_inc(*A.done("crms", l))
                rms_sums("f1", l, [V.of("x_out", "b1", l)])
                xT_out("f1", l, f"mlp_norm{l}")
                for j in range(FJ):
                    for kind, dst, c0 in (("gate", cg, 0), ("up", cv, 22)):
                        sc.wait_ge(*T.of(kind, l, j))
                        if j >= 2:
                            sc.wait_ge(*V.of("hidden1", l, j - 2))
                            sc.wait_ge(*A.of("silu1", l, j - 2))
                        if j == 0:
                            sc.wait_ge(*T.of("unit", u0 + N_IN1 + N_PROJ + N_OUT - 1))
                        for c in range(2):
                            ch = c0 + 2 * j + c
                            act_(dst[:, j % 2, c, :], banks[4 + 2 * (j % 2) + (kind == "up")][:, c * SEQ:(c + 1) * SEQ],
                                 ACT.Identity, scale=pr(f"conv_w{l}", 2 * 44 + ch), bias=pr(f"conv_b{l}", ch))\
                                .then_inc(*A.done("tap2", kind, l, j))
                    sc.wait_ge(*V.of("conv", "gate", l, j))
                    act_(act[:, j % 2, :], flat(cg[:, j % 2, :, :]), ACT.Silu).then_inc(*A.done("silu1", l, j))

            def swiglu(pre, peeled):
                for j in range(FJ):
                    sc.wait_ge(*T.of(pre + "gate", j))
                    if j >= 2:
                        sc.wait_ge(*V.of(pre + "hidden", j - 2))
                    elif not peeled:
                        sc.wait_ge(*V.before(pre + "hidden", FJ - 2 + j))
                    act_(act[:, j % 2, :], banks[4 + 2 * (j % 2)], ACT.Silu).then_inc(*A.done(pre + "silu", j))

            def layer_norm_sums(tag, l, ready):
                for tb in range(TB):
                    sc.wait_ge(*ready[tb])
                    if tb:
                        sc.wait_ge(*A.last())
                    act_(lnjunk, xr[:, tb, :], ACT.Copy, accum_out=sm("lnsum", 2)[:, tb:tb + 1])\
                        .then_inc(*A.done("lnsum", tag, l, tb))
                for tb in range(TB):
                    sc.wait_ge(*V.of("negmean", tag, l))
                    sc.wait_ge(*A.last())
                    act_(lnjunk, xr[:, tb, :], ACT.Square, bias=sm("negmean", 2)[:, tb:tb + 1],
                         accum_out=sm("lnsq", 2)[:, tb:tb + 1]).then_inc(*A.done("lnsq", tag, l, tb))

            def mixer(l, u0):
                xT_out("b2", l, None)

                def unit(n):
                    u = u0 + n
                    bank = banks[4 + n % 4]
                    bv = bank.rearrange("p (b n) -> p b n", b=2)
                    sc.wait_ge(*T.of("unit", u))
                    if n == 0 and l:
                        sc.wait_ge(*T.of("dense_unit", FFN - 1))
                    if n == 0 and l == 0:
                        sc.wait_ge(*V.of("conv", "up", DEPTH - 1, FJ - 1))
                    if n < 7:
                        for c in range(2):
                            act_(rkv[:, 2 * n + c, :], bank[:, c * SEQ:(c + 1) * SEQ], ACT.Identity,
                                 scale=sm(f"omu{l}", 14)[:, 2 * n + c:2 * n + c + 1]).then_inc(*A.done("unshift", l, n))
                    elif n == 8:
                        act_(conf[:, 2:4, :], bv, ACT.Sigmoid).then_inc(*A.done("in2", l, n))
                    elif n < 12:
                        dst = conf[:, 0:2, :] if n == 7 else short[:, 2 * (n - 9):2 * (n - 9) + 2, :]
                        act_(dst, bv, ACT.Copy).then_inc(*A.done("in2", l, n))
                    else:
                        act_(gk[:, 2 * (n - 12):2 * (n - 12) + 2, :], bv, ACT.Sigmoid).then_inc(*A.done("in2", l, n))
                sc.wait_ge(*V.of("omu", l))
                for n in range(7):
                    unit(n)
                left = list(range(7, N_IN2))

                def inject():
                    if left:
                        unit(left.pop(0))
                    if left and len(left) % 2:
                        unit(left.pop(0))
                sc.wait_ge(*V.of("shift", l, 6))
                act_(pg, pg, ACT.Sigmoid).then_inc(*A.done("pg", l))
                act_(wa[0:64, :], wa[0:64, :], ACT.Tanh).then_inc(*A.done("tanh", l))
                for x, dst, bias in ((0, t0, f"w0{l}"), (1, aa, f"a0{l}")):
                    sc.wait_ge(*T.of("lora", l, x))
                    for t in range(4):
                        act_(dst[:, t, :], banks[2 * x + t // 2][:, (t % 2) * SEQ:(t % 2 + 1) * SEQ], ACT.Sigmoid,
                             bias=pr(bias, t)).then_inc(*A.done("sig" if x == 0 else "aa", l))
                for t in range(4):
                    act_(t3[:, t, :], k_[:, t, :], ACT.Square, scale=pr(f"k_k{l}", t)).then_inc(*A.done("kksq", l))
                inject()
                sc.wait_ge(*V.of("kkms", l))
                act_(flat(t3), flat(t3), ACT.Sqrt).then_inc(*A.done("kknorm", l))
                sc.wait_ge(*V.of("cum", l))
                act_(flat(ep), flat(t1), ACT.Exp, scale=-KAPPA).then_inc(*A.done("ep", l))
                sc.wait_ge(*G.of("cumex", l))
                act_(flat(t2), flat(t2), ACT.Exp, scale=-KAPPA).then_inc(*A.done("ex", l))
                sc.wait_ge(*A.of("ep", l))
                act_(flat(t1), flat(t1), ACT.Exp, scale=KAPPA).then_inc(*A.done("en", l))
                inject()
                for n, x in enumerate((2, 2, 0, 0, 1, 1)):
                    sc.wait_ge(*T.of("tm", l, n))
                    act_(tm[:, x, n % 2, :], banks[2 + n % 2], ACT.Copy).then_inc(*A.done("tm", l, n))
                inject()
                for p in range(TB):
                    inject()
                    for lv in range(5):
                        for g in range(2):
                            sc.wait_ge(*T.of("lev", l, p, lv, g))
                            act_(flat(lev[:, 4 * g:4 * g + 4, :]), banks[2 * g], ACT.Copy)\
                                .then_inc(*A.done("lev", l, p, lv, g))
                        if lv % 2 == 1:
                            inject()
                    for cc in range(2):
                        c = 2 * p + cc
                        ch = slice(64 * cc, 64 * cc + 64)
                        sc.wait_ge(*T.of("x", l, c))
                        act_(xs[ch, :], banks[0][ch, :], ACT.Copy).then_inc(*A.done("xs", l, c))
                        sc.wait_ge(*T.of("o", l, c))
                        act_(rwo[ch, p, :], banks[2][ch, :], ACT.Copy).then_inc(*A.done("o", l, c))
                    inject()
                while left:
                    unit(left.pop(0))
                for i in range(2):
                    sc.wait_ge(*V.of("confcent", l))
                    act_(conf[:, i, :], ctmp[:, i, :], ACT.Square).then_inc(*A.done("confsq", l))
                sc.wait_ge(*T.of("confvar", l))
                act_(stmp[:, 0:SEQ], banks[3][:, 0:SEQ], ACT.Sqrt, bias=sm("ln_eps", 1)).then_inc(*A.done("confrms", l))
                sc.wait_ge(*T.of("rwoT", l))
                for t in range(2):
                    act_(yk[:, 2 * t:2 * t + 2, :], banks[t].rearrange("p (b n) -> p b n", b=2), ACT.Copy)\
                        .then_inc(*A.done("rwoT", l))
                sc.wait_ge(*V.of("confn", l))
                for i in range(2):
                    act_(yk[:, 4 + i, :], ctmp[:, i, :], ACT.Silu, scale=pr(f"conf_g{l}", i),
                         bias=pr(f"conf_lb{l}", i)).then_inc(*A.done("confy", l))
                layer_norm_sums("ln1", l, [V.of("mix", l, tb) for tb in range(TB)])
                xT_out("f2", l, None)

            lnjunk = Z[:, 12288:12288 + D]
            for l in range(min(DEPTH, n_stages)):
                block1(l)
            if n_stages >= 3:
                mixer(0, MIX2_0)
                swiglu("dense_", True)
                layer_norm_sums("ln2", 0, [V.of("res2", 0, tb) for tb in range(TB)])
            if n_stages == 4:
                mixer(1, MIX2_1)
                sc.wait_ge(*V.of("negtop"))
                for tb in range(TB):
                    act_(sm("wexp", 16)[:, 8 * tb:8 * tb + 8], sm("logit", 16)[:, 8 * tb:8 * tb + 8], ACT.Exp,
                         bias=sm("negtop", 2)[:, tb:tb + 1]).then_inc(*A.done("wexp"))
                A.enter()
                where["expert"] = 0
                swiglu("moe_", True)
                A.again()
                with sc.Fori(1, N_EXP) as e:
                    where["expert"] = e
                    swiglu("moe_", False)
                A.leave()
                where["expert"] = None
                layer_norm_sums("ln2", 1, [V.of("res2", 1, tb) for tb in range(TB)])

        @block.vector
        def _(ve):
            v = nc.vector

            def own():
                ve.wait_ge(*V.last())

            def xT_out(tag, l, gain):
                for k in (2, 3, 6, 7):
                    ve.wait_ge(*T.of("turned", tag, l, k | 1))
                    src = banks[k // 2][:, (k % 2) * SEQ:(k % 2 + 1) * SEQ]
                    if gain:
                        v.tensor_scalar(xk[:, k, :], src, pr(gain, k), None, ALU.mult).then_inc(*V.done("xT", tag, l))
                    else:
                        v.tensor_copy(xk[:, k, :], src).then_inc(*V.done("xT", tag, l))

            def rms_apply(tag, l):
                ve.wait_ge(*A.of("ss", tag, l, 1))
                v.tensor_scalar(sm("ms", 2), sm(f"ss{tag}", 2), 1.0 / D, RMS_EPS, ALU.mult, ALU.add)\
                    .then_inc(*V.done("rms", tag, l))
                ve.wait_ge(*G.of("rstd", tag, l))
                for tb in range(TB):
                    v.tensor_scalar(wide[:, tb, :], xr[:, tb, :], sm("rstd", 2)[:, tb:tb + 1], None, ALU.mult)\
                        .then_inc(*V.done("normed", tag, l, tb))

            def residual(tag, l, last):
                ve.wait_ge(*last)
                for tb in range(TB):
                    for half in range(2):
                        d = xr[:, tb, half * 512:(half + 1) * 512]
                        v.tensor_tensor(d, d, banks[2 * tb + half], ALU.add).then_inc(*V.done("x_out", tag, l))

            def merge(blk, l):
                for c in range(4):
                    g = [flat(gk[:, 8 * b + 2 * c:8 * b + 2 * c + 2, :]) for b in range(3)]
                    for b in range(3):
                        n = 3 * c + b
                        ve.wait_ge(*T.of("branch", blk, l, n))
                        v.tensor_tensor(g[b], g[b], banks[4 + n % 4], ALU.mult).then_inc(*V.done("merged", blk, l, n))
                        own()
                        if b:
                            v.tensor_tensor(g[0], g[0], g[b], ALU.add).then_inc(*V.done("merged", blk, l, n))
                            own()

            def block1(l):
                u0 = l * LAYER1
                if l == 0:
                    v.memset(sm("rms_eps", 1), RMS_EPS).then_inc(*V.done("eps"))
                    v.memset(sm("ln_eps", 1), LN_EPS).then_inc(*V.done("eps"))
                    ve.wait_ge(s_par, 16)
                    ve.wait_ge(s_const, 16)
                    ve.wait_ge(s_x, 16)
                lam = pr(f"lam{l}", 0, 128)
                for i in range(2):
                    v.tensor_tensor(sm(f"lamprod{i}", 32), lam[:, 64 * i:64 * i + 32], lam[:, 64 * i + 32:64 * i + 64], ALU.mult)\
                        .then_inc(*V.done("lamprod", l))
                own()
                for i in range(2):
                    v.tensor_reduce(sm("lamsum", 2)[:, i:i + 1], sm(f"lamprod{i}", 32), AX.X, ALU.add)\
                        .then_inc(*V.done("lamsum", l))
                lam_init = 0.8 - 0.6 * float(np.exp(-0.3 * l))
                ve.wait_ge(*A.of("lamexp", l))
                v.scalar_tensor_tensor(out=sm("neglam", 1), in0=sm("lamexp", 2)[:, 1:2], scalar=-lam_init,
                                       in1=sm("lamexp", 2)[:, 0:1], op0=ALU.add, op1=ALU.subtract)\
                    .then_inc(*V.done("neglam", l))
                v.tensor_scalar(sm("negsink", 8), pr(f"sinks{l}", 0, 8), -1.0, None, ALU.mult).then_inc(*V.done("negsink", l))
                v.tensor_scalar(sm("sublnk", 1), pr(f"subln{l}", 0), 1.0 - lam_init, None, ALU.mult)\
                    .then_inc(*V.done("sublnk", l))
                rms_apply("b1", l)
                xT_out("b1", l, f"attn_norm{l}")
                def qk_norm(i):
                    c, m = QK_PAIRS[i]
                    w, dim = m * SEQ, HD if c < 9 else 32
                    b = i % 2
                    ve.wait_ge(*A.of("qrms", l, i))
                    v.reciprocal(rs[:, b, 0:w], rs[:, b, 0:w]).then_inc(*V.done("qrstd", l, i))
                    own()
                    ve.wait_ge(*A.of("in1", l, 8))
                    for j in range(m):
                        q = qk[:, (c + j) * SEQ:(c + j + 1) * SEQ]
                        v.scalar_tensor_tensor(out=q, in0=q, scalar=pr(f"q_gain{l}", c + j),
                                               in1=rs[:, b, j * SEQ:(j + 1) * SEQ], op0=ALU.mult, op1=ALU.mult)\
                            .then_inc(*V.done("qn", l, i))

                def qk_rot(i):
                    c, m = QK_PAIRS[i]
                    w, dim = m * SEQ, "64" if c < 9 else "32"
                    ve.wait_ge(*T.of("rotated", l, i))
                    if i >= 2:
                        ve.wait_ge(*G.of("roped", l, i - 2))
                    v.tensor_tensor(halves(rot[:, i % 2, 0:w]), halves(banks[2 + i % 2][:, 0:w]),
                                    grow(ct("sin" + dim), [P, m, SEQ], 1), ALU.mult)\
                        .then_inc(*V.done("rotsin", l, i))
                for i in range(len(QK_PAIRS)):
                    qk_norm(i)
                    if i:
                        qk_rot(i - 1)
                qk_rot(len(QK_PAIRS) - 1)

                def gate_recip(n):
                    ve.wait_ge(*G.of("gate1p", l, n))
                    g = flat(gk[:, 2 * n:2 * n + 2, :])
                    v.reciprocal(g, g).then_inc(*V.done("gate", l, n))
                for n in range(5):
                    gate_recip(n)
                pend = []
                for kind, n in SCHED:
                    if kind == "gate":
                        pend.append(n)
                        if len(pend) > 1:
                            gate_recip(pend.pop(0))
                        continue
                    br, h = JOBS[n][0], JOBS[n][1]
                    scale = 32 ** -0.5 if br[0] == "c" else HD ** -0.5
                    nm, rsm, se = sm(f"negmax{n % 2}", 2), sm(f"rowsum{n % 2}", 2), sm(f"sinkexp{n % 2}", 2)
                    if kind == "score":
                        mask = ct("window" if br == "b" else "causal")
                        own()
                        ve.wait_ge(*T.of("score", l, n))
                        if n >= 2:
                            ve.wait_ge(*A.of("exp", l, n - 2))
                            ve.wait_ge(*V.of("prob", l, n - 2))
                        for i, s in enumerate((slice(0, 128), slice(128, 384))):
                            v.tensor_tensor_reduce(out=msk[:, n % 2, s], in0=banks[n % 2][:, s], in1=mask[:, s], scale=1.0,
                                                   scalar=-3.0e38, op0=ALU.add, op1=ALU.max,
                                                   accum_out=sm("rowmax", 2)[:, i:i + 1]).then_inc(*V.done("masked", l, n))
                        own()
                        if br == "b":
                            v.tensor_scalar(nm, sm("rowmax", 2), -scale, sm("negsink", 8)[:, h:h + 1], ALU.mult, ALU.min)\
                                .then_inc(*V.done("negmax", l, n))
                        else:
                            v.tensor_scalar(nm, sm("rowmax", 2), -scale, None, ALU.mult).then_inc(*V.done("negmax", l, n))
                    elif kind == "norm":
                        ve.wait_ge(*A.of("exp", l, n))
                        if br == "b":
                            v.tensor_tensor(rsm, rsm, se, ALU.add).then_inc(*V.done("den", l, n))
                            own()
                        v.reciprocal(rsm, rsm).then_inc(*V.done("rden", l, n))
                        own()
                        if br == "c1":
                            v.tensor_scalar(rsm, rsm, sm("neglam", 1), None, ALU.mult).then_inc(*V.done("rlam", l, n))
                            own()
                        for i, s in enumerate((slice(0, 128), slice(128, 384))):
                            pb = prob[:, n % 3, s]
                            if br == "c1":
                                v.scalar_tensor_tensor(out=pb, in0=pb, scalar=rsm[:, i:i + 1],
                                                       in1=prob[:, (n - 1) % 3, s], op0=ALU.mult, op1=ALU.add)\
                                    .then_inc(*V.done("prob", l, n))
                            else:
                                v.tensor_scalar(pb, pb, rsm[:, i:i + 1], None, ALU.mult).then_inc(*V.done("prob", l, n))
                        own()
                for n in pend:
                    gate_recip(n)
                ve.wait_ge(*A.of("crms", l))
                v.reciprocal(rs[:, 0, :], rs[:, 0, :]).then_inc(*V.done("crstd", l))
                own()
                for i in range(2):
                    ve.wait_ge(*A.of("csquare", l, i))
                    v.scalar_tensor_tensor(out=yk[:, 6 + i, :], in0=yk[:, 6 + i, :], scalar=sm("sublnk", 1),
                                           in1=rs[:, 0, i * SEQ:(i + 1) * SEQ], op0=ALU.mult, op1=ALU.mult)\
                        .then_inc(*V.done("cnormed", l))
                merge("b1", l)
                residual("b1", l, T.of("unit", u0 + N_IN1 + N_PROJ + N_OUT - 1))
                rms_apply("f1", l)
                xT_out("f1", l, f"mlp_norm{l}")
                for j in range(FJ):
                    for kind, dst, c0 in (("gate", cg, 0), ("up", cv, 22)):
                        ve.wait_ge(*A.of("tap2", kind, l, j))
                        bank = banks[4 + 2 * (j % 2) + (kind == "up")]
                        for tap in (1, 0):
                            lag = 2 - tap
                            for c in range(2):
                                d = dst[:, j % 2, c, lag:SEQ]
                                v.scalar_tensor_tensor(out=d, in0=bank[:, c * SEQ:(c + 1) * SEQ - lag],
                                                       scalar=pr(f"conv_w{l}", tap * 44 + c0 + 2 * j + c), in1=d,
                                                       op0=ALU.mult, op1=ALU.add).then_inc(*V.done("conv", kind, l, j))
                            own()
                    ve.wait_ge(*A.of("silu1", l, j))
                    if j >= 2:
                        ve.wait_ge(*T.of("down", l, j - 2))
                    v.tensor_tensor(flat(hid[:, j % 2, :, :]), act[:, j % 2, :], flat(cv[:, j % 2, :, :]), ALU.mult)\
                        .then_inc(*V.done("hidden1", l, j))
                residual("f1", l, T.of("down", l, FJ - 1))
                V.steps[("final_x", l)] = V.steps[("x_out", "f1", l)]

            def swiglu(pre, peeled):
                for j in range(FJ):
                    ve.wait_ge(*A.of(pre + "silu", j))
                    ve.wait_ge(*T.of(pre + "up", j))
                    if j >= 2:
                        ve.wait_ge(*T.of(pre + "down", j - 2))
                    elif not peeled:
                        ve.wait_ge(*T.before(pre + "down", FJ - 2 + j))
                    v.tensor_tensor(flat(hid[:, j % 2, :, :]), act[:, j % 2, :], banks[4 + 2 * (j % 2) + 1], ALU.mult)\
                        .then_inc(*V.done(pre + "hidden", j))

            def layer_norm(tag, l, out_key):
                ve.wait_ge(*A.of("lnsum", tag, l, 1))
                v.tensor_scalar(sm("negmean", 2), sm("lnsum", 2), -1.0 / D, None, ALU.mult).then_inc(*V.done("negmean", tag, l))
                ve.wait_ge(*A.of("lnsq", tag, l, 1))
                v.tensor_scalar(sm("ms", 2), sm("lnsq", 2), 1.0 / D, LN_EPS, ALU.mult, ALU.add)\
                    .then_inc(*V.done("lnvar", tag, l))
                ve.wait_ge(*G.of("lnrstd", tag, l))
                ve.wait_ge(s_norm_rows, 16 * (2 * l + (2 if tag == "ln2" else 1)))
                for tb in range(TB):
                    v.tensor_scalar(xr[:, tb, :], xr[:, tb, :], sm("negmean", 2)[:, tb:tb + 1],
                                    sm("rstd", 2)[:, tb:tb + 1], ALU.add, ALU.mult).then_inc(*V.done("lnn", tag, l))
                    own()
                    v.tensor_tensor(xr[:, tb, :], xr[:, tb, :], norm_rows[:, 0:D], ALU.mult)\
                        .then_inc(*V.done(out_key, l, tb))

            def mixer(l, u0):
                if l == 0:
                    for i in range(DEPTH):
                        v.tensor_scalar(sm(f"omu{i}", 14), pr(f"mu{i}", 0, 14), -1.0, 1.0, ALU.mult, ALU.add)\
                            .then_inc(*V.done("omu", i))
                        v.tensor_scalar(sm(f"oka{i}", 4), pr(f"k_a{i}", 0, 4), -1.0, 1.0, ALU.mult, ALU.add)\
                            .then_inc(*V.done("oka", i))
                if l == 0:
                    for buf in (xs, us):
                        v.memset(buf, 0.0).then_inc(*V.done("zeroed"))
                xT_out("b2", l, None)
                for n in range(7):
                    ve.wait_ge(*A.of("unshift", l, n))
                    for c in range(2):
                        d = rkv[:, 2 * n + c, 1:SEQ]
                        v.scalar_tensor_tensor(out=d, in0=banks[4 + n % 4][:, c * SEQ:(c + 1) * SEQ - 1],
                                               scalar=pr(f"mu{l}", 2 * n + c), in1=d, op0=ALU.mult, op1=ALU.add)\
                            .then_inc(*V.done("shift", l, n))
                own()
                for t in range(4):
                    v.tensor_scalar(kk[:, t, :], k_[:, t, :], pr(f"k_k{l}", t), None, ALU.mult).then_inc(*V.done("kkr", l))
                ve.wait_ge(*A.of("sig", l))
                for t in range(4):
                    v.tensor_tensor_scan(t1[:, t, :], ct("reset"), t0[:, t, :], 0.0, ALU.mult, ALU.add)\
                        .then_inc(*V.done("cum", l))
                for i in range(2):
                    ve.wait_ge(*T.of("kksum", l, 1))
                    v.tensor_scalar(flat(t3)[:, i * 512:(i + 1) * 512], banks[i], 1e-24, None, ALU.max)\
                        .then_inc(*V.done("kkms", l))
                ve.wait_ge(*A.of("kknorm", l))
                v.reciprocal(flat(t3), flat(t3)).then_inc(*V.done("kkrn", l))
                own()
                v.tensor_tensor(flat(kk), flat(kk), flat(t3), ALU.mult).then_inc(*V.done("kk", l))
                own()
                ve.wait_ge(*A.of("ex", l))
                v.tensor_tensor(flat(a_), flat(kk), flat(t2), ALU.mult).then_inc(*V.done("at", l))
                v.tensor_tensor(flat(kk), flat(kk), flat(aa), ALU.mult).then_inc(*V.done("ka", l))
                own()
                ve.wait_ge(*A.of("en", l))
                v.scalar_tensor_tensor(out=flat(b_), in0=flat(kk), scalar=-1.0, in1=flat(t1), op0=ALU.mult, op1=ALU.mult)\
                    .then_inc(*V.done("bn", l))
                own()
                for t in range(4):
                    v.tensor_scalar(kk[:, t, :], aa[:, t, :], pr(f"k_a{l}", t), sm(f"oka{l}", 4)[:, t:t + 1],
                                    ALU.mult, ALU.add).then_inc(*V.done("kscale", l))
                own()
                v.tensor_tensor(flat(k_), flat(k_), flat(kk), ALU.mult).then_inc(*V.done("k2", l))
                own()
                ve.wait_ge(*G.of("cumex", l))
                for t in range(4):
                    v.scalar_tensor_tensor(out=t0[:, t, :], in0=r_[:, t, :], scalar=pr(f"r_k{l}", t), in1=k_[:, t, :],
                                           op0=ALU.mult, op1=ALU.mult).then_inc(*V.done("rk", l))
                own()
                v.tensor_tensor(flat(k_), flat(k_), flat(t1), ALU.mult).then_inc(*V.done("kt", l))
                v.tensor_tensor(flat(r_), flat(r_), flat(ep), ALU.mult).then_inc(*V.done("rt", l))
                v.tensor_copy(sm("ends", 16), flat(ep).rearrange("p (c s) -> p c s", s=CHUNK)[:, :, CHUNK - 1])\
                    .then_inc(*V.done("ends", l))
                ve.wait_ge(*T.of("bonus", l))
                v.tensor_copy(sm("bonus", 16), banks[0][:, 0:16]).then_inc(*V.done("bonus", l))
                ends = sm("ends", 16).rearrange("p (t c) -> p t c", t=4)

                def conf_some(k):
                    if not started:
                        started.append(1)
                        ve.wait_ge(*A.of("in2", l, 8))
                        v.tensor_tensor(conf[:, 0:2, :], conf[:, 0:2, :], conf[:, 2:4, :], ALU.mult)\
                            .then_inc(*V.done("confu", l))
                        own()
                        for i in range(2):
                            v.tensor_scalar(ctmp[:, i, :], conf[:, i, :], pr(f"conf_dw{l}", i * 31 + 30),
                                            pr(f"conf_b{l}", i), ALU.mult, ALU.add).then_inc(*V.done("conf30", l))
                        own()
                    for _ in range(k):
                        if not taps:
                            return
                        lag = taps.pop(0)
                        for i in range(2):
                            d = ctmp[:, i, lag:SEQ]
                            v.scalar_tensor_tensor(out=d, in0=conf[:, i, 0:SEQ - lag],
                                                   scalar=pr(f"conf_dw{l}", i * 31 + 30 - lag), in1=d,
                                                   op0=ALU.mult, op1=ALU.add).then_inc(*V.done("confconv", l))
                        own()
                started, taps = [], list(range(1, CONF_TAPS))
                for p in range(TB):
                    for h in range(8):
                        ve.wait_ge(*T.of("gram", l, p, h))
                        if h == 0 and p:
                            ve.wait_ge(*T.of("o", l, 1))
                        v.tensor_tensor(gram[:, 4 * (h % 2) + h // 2, :], banks[h % 2], ct("chunk4"), ALU.mult)\
                            .then_inc(*V.done("gram", l, p, h))
                        if h >= 6:
                            g = h % 2
                            ve.wait_ge(*T.of("m", l, p, g))
                            if p == 0 and g == 0:
                                ve.wait_ge(*A.of("tm", l, 1))
                            v.tensor_tensor(tri[:, 4 * g:4 * g + 4, :], banks[2 + g].rearrange("p (h n) -> p h n", h=4),
                                            grow(ct("first"), [P, 4, P], 1), ALU.mult).then_inc(*V.done("first", l, p, g))
                    for lv in range(5):
                        for g in range(2):
                            ve.wait_ge(*T.of("inv", l, p, lv, g))
                            hs = slice(4 * g, 4 * g + 4)
                            if lv < 4:
                                v.tensor_tensor(flat(tri[:, hs, :]), flat(tri[:, hs, :]), banks[2 * g + 1],
                                                ALU.add).then_inc(*V.done("tri", l, p, lv, g))
                            v.tensor_tensor(flat(inv[:, hs, :]), flat(inv[:, hs, :]), banks[2 * g],
                                            ALU.add).then_inc(*V.done("inv", l, p, lv, g))
                            if p or lv >= 1:
                                conf_some(2)
                    for cc in range(2):
                        c = 2 * p + cc
                        ch = slice(64 * cc, 64 * cc + 64)
                        ve.wait_ge(*T.of("u", l, c))
                        v.tensor_copy(us[ch, :], banks[1][ch, :]).then_inc(*V.done("us", l, c))
                        ve.wait_ge(*T.of("s", l, c))
                        if c:
                            v.tensor_tensor(stmp, flat(state), banks[3], ALU.add).then_inc(*V.done("stmp", l, c))
                            own()
                            ve.wait_ge(*T.of("o", l, c))
                        src = stmp if c else banks[3]
                        for t in range(4):
                            v.scalar_tensor_tensor(out=state[:, t, :], in0=src[:, t * P:(t + 1) * P],
                                                   scalar=ends[:, t, c:c + 1], in1=ct("ones64"), op0=ALU.mult,
                                                   op1=ALU.mult).then_inc(*V.done("state", l, c))
                        own()
                conf_some(99)
                own()
                ve.wait_ge(*A.of("o", l, 3))
                og = rwo.rearrange("p b (h n) -> p (b h) n", n=HD)
                sqv = t0.rearrange("p t n -> p (t n)").rearrange("p (h n) -> p h n", n=HD)
                ve.wait_ge(*T.of("o", l, 3))
                v.tensor_reduce(sm("gsum", 16), og, AX.X, ALU.add).then_inc(*V.done("gsum", l))
                own()
                v.tensor_scalar(sm("gsum", 16), sm("gsum", 16), 1.0 / HD, None, ALU.mult).then_inc(*V.done("gmean", l))
                own()
                v.tensor_tensor(og, og, grow(sm("gsum", 16), [P, 16, HD], 2), ALU.subtract).then_inc(*V.done("gcent", l))
                own()
                v.tensor_tensor(sqv, og, og, ALU.mult).then_inc(*V.done("gsq", l))
                own()
                v.tensor_reduce(sm("gsum", 16), sqv, AX.X, ALU.add).then_inc(*V.done("gvar", l))
                own()
                v.tensor_scalar(sm("gvar", 16), sm("gsum", 16), 1.0 / HD, GN_EPS, ALU.mult, ALU.add).then_inc(*V.done("gms", l))
                tmv = tm[:, 2, :, :].rearrange("p b (h n) -> p (b h) n", n=HD)
                v.tensor_tensor(tmv, tmv, grow(sm("bonus", 16), [P, 16, HD], 2), ALU.mult).then_inc(*V.done("bv", l))
                ve.wait_ge(*G.of("grstd", l))
                v.tensor_tensor(og, og, grow(sm("gvar", 16), [P, 16, HD], 2), ALU.mult).then_inc(*V.done("gn", l))
                own()
                ve.wait_ge(s_group_rows, 16 * (l + 1))
                v.tensor_tensor(rwo, rwo, grow(group_rows[:, 0:512], [P, TB, 512], 1), ALU.mult).then_inc(*V.done("gg", l))
                own()
                v.tensor_tensor(rwo, rwo, grow(group_rows[:, 512:1024], [P, TB, 512], 1), ALU.add).then_inc(*V.done("gb", l))
                own()
                v.tensor_tensor(rwo, rwo, tm[:, 2, :, :], ALU.add).then_inc(*V.done("gbonus", l))
                own()
                ve.wait_ge(*T.of("outgate", l))
                for tb in range(TB):
                    v.tensor_tensor(rwo[:, tb, :], rwo[:, tb, :], banks[tb], ALU.mult).then_inc(*V.done("gated", l))
                ve.wait_ge(*A.of("in2", l, 11))
                v.tensor_tensor(short[:, 2:4, :], short[:, 2:4, :], short[:, 4:6, :], ALU.mult).then_inc(*V.done("shortu", l))
                own()
                for i in range(2):
                    v.tensor_scalar(short[:, 4 + i, :], short[:, 2 + i, :], pr(f"short_dw{l}", 3 * i + 2), None, ALU.mult)\
                        .then_inc(*V.done("short2", l))
                own()
                for lag in (1, 2):
                    for i in range(2):
                        d = short[:, 4 + i, lag:SEQ]
                        v.scalar_tensor_tensor(out=d, in0=short[:, 2 + i, 0:SEQ - lag],
                                               scalar=pr(f"short_dw{l}", 3 * i + 2 - lag), in1=d, op0=ALU.mult,
                                               op1=ALU.add).then_inc(*V.done("shortc", l))
                    own()
                v.tensor_tensor(yk[:, 6:8, :], short[:, 0:2, :], short[:, 4:6, :], ALU.mult).then_inc(*V.done("shorty", l))
                ve.wait_ge(*T.of("confmean", l))
                v.tensor_tensor(ctmp, ctmp, grow(banks[2][:, 0:SEQ], [P, 2, SEQ], 1), ALU.subtract)\
                    .then_inc(*V.done("confcent", l))
                ve.wait_ge(*T.of("confvar", l))
                ve.wait_ge(*A.of("confrms", l))
                v.reciprocal(stmp[:, 0:SEQ], stmp[:, 0:SEQ]).then_inc(*V.done("confrstd", l))
                own()
                ve.wait_ge(*A.of("confsq", l))
                v.tensor_tensor(ctmp, ctmp, grow(stmp[:, 0:SEQ], [P, 2, SEQ], 1), ALU.mult).then_inc(*V.done("confn", l))
                for n in range(N_IN2 - 4, N_IN2):
                    ve.wait_ge(*A.of("in2", l, n))
                merge("b2", l)
                ve.wait_ge(*T.of("unit", u0 + MIX2 - 1))
                for tb in range(TB):
                    for half in range(2):
                        d = xr[:, tb, half * 512:(half + 1) * 512]
                        v.scalar_tensor_tensor(out=d, in0=d, scalar=ALPHA, in1=banks[2 * tb + half], op0=ALU.mult,
                                               op1=ALU.add).then_inc(*V.done("mix", l, tb))
                own()
                layer_norm("ln1", l, "x1")
                V.steps[("mixed", l)] = V.steps[("x1", l, 1)]
                xT_out("f2", l, None)

            for l in range(min(DEPTH, n_stages)):
                block1(l)
            if n_stages >= 3:
                mixer(0, MIX2_0)
                swiglu("dense_", True)
                ve.wait_ge(*T.of("dense_down", FJ - 1))
                for tb in range(TB):
                    for half in range(2):
                        d = xr[:, tb, half * 512:(half + 1) * 512]
                        v.scalar_tensor_tensor(out=d, in0=d, scalar=ALPHA, in1=banks[2 * tb + half], op0=ALU.mult,
                                               op1=ALU.add).then_inc(*V.done("res2", 0, tb))
                own()
                layer_norm("ln2", 0, "x2")
            if n_stages == 4:
                mixer(1, MIX2_1)
                lg, wt = sm("logit", 16), sm("wexp", 16)
                ve.wait_ge(*T.of("router"))
                v.tensor_copy(lg, banks[0][:, 0:16]).then_inc(*V.done("logit"))
                own()
                lv = lg.rearrange("p (b e) -> p b e", b=TB)
                v.tensor_reduce(sm("negtop", 2), lv, AX.X, ALU.max, negate=True).then_inc(*V.done("negtop"))
                for tb in range(TB):
                    fs = grow(lv[:, tb, :], [P, 8, 8], 1)
                    es = grow(lv[:, tb, :], [P, 8, 8], 2)
                    cmp_, eq = sm("cmp", 64).rearrange("p (e f) -> p e f", e=8), sm("eq", 64).rearrange("p (e f) -> p e f", e=8)
                    v.tensor_tensor(eq, fs, es, ALU.is_equal).then_inc(*V.done("eq"))
                    v.tensor_tensor(cmp_, fs, es, ALU.is_gt).then_inc(*V.done("gt"))
                    own()
                    v.tensor_tensor(sm("eq", 64), sm("eq", 64), ct("tie"), ALU.mult).then_inc(*V.done("tie"))
                    own()
                    v.tensor_tensor(sm("cmp", 64), sm("cmp", 64), sm("eq", 64), ALU.add).then_inc(*V.done("rank"))
                    own()
                    v.tensor_reduce(sm("rank", 16)[:, 8 * tb:8 * tb + 8], cmp_, AX.X, ALU.add).then_inc(*V.done("rank"))
                    own()
                ve.wait_ge(*A.of("wexp"))
                v.scalar_tensor_tensor(out=wt, in0=sm("rank", 16), scalar=1.5, in1=wt, op0=ALU.is_lt, op1=ALU.mult)\
                    .then_inc(*V.done("wsel"))
                own()
                wv = wt.rearrange("p (b e) -> p b e", b=TB)
                v.tensor_reduce(sm("wsum", 2), wv, AX.X, ALU.add).then_inc(*V.done("wsum"))
                own()
                v.reciprocal(sm("wsum", 2), sm("wsum", 2)).then_inc(*V.done("wrec"))
                own()
                v.tensor_tensor(wv, wv, grow(sm("wsum", 2), [P, TB, 8], 2), ALU.mult).then_inc(*V.done("weights"))
                v.memset(gates[:, 4096:6144], 0.0).then_inc(*V.done("routed"))
                own()

                def expert(e, peeled):
                    where["expert"] = e
                    swiglu("moe_", peeled)
                    ve.wait_ge(*T.of("moe_down", FJ - 1))
                    for tb in range(TB):
                        for half in range(2):
                            d = moe_acc[:, tb, half * 512:(half + 1) * 512]
                            v.scalar_tensor_tensor(out=d, in0=banks[2 * tb + half], scalar=wt[:, bass.ds(e + 8 * tb, 1)],
                                                   in1=d, op0=ALU.mult, op1=ALU.add).then_inc(*V.done("acc"))
                V.enter()
                expert(0, True)
                own()
                V.again()
                with ve.Fori(1, N_EXP) as e:
                    expert(e, False)
                    own()
                V.leave()
                where["expert"] = None
                for tb in range(TB):
                    v.scalar_tensor_tensor(out=xr[:, tb, :], in0=xr[:, tb, :], scalar=ALPHA, in1=moe_acc[:, tb, :],
                                           op0=ALU.mult, op1=ALU.add).then_inc(*V.done("res2", 1, tb))
                own()
                layer_norm("ln2", 1, "x2")
            V.steps[("final",)] = ("once", V.now)

        @block.gpsimd
        def _(po):
            g = nc.gpsimd

            def own():
                po.wait_ge(*G.last())

            def power(out, in_, key):
                n = in_.shape[-1]
                g.tensor_tensor(out, in_, mh.broadcast_to([P, n]), ALU.pow).then_inc(*key)

            def rms(tag, l):
                po.wait_ge(*V.of("rms", tag, l))
                power(sm("rstd", 2), sm("ms", 2), G.done("rstd", tag, l))

            def block1(l):
                rms("b1", l)

                def roped(i):
                    c, m = QK_PAIRS[i]
                    w, dim = m * SEQ, "64" if c < 9 else "32"
                    q = qk[:, c * SEQ:(c + m) * SEQ]
                    po.wait_ge(*T.of("rotated", l, i))
                    g.tensor_tensor(halves(q), halves(q), grow(ct("cos" + dim), [P, m, SEQ], 1), ALU.mult).then_inc(*G.done("cosq", l, i))
                    own()
                    po.wait_ge(*V.of("rotsin", l, i))
                    g.tensor_tensor(q, q, rot[:, i % 2, 0:w], ALU.add).then_inc(*G.done("roped", l, i))

                def gate(n):
                    po.wait_ge(*A.of("in1", l, 9 + n))
                    gv = flat(gk[:, 2 * n:2 * n + 2, :])
                    g.tensor_scalar(gv, gv, 1.0, None, ALU.add).then_inc(*G.done("gate1p", l, n))
                for i in range(len(QK_PAIRS)):
                    if i < 5:
                        gate(i)
                    if i:
                        roped(i - 1)
                roped(len(QK_PAIRS) - 1)
                for kind, n in SCHED:
                    if kind == "gate":
                        gate(n)
                rms("f1", l)

            def ln(tag, l, key):
                po.wait_ge(*V.of("lnvar", tag, l))
                power(sm("rstd", 2), sm("ms", 2), G.done("lnrstd", tag, l))
                for tb in range(TB):
                    po.wait_ge(*V.of(key, l, tb))
                    g.tensor_tensor(xr[:, tb, :], xr[:, tb, :], norm_rows[:, D:2 * D], ALU.add).then_inc(*G.done(key, l))

            def load_norm_rows(l, which):
                own()
                g.dma_start(norm_rows, rows_d[l, 2 * D * which:2 * D * (which + 1)].partition_broadcast(P))\
                    .then_inc(s_norm_rows, 16)

            def load_group_rows(l):
                g.dma_start(group_rows, rows_d[l, 4 * D:4 * D + 1024].partition_broadcast(P)).then_inc(s_group_rows, 16)

            def mixer(l, u0):
                po.wait_ge(*V.of("cum", l))
                g.tensor_tensor(flat(t2), flat(t1), flat(t0), ALU.subtract).then_inc(*G.done("cumex", l))
                for p in range(TB):
                    for gg in range(2):
                        hs = slice(4 * gg, 4 * gg + 4)
                        po.wait_ge(*V.of("first", l, p, gg))
                        po.wait_ge(*V.of("gram", l, p, 6 + gg))
                        if p:
                            po.wait_ge(*T.of("o", l, 1))
                        else:
                            po.wait_ge(*V.of("bonus", l))
                            po.wait_ge(*V.of("ends", l))
                        ident4 = grow(ct("ident"), [P, 4, P], 1)
                        g.tensor_tensor(tri[:, hs, :], tri[:, hs, :], ident4, ALU.add).then_inc(*G.done("tri1", l, p, gg))
                        g.tensor_tensor(inv[:, hs, :], gram[:, hs, 0:P], grow(ct("levels", 0, P), [P, 4, P], 1), ALU.mult)\
                            .then_inc(*G.done("inv1", l, p, gg))
                        own()
                        g.tensor_tensor(inv[:, hs, :], inv[:, hs, :], ident4, ALU.add).then_inc(*G.done("first", l, p, gg))
                    for lv in range(5):
                        for gg in range(2):
                            hs = slice(4 * gg, 4 * gg + 4)
                            if lv:
                                po.wait_ge(*T.of("lev", l, p, lv - 1, gg))
                            g.tensor_tensor(off[:, hs, :], gram[:, hs, 0:P],
                                            grow(ct("levels", (lv + 1) * P, P), [P, 4, P], 1), ALU.mult).then_inc(*G.done("off", l, p, lv, gg))
                po.wait_ge(*V.of("gms", l))
                power(sm("gvar", 16), sm("gvar", 16), G.done("grstd", l))
                ln("ln1", l, "x1")
                load_norm_rows(l, 1)

            g.memset(mh, -0.5).then_inc(*G.done("minus_half"))
            g.dma_start(norm_rows, rows_d[0, 0:2 * D].partition_broadcast(P)).then_inc(s_norm_rows, 16)
            load_group_rows(0)
            own()
            for l in range(min(DEPTH, n_stages)):
                block1(l)
            if n_stages >= 3:
                mixer(0, MIX2_0)
                po.wait_ge(*V.of("gb", 0))
                load_group_rows(1)
                ln("ln2", 0, "x2")
            if n_stages == 4:
                load_norm_rows(1, 0)
                mixer(1, MIX2_1)
                ln("ln2", 1, "x2")
            G.steps[("final",)] = ("once", G.now)

    return {"matmul_done": T.steps, "scalar_done": A.steps, "vector_done": V.steps, "pool_done": G.steps}


def constants():
    f = np.float32
    c = {}
    i, j = np.meshgrid(np.arange(P), np.arange(P), indexing="ij")
    c["ident"] = (i == j).astype(f)
    c["ones64"] = (i // 64 == j // 64).astype(f)
    c["ones32"] = (i // 32 == j // 32).astype(f)
    c["mean256"] = np.full((P, P), 1.0 / 256, f)
    for dim in (64, 32):
        half = dim // 2
        rot = np.zeros((P, P), f)
        for m in range(P):
            if m % dim < half:
                rot[m + half, m] = -1.0
            else:
                rot[m - half, m] = 1.0
        c[f"rot{dim}"] = rot
        inv = (f(1.0) / np.power(f(10000.0), np.arange(0, dim, 2, dtype=f) / f(dim))).astype(f)
        ang = np.arange(SEQ, dtype=f)[None, :] * inv[np.arange(P) % half][:, None]
        c[f"cos{dim}"] = np.cos(ang).astype(f)
        c[f"sin{dim}"] = np.sin(ang).astype(f)
    causal = np.where(j <= i, 0.0, -BIG).astype(f)
    c["causal"] = np.concatenate([causal, np.zeros((P, P), f), causal], 1)
    c["window"] = np.concatenate([causal, np.where(j > i, 0.0, -BIG).astype(f), causal], 1)
    same = i // CHUNK == j // CHUNK
    strict, upto = (same & (i < j)).astype(f), (same & (i <= j)).astype(f)
    c["chunk4"] = np.concatenate([strict, upto, strict, upto], 1)

    def level(n, lo, hi):
        return ((lo // (2 * n) == hi // (2 * n)) & (lo % (2 * n) < n) & (hi % (2 * n) >= n)).astype(f)
    c["first"] = level(1, j, i)
    c["levels"] = np.concatenate([level(n, i, j) for n in (1, 2, 4, 8, 16, 32)], 1)
    c["heads2"] = (i[:, 0:2] // 64 == j[:, 0:2]).astype(f)
    c["reset"] = np.tile((np.arange(SEQ) % CHUNK != 0).astype(f), (P, 1))
    e, g = np.meshgrid(np.arange(8), np.arange(8), indexing="ij")
    c["tie"] = np.tile((g < e).astype(f).reshape(1, 64), (P, 1))
    return pack(CST, c)


def pack(names, arrays):
    out = np.zeros((P, names.size), np.float32)
    for name, (a, w) in names.at.items():
        out[:, a:a + w] = arrays[name]
    return out


def columns(v):
    return v.reshape(-1, P).T


def features_units(w):
    return w.reshape(KT, P, -1, 256).transpose(2, 1, 0, 3).reshape(-1, P, UNIT)


def rows_units(w):
    return w.reshape(-1, 2, P, D).transpose(0, 2, 1, 3).reshape(-1, P, UNIT)


HEAD_ORDER = [(h // 2) + 4 * (h % 2) for h in range(8)]


def lay_out(x):
    stream, par = np.empty((N_UNITS, P, UNIT), np.float32), {}
    at = [0]

    def put(u):
        stream[at[0]:at[0] + len(u)] = u
        at[0] += len(u)

    def put_ffn(gate, up, down):
        gate, up, down = features_units(gate), features_units(up), rows_units(down)
        for kind, j in ffn_order():
            put({"gate": gate, "up": up, "down": down}[kind][j:j + 1])

    for l in range(DEPTH):
        w = np.array(x["w_in"][l])
        w[:, 768:1280] = w[:, 768:1280].reshape(D, 8, HD)[:, HEAD_ORDER, :].reshape(D, 512)
        put(features_units(w))
        put(rows_units(x["w_pa"][l]))
        put(rows_units(x["w_pb"][l].reshape(8, HD, D)[HEAD_ORDER].reshape(512, D)))
        put(rows_units(x["w_pc"][l]))
        put(rows_units(x["w_out"][l]))
        put_ffn(x["w_up"][l][:, :FF], x["w_up"][l][:, FF:], x["w_down"][l])
        par[f"attn_norm{l}"] = columns(x["attn_norm"][l])
        par[f"mlp_norm{l}"] = columns(x["mlp_norm"][l])
        two = lambda n: np.tile(x[n][l], 2).reshape(P, 1)
        four = lambda n: np.tile(x[n][l], 4).reshape(P, 1)
        par[f"q_gain{l}"] = np.concatenate([two("qn_a")] * 2 + [two("kn_a")] * 2 + [two("qn_b")] * 4 + [two("kn_b")]
                                           + [four("qn_c")] * 2 + [four("kn_c")] * 2, 1)
        par[f"subln{l}"] = two("subln")
        par[f"sinks{l}"] = np.tile(x["sinks"][l].reshape(1, 8), (P, 1))
        lam = np.concatenate([x[n][l] for n in ("lam_q1", "lam_k1", "lam_q2", "lam_k2")])
        par[f"lam{l}"] = np.tile(lam.reshape(1, 128), (P, 1))
        par[f"conv_w{l}"] = x["conv_w"][l].reshape(3, 44, P).transpose(2, 0, 1).reshape(P, 132)
        par[f"conv_b{l}"] = columns(x["conv_b"][l])
    for l in range(DEPTH):
        put(features_units(x["w_in_2"][l]))
        for n in ("rwkv_w_o_2", "conf_w_o_2", "short_w_o_2", "w_out_2"):
            put(rows_units(x[n][l]))
        if l == 0:
            put_ffn(x["ffn_w_gate_2"][0], x["ffn_w_up_2"][0], x["ffn_w_down_2"][0])
        else:
            for e in range(N_EXP):
                put_ffn(x["moe_w_gate_2"][0, e], x["moe_w_up_2"][0, e], x["moe_w_down_2"][0, e])
        for name, n in (("mu", "rwkv_mu_2"), ("w0", "rwkv_w0_2"), ("a0", "rwkv_a0_2"), ("k_k", "rwkv_k_k_2"),
                        ("k_a", "rwkv_k_a_2"), ("r_k", "rwkv_r_k_2"), ("conf_b", "conf_dw_b_2"),
                        ("conf_g", "conf_ln_g_2"), ("conf_lb", "conf_ln_b_2")):
            par[f"{name}{l}"] = columns(x[n][l].reshape(-1))
        par[f"conf_dw{l}"] = x["conf_dw_2"][l].reshape(31, 2, P).transpose(2, 1, 0).reshape(P, 62)
        par[f"short_dw{l}"] = x["short_dw_2"][l].reshape(3, 2, P).transpose(2, 1, 0).reshape(P, 6)
        par[f"lora{l}"] = np.concatenate([x["rwkv_w2_2"][l], x["rwkv_a2_2"][l]], 0)
        par[f"g2{l}"] = x["rwkv_g2_2"][l]
    par["router"] = x["moe_router_2"][0].reshape(KT, P, N_EXP).transpose(1, 0, 2).reshape(P, KT * N_EXP)
    assert at[0] == N_UNITS
    rows = np.stack([np.concatenate([x[n][l] for n in ("ln1_g_2", "ln1_b_2", "ln2_g_2", "ln2_b_2", "rwkv_ln_g_2",
                                                       "rwkv_ln_b_2")]) for l in range(DEPTH)])
    return {"stream": stream, "par": pack(PAR, par), "cst": constants(), "rows": rows, "x": x["x"][0]}


N_STAGES = 4


def kernel(**inputs):
    import concourse.bacc as _bacc
    from concourse.bass_utils import run_bass_kernel_spmd as _run

    arrays = lay_out({n: np.asarray(a) for n, a in inputs.items()})
    known = {}
    for _ in range(2):
        nc = _bacc.Bacc("TRN2", target_bir_lowering=False, num_devices=1)
        d = {n: nc.dram_tensor(f"in_{n}", a.shape, F32, kind="ExternalInput").ap() for n, a in arrays.items()}
        out = nc.dram_tensor("out", (SEQ, D), F32, kind="ExternalOutput").ap()
        learned = known
        known = emit(nc, known, d["stream"], d["par"], d["cst"], d["rows"], d["x"], out, N_STAGES)
    assert known == learned
    r = _run(nc, [{f"in_{n}": a for n, a in arrays.items()}], core_ids=[0])
    return r.results[0]["out"].reshape(1, SEQ, D)
```

```python
from contextlib import ExitStack

import numpy as np

import concourse.bass as bass
from concourse import mybir

F32 = mybir.dt.float32
F32R = mybir.dt.float32r
ALU = mybir.AluOpType
ACT = mybir.ActivationFunctionType
AX = mybir.AxisListType

P = 128
SEQ = 256
TB = SEQ // P
D = 1024
KT = D // P
DEPTH = 2
FF = 2816
FJ = FF // 256
N_EXP = 8
MORE = 3
UNIT = 2048
HD = 64
N_QK = 13
CHUNK = 64
KAPPA = float(np.exp(-0.5))
ALPHA = (2.0 * DEPTH) ** 0.25
RMS_EPS = 1e-6
LN_EPS = 1e-5
GN_EPS = 64e-5
BIG = 1e30
CONF_TAPS = 31

N_IN1 = 21
N_PROJ = 4
N_OUT = 4
LAYER1 = N_IN1 + N_PROJ + N_OUT + 3 * FJ
N_IN2 = 24
MIX2 = N_IN2 + N_PROJ + N_OUT
FFN = 3 * FJ
MIX2_0 = DEPTH * LAYER1
FFN_0 = MIX2_0 + MIX2
MIX2_1 = FFN_0 + FFN
MOE_0 = MIX2_1 + MIX2
N_UNITS = MOE_0 + N_EXP * FFN
RING = 4
MOE_RING = 3
SPLIT = 3


def ffn_order():
    order = []
    for j in range(FJ):
        order += [("gate", j), ("up", j)]
        if j:
            order.append(("down", j - 1))
    return order + [("down", FJ - 1)]


FFN_UNIT = {key: n for n, key in enumerate(ffn_order())}


class Names:

    def __init__(self):
        self.at, self.size = {}, 0

    def add(self, name, width):
        self.at[name] = (self.size, width)
        self.size += width


def param_names():
    n = Names()
    for l in range(DEPTH):
        for name, w in (("attn_norm", 8), ("mlp_norm", 8), ("q_gain", N_QK), ("subln", 1), ("sinks", 8), ("lam", 128),
                        ("conv_w", 3 * 44), ("conv_b", 44)):
            n.add(f"{name}{l}", w)
        for name, w in (("mu", 14), ("w0", 4), ("a0", 4), ("k_k", 4), ("k_a", 4), ("r_k", 4), ("conf_dw", 62),
                        ("conf_b", 2), ("conf_g", 2), ("conf_lb", 2), ("short_dw", 6), ("lora", 512), ("g2", 512)):
            n.add(f"{name}{l}", w)
    n.add("router", KT * N_EXP)
    return n


def const_names():
    n = Names()
    for name, w in (("ident", 128), ("ones64", 128), ("ones32", 128), ("rot64", 128), ("rot32", 128), ("mean256", 128),
                    ("causal", 384), ("window", 384), ("cos64", 256), ("sin64", 256), ("cos32", 256), ("sin32", 256),
                    ("chunk2", 256), ("earlier", 128), ("slots", 128), ("ones", 128), ("first", 128), ("levels", 6 * 128), ("heads2", 2), ("reset", 256), ("tie", 64)):
        n.add(name, w)
    return n


PAR = param_names()
CST = const_names()


class Steps:

    def __init__(self, sem, known, where):
        self.sem, self.known, self.where = sem, known, where
        self.now, self.steps, self.kind, self.start = 0, {}, "once", 0

    def done(self, *key):
        self.now += 1
        self.steps[key] = (self.kind, self.now - self.start)
        return self.sem, 1

    def _value(self, kind, n, lag=0):
        if kind == "once":
            return n
        base, per = self.known.get("base", 1), self.known.get("per", 1)
        if kind == "turn":
            return self.where["turn"] * per + (base - lag * per + n)
        return self.where["turns"] * per + (base + n)

    def of(self, *key):
        return self.sem, self._value(*(self.steps.get(key) or self.known.get(key, ("once", 1))))

    def before(self, *key):
        return self.sem, self._value(*self.known.get(key, ("turn", 1)), lag=1)

    def last(self):
        return self.sem, self._value(self.kind, self.now - self.start)

    def same(self, key, as_key):
        self.steps[key] = self.steps[as_key]

    def enter(self):
        self.kind, self.start = "turn", self.now
        self.steps["base"] = self.now

    def again(self):
        self.steps["per"] = self.now - self.start
        self.now = self.start

    def leave(self):
        self.kind, self.start = "after", self.now


def emit(nc, known, stream, par_d, cst_d, rows_d, x_d, out_d, n_stages):
    ctx = ExitStack()
    with ctx:
        def sb(name, width):
            return ctx.enter_context(nc.sbuf_tensor(name, [P, -(-width // 8) * 8], F32))[:, 0:width]

        where = {"turn": None, "turns": None}

        def steps(name):
            return Steps(ctx.enter_context(nc.semaphore(name)), known.get(name, {}), where)

        ring = sb("ring", RING * UNIT)
        par = sb("par", PAR.size)
        cst = sb("cst", CST.size)
        norm_rows = sb("norm_rows", 2 * D)
        group_rows = sb("group_rows", 2 * 512)
        xres = sb("xres", TB * D)
        xT = sb("xT", KT * SEQ)
        gates = sb("gates", 24 * SEQ)
        yT = sb("yT", KT * SEQ)
        small = sb("small", 512)
        mh = sb("minus_half", 1)
        z_at = nc.sbuf_base
        Z = sb("Z", 21504)

        def rounded(name, at, width):
            return nc.alloc_sbuf_tensor_at(name, [P, width], F32R, offset=z_at + 4 * at)[:, :]

        w_hi, w_lo = rounded("w_hi", 0, SPLIT * UNIT), rounded("w_lo", SPLIT * UNIT, SPLIT * UNIT)
        x_hi, x_lo = (rounded(n, a, KT * SEQ).rearrange("p (k n) -> p k n", k=KT)
                      for n, a in (("x_hi", 13440), ("x_lo", 15488)))
        h_hi, h_lo = (rounded(n, a, 1024).rearrange("p (b c n) -> p b c n", b=2, c=2)
                      for n, a in (("h_hi", 17536), ("h_lo", 18560)))

        def part(w, n):
            return w[:, (n % SPLIT) * UNIT:(n % SPLIT + 1) * UNIT]
        banks = [ctx.enter_context(nc.psum_tensor(f"bank{i}", [P, 512], F32))[:, :] for i in range(8)]

        def pr(name, i=0, n=1):
            a, _ = PAR.at[name]
            return par[:, a + i:a + i + n]

        def ct(name, i=0, n=None):
            a, w = CST.at[name]
            return cst[:, a + i:a + (w if n is None else i + n)]

        small_at = {}

        def sm(name, width):
            if name not in small_at:
                used = sum(w for _, w in small_at.values())
                assert used + width <= 512
                small_at[name] = (used, width)
            a, w = small_at[name]
            return small[:, a:a + w]

        T = steps("matmul_done")
        A = steps("scalar_done")
        V = steps("vector_done")
        G = steps("pool_done")
        s_const = ctx.enter_context(nc.semaphore("const_loaded"))
        s_par = ctx.enter_context(nc.semaphore("par_loaded"))
        s_x = ctx.enter_context(nc.semaphore("x_loaded"))
        s_norm_rows = ctx.enter_context(nc.semaphore("norm_rows_loaded"))
        s_group_rows = ctx.enter_context(nc.semaphore("group_rows_loaded"))
        s_out = ctx.enter_context(nc.semaphore("out_stored"))
        s_slot = [ctx.enter_context(nc.semaphore(f"slot{i}_loaded")) for i in range(RING)]
        s_moe_slot = [ctx.enter_context(nc.semaphore(f"moe_slot{i}_loaded")) for i in range(MOE_RING)]
        block = ctx.enter_context(nc.Block())

        def slot(u):
            return ring[:, (u % RING) * UNIT:(u % RING + 1) * UNIT]

        def loaded(u):
            return s_slot[u % RING], 16 * (u // RING + 1)

        def moe_slot(i):
            return slot(i % MOE_RING)

        def moe_loaded(i, e):
            per = FFN // MOE_RING
            return s_moe_slot[i % MOE_RING], e * (16 * per) + 16 * (i // MOE_RING + 1)

        def cols3(i):
            return slice(i * P, (i + 1) * P)

        QK_TILES = {0: 0, 1: 1, 2: 2, 3: 3, 6: 4, 7: 5, 8: 6, 9: 7, 10: 8, 12: 9, 13: 10, 14: 11, 15: 12}
        QK_PAIRS = [(0, 2), (2, 2), (4, 2), (6, 2), (8, 1), (9, 2), (11, 2)]

        JOBS = []
        for h in range(4):
            JOBS.append(("a", h, h // 2, 64 * (h % 2), h // 2, 2 + h // 2, 64 * (h % 2), 64, h * 64))
        for h in range(8):
            JOBS.append(("b", (h // 2) + 4 * (h % 2), 2 + h // 2, 64 * (h % 2), 4 + h // 2, 8, 64 * (h % 2), 64,
                         256 + 64 * (h % 2)))
        for h in range(4):
            for c in range(2):
                JOBS.append((f"c{c}", h, 6 + h // 2, 64 * (h % 2), 9 + h // 2, 11 + h // 2, 64 * (h % 2) + 32 * c, 32,
                             384 + h * 64))

        def attention_schedule():
            out, gate = [], 0
            for t in range(len(JOBS) + 3):
                if t < len(JOBS):
                    out.append(("score", t))
                if 1 <= t <= len(JOBS):
                    out.append(("norm", t - 1))
                if 2 <= t <= len(JOBS) + 1:
                    out.append(("turn", t - 2))
                if 3 <= t:
                    out.append(("value", t - 3))
                if t % 2 == 1 and gate < 7:
                    out.append(("gate", 5 + gate))
                    gate += 1
            while gate < 7:
                out.append(("gate", 5 + gate))
                gate += 1
            return out

        SCHED = attention_schedule()

        qk = Z[:, 0:N_QK * SEQ]
        vtm = Z[:, 3328:3328 + TB * 640].rearrange("p (b n) -> p b n", b=TB)
        o = 3328 + TB * 640
        sq = Z[:, o:o + 1024].rearrange("p (b n) -> p b n", b=2)
        rs = Z[:, o + 1024:o + 2048].rearrange("p (b n) -> p b n", b=2)
        rot = Z[:, o + 2048:o + 3072].rearrange("p (b n) -> p b n", b=2)
        msk = Z[:, o + 3072:o + 3072 + 2 * 384].rearrange("p (b n) -> p b n", b=2)
        prob = Z[:, o + 3840:o + 3840 + 3 * 384].rearrange("p (b n) -> p b n", b=3)
        probT = Z[:, o + 4992:o + 4992 + 2 * 384].rearrange("p (b n) -> p b n", b=2)
        wide = Z[:, o + 5760:o + 5760 + 2 * D].rearrange("p (b n) -> p b n", b=TB)
        junk = Z[:, o + 5760 + 2 * D:o + 5760 + 3 * D]
        squares = Z[:, o + 5760 + 3 * D:o + 5760 + 3 * D + N_QK * SEQ]
        xr = xres.rearrange("p (b n) -> p b n", b=TB)
        xk = xT.rearrange("p (k n) -> p k n", k=KT)
        yk = yT.rearrange("p (k n) -> p k n", k=KT)
        gk = gates.rearrange("p (k n) -> p k n", k=24)

        hid = gates[:, 0:1024].rearrange("p (b c n) -> p b c n", b=2, c=2)
        act = gates[:, 1024:2048].rearrange("p (b n) -> p b n", b=2)
        cg = gates[:, 2048:3072].rearrange("p (b c n) -> p b c n", b=2, c=2)
        cv = gates[:, 3072:4096].rearrange("p (b c n) -> p b c n", b=2, c=2)
        act_m, hid_m = (gates[:, a:a + 512].rearrange("p (b n) -> p b n", b=2) for a in (0, 512))
        y_m = gates[:, 1536:2560]
        pick = gates[:, 2560:2816].rearrange("p (b n) -> p b n", b=TB)
        pickw = gates[:, 2816:3072].rearrange("p (b n) -> p b n", b=TB)
        pickT = gates[:, 3072:3328]
        moe_acc = gates[:, 4096:6144].rearrange("p (b n) -> p b n", b=TB)
        xe_hi, xe_lo = (rounded(n, a, KT * P).rearrange("p (k n) -> p k n", k=KT)
                        for n, a in (("xe_hi", 13440), ("xe_lo", 14464)))
        hT_hi, hT_lo = (rounded(n, a, 512).rearrange("p (b n) -> p b n", b=2) for n, a in (("hT_hi", 15488), ("hT_lo", 16000)))
        turn_cells = ctx.enter_context(nc.sbuf_tensor("turn_cells", [1, 1 + MORE], mybir.dt.int32))[:, :]

        rkv = Z[:, 0:3584].rearrange("p (t n) -> p t n", n=SEQ)
        r_, k_, v_ = rkv[:, 0:4, :], rkv[:, 4:8, :], rkv[:, 8:12, :]
        wa, pg = rkv[:, 12, :], rkv[:, 13, :]
        conf = Z[:, 3584:4608].rearrange("p (t n) -> p t n", n=SEQ)
        short = Z[:, 4608:6144].rearrange("p (t n) -> p t n", n=SEQ)
        a_ = Z[:, 6144:7168].rearrange("p (t n) -> p t n", n=SEQ)
        b_ = Z[:, 7168:8192].rearrange("p (t n) -> p t n", n=SEQ)
        tm = Z[:, 8192:11264].rearrange("p (x b n) -> p x b n", x=3, b=TB)
        rwo = Z[:, 11264:12288].rearrange("p (b n) -> p b n", b=TB)
        gram = Z[:, 12288:16384].rearrange("p (h n) -> p h n", h=8)
        inv = Z[:, 16384:17408].rearrange("p (h n) -> p h n", h=8)
        tri = v_.rearrange("p t n -> p (t n)").rearrange("p (h n) -> p h n", h=8)
        off = Z[:, 17408:18432].rearrange("p (h n) -> p h n", h=8)
        lev = Z[:, 18432:19456].rearrange("p (h n) -> p h n", h=8)
        xs = Z[:, 19456:19968]
        us = Z[:, 19968:20480]
        state = Z[:, 20480:20992].rearrange("p (t n) -> p t n", n=P)
        stmp = Z[:, 20992:21504]
        ctmp = yk[:, 4:6, :]
        t0 = Z[:, 12288:13312].rearrange("p (t n) -> p t n", n=SEQ)
        t1 = Z[:, 13312:14336].rearrange("p (t n) -> p t n", n=SEQ)
        t2 = Z[:, 14336:15360].rearrange("p (t n) -> p t n", n=SEQ)
        t3 = Z[:, 15360:16384].rearrange("p (t n) -> p t n", n=SEQ)
        kk = Z[:, 16384:17408].rearrange("p (t n) -> p t n", n=SEQ)
        aa = Z[:, 17408:18432].rearrange("p (t n) -> p t n", n=SEQ)
        ep = Z[:, 18432:19456].rearrange("p (t n) -> p t n", n=SEQ)

        def flat(v):
            return v.rearrange("p a b -> p (a b)")

        def halves(v):
            return v.rearrange("p (b n) -> p b n", n=SEQ)

        def grow(v, shape, axis):
            return v.unsqueeze(axis).broadcast_to(shape)

        def load_turns(eng):
            eng.wait_ge(*V.of("turns"))
            where["turns"] = eng.value_load(turn_cells[0:1, 0:1], min_val=N_EXP, max_val=N_EXP + MORE)

        @block.sync
        def _(sp):
            sp.dma_start(xr, x_d.rearrange("(b p) n -> p b n", p=P)).then_inc(s_x, 16)
            sp.dma_start(cst, cst_d).then_inc(s_const, 16)
            sp.dma_start(par, par_d).then_inc(s_par, 16)
            n_main = {1: LAYER1, 2: 2 * LAYER1, 3: FFN_0 + FFN, 4: MOE_0}[n_stages]
            ffn_starts = [l * LAYER1 + N_IN1 + N_PROJ + N_OUT for l in range(DEPTH)] + [FFN_0]
            for u in range(n_main):
                if u >= RING:
                    split = any(f <= u - RING < f + FFN for f in ffn_starts)
                    sp.wait_ge(*(V.of("lo", u - RING) if split else T.of("unit", u - RING)))
                sp.dma_start(slot(u), stream[u]).then_inc(s_slot[u % RING], 16)
            if n_stages == 4:
                def turn(n, peeled, expert):
                    where["turn"] = n
                    for i in range(FFN):
                        s = i % MOE_RING
                        if i >= MOE_RING:
                            sp.wait_ge(*V.of("moe_lo", i - MOE_RING))
                        elif not peeled:
                            sp.wait_ge(*V.before("moe_lo", i + FFN - MOE_RING))
                        else:
                            sp.wait_ge(*T.of("unit", max(u for u in range(MOE_0) if u % RING == s)))
                        sp.dma_start(moe_slot(i), stream[expert * FFN + (MOE_0 + i)]).then_inc(s_moe_slot[s], 16)
                turn(0, True, 0)
                with sp.Fori(1, N_EXP) as n:
                    turn(n, False, n)
                load_turns(sp)
                with sp.If(N_EXP < where["turns"]):
                    with sp.Fori(N_EXP, where["turns"]) as n:
                        turn(n, False, sp.value_load(turn_cells[0:1, bass.ds(n - (N_EXP - 1), 1)], min_val=0,
                                                     max_val=N_EXP - 1))
            sp.wait_ge(*V.of("final"))
            if n_stages >= 3:
                sp.wait_ge(*G.of("final"))
            sp.dma_start(out_d.rearrange("(b p) n -> p b n", p=P), xr).then_inc(s_out, 16)
            sp.wait_ge(s_out, 16)

        @block.tensor
        def _(pe):
            mm = nc.tensor.matmul

            def turn_wide(src, tag, l, ready):
                for k in range(KT):
                    for tb in range(TB):
                        if k == 0:
                            pe.wait_ge(*ready[tb])
                        t = nc.tensor.transpose(banks[k // 2][:, (k % 2) * SEQ + tb * P:(k % 2) * SEQ + (tb + 1) * P],
                                                src[:, tb, k * P:(k + 1) * P], ct("ident"))
                    t.then_inc(*T.done("turned", tag, l, k))

            def features(bank, w, l):
                wv = w.rearrange("p (k n) -> p k n", k=KT)
                for c in range(2):
                    for k in range(KT):
                        r = mm(bank[:, c * SEQ:(c + 1) * SEQ], wv[:, k, c * P:(c + 1) * P], xk[:, k, :],
                               start=(k == 0), stop=(k == KT - 1))
                return r

            def tokens(bank, at, w, c0, width):
                wv = w.rearrange("p (k n) -> p k n", k=KT)
                for tb in range(TB):
                    for k in range(KT):
                        r = mm(bank[:, at + tb * width:at + (tb + 1) * width], xk[:, k, tb * P:(tb + 1) * P],
                               wv[:, k, c0:c0 + width], start=(k == 0), stop=(k == KT - 1))
                return r

            def rows(src, w, first, last):
                wv = w.rearrange("p (c n) -> p c n", c=2)
                for c in range(2):
                    for tb in range(TB):
                        for half in range(2):
                            r = mm(banks[2 * tb + half], src(c)[:, tb * P:(tb + 1) * P],
                                   wv[:, c, half * 512:(half + 1) * 512], start=(first and c == 0),
                                   stop=(last and c == 1))
                return r

            def features_split(bank, n):
                for c in range(2):
                    for k in range(KT):
                        at = slice(k * 256 + c * P, k * 256 + (c + 1) * P)
                        for a, b in ((w_hi, x_hi), (w_hi, x_lo), (w_lo, x_hi)):
                            r = mm(bank[:, c * SEQ:(c + 1) * SEQ], part(a, n)[:, at], b[:, k, :],
                                   start=(k == 0 and b is x_hi and a is w_hi), stop=(k == KT - 1 and a is w_lo))
                return r

            def rows_split(j, n):
                for c in range(2):
                    for tb in range(TB):
                        for half in range(2):
                            for a, b in ((h_hi, w_hi), (h_lo, w_hi), (h_hi, w_lo)):
                                r = mm(banks[2 * tb + half], a[:, j % 2, c, tb * P:(tb + 1) * P],
                                       part(b, n)[:, c * D + half * 512:c * D + (half + 1) * 512],
                                       start=(j == 0 and c == 0 and a is h_hi and b is w_hi),
                                       stop=(j == FJ - 1 and c == 1 and b is w_lo))
                return r

            def project(l, blk, splits, u0):
                for n in range(N_PROJ):
                    pe.wait_ge(*loaded(u0 + n))
                k_at = [0, splits[0], splits[0] + splits[1]]
                for c in range(4):
                    for b in range(3):
                        bank = banks[4 + (3 * c + b) % 4]
                        if 3 * c + b >= 4:
                            pe.wait_ge(*V.of("merged", blk, l, 3 * c + b - 4))
                        for half in range(2):
                            for k in range(k_at[b], k_at[b] + splits[b]):
                                wv = slot(u0 + k // 2).rearrange("p (c n) -> p c n", c=2)
                                col = (2 * c + half) * P
                                r = mm(bank[:, half * SEQ:(half + 1) * SEQ], wv[:, k % 2, col:col + P], yk[:, k, :],
                                       start=(k == k_at[b]), stop=(k == k_at[b] + splits[b] - 1))
                        r.then_inc(*T.done("branch", blk, l, 3 * c + b))
                for n in range(N_PROJ):
                    T.steps[("unit", u0 + n)] = T.steps[("branch", blk, l, 11)]

            def project_out(l, blk, u0):
                for n in range(N_OUT):
                    u = u0 + n
                    pe.wait_ge(*loaded(u))
                    pe.wait_ge(*V.of("merged", blk, l, 11))
                    rows(lambda c: gk[:, 2 * n + c, :], slot(u), n == 0, n == N_OUT - 1).then_inc(*T.done("unit", u))

            def block1(l):
                u0 = l * LAYER1
                if l == 0:
                    pe.wait_ge(s_const, 16)
                turn_wide(wide, "b1", l, [V.of("normed", "b1", l, tb) for tb in range(TB)])

                def unit(n):
                    u = u0 + n
                    pe.wait_ge(*loaded(u))
                    if n == 0:
                        pe.wait_ge(*A.of("xT", "b1", l))
                        pe.wait_ge(*V.of("xT", "b1", l))
                    if n >= 4:
                        pe.wait_ge(*A.of("in1", l, n - 4))
                    bank = banks[4 + n % 4]
                    if n in (2, 8):
                        r = tokens(bank, 0, slot(u), 0, 256)
                    elif n == 5:
                        wv = slot(u).rearrange("p (k n) -> p k n", k=KT)
                        for k in range(KT):
                            mm(bank[:, 0:SEQ], wv[:, k, 0:P], xk[:, k, :], start=(k == 0), stop=(k == KT - 1))
                        r = tokens(bank, SEQ, slot(u), P, P)
                    else:
                        r = features(bank, slot(u), l)
                    r.then_inc(*T.done("unit", u))

                for n in range(9):
                    unit(n)
                for i, (c, m) in enumerate(QK_PAIRS):
                    w = m * SEQ
                    ones = "ones64" if c < 9 else "ones32"
                    if i < 5:
                        unit(9 + i)
                    pe.wait_ge(*A.of("square", l, c + m - 1))
                    if i >= 2:
                        pe.wait_ge(*A.of("qrms", l, i - 2))
                    mm(banks[i % 2][:, 0:w], ct(ones), squares[:, c * SEQ:(c + m) * SEQ], start=True, stop=True)\
                        .then_inc(*T.done("sumsq", l, i))
                    if i >= 1:
                        rotate(l, i - 1)
                rotate(l, len(QK_PAIRS) - 1)

                for kind, n in SCHED:
                    if kind == "gate":
                        unit(9 + n)
                    elif kind == "score":
                        br, h, ot, ob, qt, kt, base, kk_, vc = JOBS[n]
                        if n == 0:
                            pe.wait_ge(*G.of("roped", l, len(QK_PAIRS) - 1))
                            pe.wait_ge(*V.of("qn", l, len(QK_PAIRS) - 1))
                            pe.wait_ge(*V.of("rotsin", l, len(QK_PAIRS) - 1))
                        if n >= 2:
                            pe.wait_ge(*V.of("masked", l, n - 2))
                        q = qk[base:base + kk_, qt * SEQ:(qt + 1) * SEQ]
                        k = qk[base:base + kk_, kt * SEQ:(kt + 1) * SEQ]
                        mm(banks[n % 2][:, 0:128], q[:, 0:128], k[:, 0:128], start=True, stop=True)
                        mm(banks[n % 2][:, 128:384], q[:, 128:256], k, start=True, stop=True)\
                            .then_inc(*T.done("score", l, n))
                    elif kind == "turn" and JOBS[n][0] != "c0":
                        pe.wait_ge(*V.of("prob", l, n))
                        if n >= 1:
                            m = n - 1 if JOBS[n - 1][0] != "c0" else n - 2
                            pe.wait_ge(*A.of("probT", l, m))
                        for i in range(3):
                            r = nc.tensor.transpose(banks[2][:, i * P:(i + 1) * P], prob[:, n % 3, cols3(i)], ct("ident"))
                        r.then_inc(*T.done("turnp", l, n))
                    elif kind == "value" and JOBS[n][0] != "c0":
                        br, h, ot, ob, qt, kt, base, kk_, vc = JOBS[n]
                        pe.wait_ge(*A.of("probT", l, n))
                        if ob == 0 and ot >= 1:
                            pe.wait_ge(*A.of("y", l, ot - 1))
                        dst = banks[3][ob:ob + HD, 0:SEQ]
                        mm(dst, vtm[:, 0, vc:vc + HD], probT[:, n % 2, 0:256], start=True, stop=False)
                        mm(dst[:, 128:256], vtm[:, 1, vc:vc + HD], probT[:, n % 2, 256:384], start=False, stop=True)\
                            .then_inc(*T.done("value", l, n))
                for i in range(2):
                    pe.wait_ge(*A.of("csquare", l, i))
                    if i == 0:
                        pe.wait_ge(*V.of("masked", l, len(JOBS) - 1))
                    r = mm(banks[0][:, i * SEQ:(i + 1) * SEQ], ct("ones64"), sq[:, 0, i * SEQ:(i + 1) * SEQ],
                           start=True, stop=True)
                r.then_inc(*T.done("csum", l))
                pe.wait_ge(*V.of("cnormed", l))
                pe.wait_ge(*A.of("in1", l, N_IN1 - 1))
                project(l, "b1", (2, 4, 2), u0 + N_IN1)
                project_out(l, "b1", u0 + N_IN1 + N_PROJ)
                turn_wide(wide, "f1", l, [V.of("normed", "f1", l, tb) for tb in range(TB)])
                f0 = u0 + N_IN1 + N_PROJ + N_OUT
                for (kind, j), n in FFN_UNIT.items():
                    u = f0 + n
                    pe.wait_ge(*V.of("lo", u))
                    if n == 0:
                        pe.wait_ge(*V.of("x_lo", "f1", l))
                    if kind == "down":
                        pe.wait_ge(*V.of("hidden1", l, j))
                        r = rows_split(j, n)
                    else:
                        if j >= 2:
                            pe.wait_ge(*V.of("conv", kind, l, j - 2))
                        r = features_split(banks[4 + 2 * (j % 2) + (kind == "up")], n)
                    r.then_inc(*T.done("unit", u))
                    T.same((kind, l, j), ("unit", u))

            def rotate(l, i):
                c, m = QK_PAIRS[i]
                pe.wait_ge(*V.of("qn", l, i))
                if i >= 2:
                    pe.wait_ge(*V.of("rotsin", l, i - 2))
                mm(banks[2 + i % 2][:, 0:m * SEQ], ct("rot64" if c < 9 else "rot32"), qk[:, c * SEQ:(c + m) * SEQ],
                   start=True, stop=True).then_inc(*T.done("rotated", l, i))

            def swiglu():
                for (kind, j), n in FFN_UNIT.items():
                    u = FFN_0 + n
                    pe.wait_ge(*V.of("lo", u))
                    if n == 0:
                        pe.wait_ge(*V.of("x_lo", "f2", 0))
                    if kind == "down":
                        pe.wait_ge(*V.of("dense_hidden", j))
                        r = rows_split(j, n)
                    else:
                        if j >= 2:
                            pe.wait_ge(*V.of("dense_hidden", j - 2))
                        r = features_split(banks[4 + 2 * (j % 2) + (kind == "up")], n)
                    r.then_inc(*T.done("unit", u))
                    T.same(("dense_" + kind, j), ("unit", u))

            def rwkv(l, inject):
                tc = nc.tensor
                pe.wait_ge(*A.of("tanh", l))
                for x in range(2):
                    for t in range(4):
                        r = mm(banks[2 * x + t // 2][:, (t % 2) * SEQ:(t % 2 + 1) * SEQ],
                               pr(f"lora{l}", t * P, P)[64 * x:64 * x + 64, :], wa[64 * x:64 * x + 64, :],
                               start=True, stop=True)
                    r.then_inc(*T.done("lora", l, x))
                inject()
                pe.wait_ge(*A.of("kksq", l))
                pe.wait_ge(*A.of("aa", l))
                for i in range(2):
                    mm(banks[i], ct("ones64"), flat(t3)[:, i * 512:(i + 1) * 512], start=True, stop=True)\
                        .then_inc(*T.done("kksum", l, i))
                inject()
                n = 0
                for x, src, ready in ((2, v_, V.of("shift", l, 5)), (0, b_, V.of("bn", l)), (1, k_, V.of("kt", l))):
                    pe.wait_ge(*ready)
                    for tb in range(TB):
                        if n >= 2:
                            pe.wait_ge(*A.of("tm", l, n - 2))
                        elif n == 0:
                            pe.wait_ge(*V.of("kkms", l))
                        for t in range(4):
                            r = tc.transpose(banks[2 + n % 2][:, t * P:(t + 1) * P], src[:, t, tb * P:(tb + 1) * P],
                                             ct("ident"))
                        r.then_inc(*T.done("tm", l, n))
                        n += 1
                inject()
                pe.wait_ge(*V.of("rk", l))
                for tb in range(TB):
                    for t in range(4):
                        r = mm(banks[0][:, tb * 8 + 2 * t:tb * 8 + 2 * t + 2], t0[:, t, tb * P:(tb + 1) * P],
                               ct("heads2"), start=True, stop=True)
                r.then_inc(*T.done("bonus", l))
                pe.wait_ge(*V.of("bonus", l))
                pe.wait_ge(*V.of("rt", l))
                pe.wait_ge(*V.of("at", l))
                pe.wait_ge(*A.of("tm", l, 5))
                for p in range(TB):
                    cols = slice(p * P, (p + 1) * P)
                    for h in range(8):
                        bs, t = slice(64 * (h % 2), 64 * (h % 2) + 64), h // 2
                        if h >= 2:
                            pe.wait_ge(*V.of("gram", l, p, h - 2))
                        elif p:
                            pe.wait_ge(*A.of("o", l, 1) if h == 0 else V.of("state", l, 1))
                            pe.wait_ge(*V.of("us", l, 1))
                        bank = banks[h % 2]
                        mm(bank[:, 0:128], b_[bs, t, cols], a_[bs, t, cols], start=True, stop=True)
                        mm(bank[:, 128:256], b_[bs, t, cols], r_[bs, t, cols], start=True, stop=True)
                        mm(bank[:, 256:384], k_[bs, t, cols], a_[bs, t, cols], start=True, stop=True)
                        mm(bank[:, 384:512], k_[bs, t, cols], r_[bs, t, cols], start=True, stop=True)\
                            .then_inc(*T.done("gram", l, p, h))
                        r = mm(banks[2 + h % 2][:, t * P:(t + 1) * P], a_[bs, t, cols], b_[bs, t, cols],
                               start=True, stop=True)
                        if h >= 6:
                            r.then_inc(*T.done("m", l, p, h % 2))
                    inject()
                    for lv in range(5):
                        for g in range(2):
                            hs = range(4 * g, 4 * g + 4)
                            if lv == 0:
                                pe.wait_ge(*G.of("first", l, p, g))
                                pe.wait_ge(*V.of("gram", l, p, 7))
                            else:
                                pe.wait_ge(*V.of("inv", l, p, lv - 1, g))
                            pe.wait_ge(*G.of("off", l, p, lv, g))
                            for h in hs:
                                r = mm(banks[2 * g][:, (h % 4) * P:(h % 4 + 1) * P], off[:, h, :], tri[:, h, :],
                                       start=True, stop=True)
                            r.then_inc(*T.done("lev", l, p, lv, g))
                        for g in range(2):
                            hs = range(4 * g, 4 * g + 4)
                            pe.wait_ge(*A.of("lev", l, p, lv, g))
                            if lv < 4:
                                for h in hs:
                                    mm(banks[2 * g + 1][:, (h % 4) * P:(h % 4 + 1) * P], inv[:, h, :], lev[:, h, :],
                                       start=True, stop=True)
                            for h in hs:
                                r = mm(banks[2 * g][:, (h % 4) * P:(h % 4 + 1) * P], lev[:, h, :], inv[:, h, :],
                                       start=True, stop=True)
                            r.then_inc(*T.done("inv", l, p, lv, g))
                        if lv % 2 == 1:
                            inject()
                    for cc in range(2):
                        c = 2 * p + cc
                        ch = slice(64 * cc, 64 * cc + 64)
                        tc_ = slice(c * 64, c * 64 + 64)
                        if c == 0 or cc == 0:
                            pe.wait_ge(*V.of("inv", l, p, 4, 0))
                            pe.wait_ge(*V.of("inv", l, p, 4, 1))
                        if c:
                            pe.wait_ge(*V.of("state", l, c - 1))
                            pe.wait_ge(*A.of("o", l, c - 1))
                        for t in range(4):
                            dst = banks[0][ch, t * P:(t + 1) * P]
                            if c:
                                mm(dst, a_[:, t, tc_], state[:, t, :], start=True, stop=False)
                            for x in range(2):
                                r = mm(dst[:, x * HD:(x + 1) * HD], gram[:, 4 * x + t, 256 + 64 * cc:320 + 64 * cc],
                                       tm[:, 2, p, t * P + x * HD:t * P + (x + 1) * HD], start=(c == 0), stop=(c == 0 or x == 1))
                        r.then_inc(*T.done("x", l, c))
                        pe.wait_ge(*A.of("xs", l, c))
                        for h in range(8):
                            r = mm(banks[1][ch, h * 64:h * 64 + 64], inv[:, 4 * (h % 2) + h // 2, ch],
                                   xs[:, h * 64:h * 64 + 64], start=True, stop=True)
                        r.then_inc(*T.done("u", l, c))
                        pe.wait_ge(*V.of("us", l, c))
                        for t in range(4):
                            dst, two = banks[3][:, t * P:(t + 1) * P], slice(t * P, (t + 1) * P)
                            mm(dst, tm[ch, 0, p, two], us[ch, two], start=True, stop=False)
                            r = mm(dst, tm[ch, 1, p, two], tm[ch, 2, p, two], start=False, stop=True)
                        r.then_inc(*T.done("s", l, c))
                        for t in range(4):
                            dst = banks[2][ch, t * P:(t + 1) * P]
                            if c:
                                mm(dst, r_[:, t, tc_], state[:, t, :], start=True, stop=False)
                            for x in range(2):
                                d, hv = dst[:, x * HD:(x + 1) * HD], slice(t * P + x * HD, t * P + (x + 1) * HD)
                                mm(d, gram[:, 4 * x + t, 128 + 64 * cc:192 + 64 * cc], us[:, hv], start=(c == 0), stop=False)
                                r = mm(d, gram[:, 4 * x + t, 384 + 64 * cc:448 + 64 * cc], tm[:, 2, p, hv],
                                       start=False, stop=(c == 0 or x == 1))
                        r.then_inc(*T.done("o", l, c))
                    inject()
                for tb in range(TB):
                    pe.wait_ge(*V.of("state", l, 3))
                    pe.wait_ge(*A.of("o", l, 3))
                    r = mm(banks[tb], pg[:, tb * P:(tb + 1) * P], pr(f"g2{l}", 0, 512), start=True, stop=True)
                r.then_inc(*T.done("outgate", l))

            def mixer(l, u0):
                ready = [V.of("final_x", DEPTH - 1) if l == 0 else V.of("x2", 0, tb) for tb in range(TB)]
                if l:
                    pe.wait_ge(*G.of("x2", 0))
                turn_wide(xr, "b2", l, ready)

                def unit(n):
                    u = u0 + n
                    pe.wait_ge(*loaded(u))
                    if n == 0:
                        pe.wait_ge(*A.of("xT", "b2", l))
                        pe.wait_ge(*V.of("xT", "b2", l))
                    if n >= 4:
                        pe.wait_ge(*(V.of("shift", l, n - 4) if n - 4 < 7 else A.of("in2", l, n - 4)))
                    features(banks[4 + n % 4], slot(u), l).then_inc(*T.done("unit", u))
                for n in range(7):
                    unit(n)
                left = list(range(7, N_IN2))

                def inject():
                    if left:
                        unit(left.pop(0))
                    if left and len(left) % 2:
                        unit(left.pop(0))
                rwkv(l, inject)
                while left:
                    unit(left.pop(0))
                pe.wait_ge(*V.of("confconv", l))
                pe.wait_ge(*V.of("gated", l))
                for i in range(2):
                    r = mm(banks[2][:, 0:SEQ], ct("mean256"), ctmp[:, i, :], start=(i == 0), stop=(i == 1))
                r.then_inc(*T.done("confmean", l))
                pe.wait_ge(*A.of("confsq", l))
                for i in range(2):
                    r = mm(banks[3][:, 0:SEQ], ct("mean256"), conf[:, i, :], start=(i == 0), stop=(i == 1))
                r.then_inc(*T.done("confvar", l))
                for t in range(4):
                    for tb in range(TB):
                        r = nc.tensor.transpose(banks[t // 2][:, (t % 2) * SEQ + tb * P:(t % 2) * SEQ + (tb + 1) * P],
                                                rwo[:, tb, t * P:(t + 1) * P], ct("ident"))
                r.then_inc(*T.done("rwoT", l))
                pe.wait_ge(*A.of("rwoT", l))
                pe.wait_ge(*A.of("confy", l))
                pe.wait_ge(*V.of("shorty", l))
                for n in range(N_IN2 - 4, N_IN2):
                    pe.wait_ge(*A.of("in2", l, n))
                project(l, "b2", (4, 2, 2), u0 + N_IN2)
                project_out(l, "b2", u0 + N_IN2 + N_PROJ)
                pe.wait_ge(*G.of("x1", l))
                turn_wide(xr, "f2", l, [V.of("x1", l, tb) for tb in range(TB)])

            for l in range(min(DEPTH, n_stages)):
                block1(l)
            if n_stages >= 3:
                mixer(0, MIX2_0)
                swiglu()
            if n_stages == 4:
                mixer(1, MIX2_1)
                pe.wait_ge(*A.of("xT", "f2", 1))
                pe.wait_ge(*V.of("xT", "f2", 1))
                for tb in range(TB):
                    for k in range(KT):
                        r = mm(banks[0][:, tb * 8:tb * 8 + 8], xk[:, k, tb * P:(tb + 1) * P],
                               pr("router", k * N_EXP, N_EXP), start=(k == 0), stop=(k == KT - 1))
                r.then_inc(*T.done("router"))
                sel = sm("sel", 48).rearrange("p (b c) -> p b c", b=TB)
                pe.wait_ge(*V.of("selected"))
                mm(banks[1][:, 0:8], ct("earlier"), sel[:, 0, 0:8], start=True, stop=True)
                mm(banks[1][:, 8:16], ct("earlier"), sel[:, 1, 0:8], start=True, stop=False)
                mm(banks[1][:, 8:16], ct("ones"), sel[:, 0, 0:8], start=False, stop=True)
                mm(banks[1][:, 16:24], ct("ones"), sel[:, 0, 0:8], start=True, stop=False)
                mm(banks[1][:, 16:24], ct("ones"), sel[:, 1, 0:8], start=False, stop=True).then_inc(*T.done("places"))

                def gather():
                    for k in range(KT):
                        for tb in range(TB):
                            r = mm(banks[2 + k // 4][:, (k % 4) * P:(k % 4 + 1) * P], xr[:, tb, k * P:(k + 1) * P],
                                   pick[:, tb, :], start=(tb == 0), stop=(tb == TB - 1))
                    return r
                pe.wait_ge(*V.of("pick0"))
                gather().then_inc(*T.done("gather0"))

                def turn(n, peeled):
                    where["turn"] = n

                    def up(kind, j):
                        i = FFN_UNIT[(kind, j)]
                        pe.wait_ge(*V.of("moe_lo", i))
                        for k in range(KT):
                            for a, b in ((xe_hi, w_hi), (xe_lo, w_hi), (xe_hi, w_lo)):
                                r = mm(banks[4 + (kind == "up")][:, 0:256], a[:, k, :], part(b, i)[:, k * 256:(k + 1) * 256],
                                       start=(k == 0 and a is xe_hi and b is w_hi), stop=(k == KT - 1 and b is w_lo))
                        r.then_inc(*T.done("moe_unit", i))
                        T.same((f"moe_{kind}", j), ("moe_unit", i))

                    def turn_hidden(j):
                        pe.wait_ge(*V.of("moe_hidden", j))
                        if j == 0:
                            if not peeled:
                                pe.wait_ge(*V.before("acc"))
                        else:
                            pe.wait_ge(*V.of("hT", j - 1))
                        for c in range(2):
                            r = nc.tensor.transpose(banks[6][:, c * P:(c + 1) * P], hid_m[:, j % 2, c * P:(c + 1) * P],
                                                    ct("ident"))
                        r.then_inc(*T.done("turned_hidden", j))

                    def down(j):
                        i = FFN_UNIT[("down", j)]
                        pe.wait_ge(*V.of("moe_lo", i))
                        pe.wait_ge(*V.of("hT", j))
                        for c in range(2):
                            for half in range(2):
                                for a, b in ((hT_hi, w_hi), (hT_lo, w_hi), (hT_hi, w_lo)):
                                    r = mm(banks[half], a[:, j % 2, c * P:(c + 1) * P],
                                           part(b, i)[:, c * D + half * 512:c * D + (half + 1) * 512],
                                           start=(j == 0 and c == 0 and a is hT_hi and b is w_hi),
                                           stop=(j == FJ - 1 and c == 1 and b is w_lo))
                        r.then_inc(*T.done("moe_unit", i))
                        T.same(("moe_down", j), ("moe_unit", i))

                    for j in range(FJ):
                        if j == 0:
                            pe.wait_ge(*(V.of("xe0") if peeled else V.before("xe")))
                        else:
                            pe.wait_ge(*A.of("moe_silu", j - 1))
                        up("gate", j)
                        if j:
                            turn_hidden(j - 1)
                        up("up", j)
                        if j:
                            down(j - 1)
                        if j == 1:
                            pe.wait_ge(*V.of("pickw"))
                            for tb in range(TB):
                                r = nc.tensor.transpose(banks[7][:, tb * P:(tb + 1) * P], pickw[:, tb, :], ct("ident"))
                            r.then_inc(*T.done("pickT"))
                    pe.wait_ge(*V.of("pick"))
                    gather().then_inc(*T.done("gather"))
                    turn_hidden(FJ - 1)
                    down(FJ - 1)
                    pe.wait_ge(*A.of("y"))
                    pe.wait_ge(*V.of("y"))
                    pe.wait_ge(*V.of("xe"))
                    pe.wait_ge(*A.of("pickT"))
                    for tb in range(TB):
                        for half in range(2):
                            r = mm(banks[2 + 4 * tb + half], pickT[:, tb * P:(tb + 1) * P],
                                   y_m[:, half * 512:(half + 1) * 512], start=True, stop=True)
                    r.then_inc(*T.done("scattered"))
                T.enter()
                turn(0, True)
                T.again()
                load_turns(pe)
                with pe.Fori(1, where["turns"]) as n:
                    turn(n, False)
                T.leave()

        @block.scalar
        def _(sc):
            act_ = nc.scalar.activation

            def xT_out(tag, l, gain):
                for k in (0, 1, 4, 5):
                    sc.wait_ge(*T.of("turned", tag, l, k | 1))
                    src = banks[k // 2][:, (k % 2) * SEQ:(k % 2 + 1) * SEQ]
                    act_(xk[:, k, :], src, ACT.Copy, scale=pr(gain, k) if gain else 1.0)\
                        .then_inc(*A.done("xT", tag, l))

            def x_hi_out(tag, l, gain):
                for k in range(KT):
                    sc.wait_ge(*T.of("turned", tag, l, k | 1))
                    act_(x_hi[:, k, :], banks[k // 2][:, (k % 2) * SEQ:(k % 2 + 1) * SEQ], ACT.Copy,
                         scale=pr(gain, k) if gain else 1.0).then_inc(*A.done("x_hi", tag, l, k))

            def with_splits(f0, evacuate):
                order = ffn_order()
                for n in range(FFN + 2):
                    if n < FFN:
                        u = f0 + n
                        sc.wait_ge(*loaded(u))
                        if n >= SPLIT:
                            sc.wait_ge(*T.of("unit", u - SPLIT))
                        act_(part(w_hi, n), slot(u), ACT.Copy).then_inc(*A.done("hi", u))
                    if n >= 2:
                        evacuate(*order[n - 2])

            def rms_sums(tag, l, ready):
                for tb in range(TB):
                    for s in ready:
                        sc.wait_ge(*s)
                    act_(junk, xr[:, tb, :], ACT.Square, accum_out=sm(f"ss{tag}", 2)[:, tb:tb + 1])\
                        .then_inc(*A.done("ss", tag, l, tb))
                    sc.wait_ge(*A.last())

            def block1(l):
                u0 = l * LAYER1
                if l == 0:
                    sc.wait_ge(s_x, 16)
                    sc.wait_ge(s_par, 16)
                rms_sums("b1", l, [] if l == 0 else [V.of("x_out", "f1", l - 1)])
                sc.wait_ge(*V.of("lamsum", l))
                act_(sm("lamexp", 2), sm("lamsum", 2), ACT.Exp).then_inc(*A.done("lamexp", l))
                xT_out("b1", l, f"attn_norm{l}")

                def unit(n):
                    u = u0 + n
                    bank = banks[4 + n % 4]
                    sc.wait_ge(*T.of("unit", u))
                    if n == 0 and l:
                        sc.wait_ge(*V.of("merged", "b1", l - 1, 11))
                    if n in (2, 8):
                        c = 0 if n == 2 else 384
                        act_(vtm[:, :, c:c + 256], bank.rearrange("p (b n) -> p b n", b=TB), ACT.Copy)\
                            .then_inc(*A.done("in1", l, n))
                    elif n == 5:
                        act_(qk[:, 8 * SEQ:9 * SEQ], bank[:, 0:SEQ], ACT.Copy).then_inc(*A.done("q8", l))
                        act_(squares[:, 8 * SEQ:9 * SEQ], bank[:, 0:SEQ], ACT.Square).then_inc(*A.done("square", l, 8))
                        act_(vtm[:, :, 256:384], bank[:, SEQ:2 * SEQ].rearrange("p (b n) -> p b n", b=TB), ACT.Copy)\
                            .then_inc(*A.done("in1", l, n))
                    elif n < 9:
                        c = QK_TILES[2 * n]
                        act_(squares[:, c * SEQ:(c + 2) * SEQ], bank, ACT.Square).then_inc(*A.done("square", l, c + 1))
                        act_(qk[:, c * SEQ:(c + 2) * SEQ], bank, ACT.Copy).then_inc(*A.done("in1", l, n))
                    else:
                        act_(gk[:, 2 * (n - 9):2 * (n - 9) + 2, :], bank.rearrange("p (b n) -> p b n", b=2), ACT.Exp,
                             scale=-1.0).then_inc(*A.done("in1", l, n))

                for n in range(9):
                    unit(n)
                for i, (c, m) in enumerate(QK_PAIRS):
                    if i < 5:
                        unit(9 + i)
                    if i >= 2:
                        sc.wait_ge(*V.of("qn", l, i - 2))
                    sc.wait_ge(*T.of("sumsq", l, i))
                    act_(rs[:, i % 2, 0:m * SEQ], banks[i % 2][:, 0:m * SEQ], ACT.Sqrt, bias=sm("rms_eps", 1),
                         scale=1.0 / (HD if c < 9 else 32)).then_inc(*A.done("qrms", l, i))
                for kind, n in SCHED:
                    if kind == "gate":
                        unit(9 + n)
                        continue
                    br = JOBS[n][0]
                    scale = 32 ** -0.5 if br[0] == "c" else HD ** -0.5
                    if kind == "score":
                        sc.wait_ge(*V.of("negmax", l, n))
                        if n >= 3:
                            if JOBS[n - 3][0] != "c0":
                                sc.wait_ge(*T.of("turnp", l, n - 3))
                            else:
                                sc.wait_ge(*V.of("prob", l, n - 2))
                        for i, s in enumerate((slice(0, 128), slice(128, 384))):
                            act_(prob[:, n % 3, s], msk[:, n % 2, s], ACT.Exp, bias=sm(f"negmax{n % 2}", 2)[:, i:i + 1],
                                 scale=scale, accum_out=sm(f"rowsum{n % 2}", 2)[:, i:i + 1])\
                                .then_inc(*A.done("exp", l, n))
                        if br == "b":
                            act_(sm(f"sinkexp{n % 2}", 2), sm(f"negmax{n % 2}", 2), ACT.Exp,
                                 bias=pr(f"sinks{l}", JOBS[n][1])).then_inc(*A.done("exp", l, n))
                    elif kind == "turn" and br != "c0":
                        sc.wait_ge(*T.of("turnp", l, n))
                        m = [i for i in range(n - 1) if JOBS[i][0] != "c0" and i % 2 == n % 2]
                        if m:
                            sc.wait_ge(*T.of("value", l, m[-1]))
                        act_(probT[:, n % 2, :], banks[2][:, 0:384], ACT.Copy).then_inc(*A.done("probT", l, n))
                    elif kind == "value" and br != "c0" and JOBS[n][3] == 64:
                        ot = JOBS[n][2]
                        sc.wait_ge(*T.of("value", l, n))
                        if ot == 0:
                            sc.wait_ge(*T.of("rotated", l, len(QK_PAIRS) - 1))
                            sc.wait_ge(*T.of("sumsq", l, len(QK_PAIRS) - 1))
                        act_(yk[:, ot, :], banks[3][:, 0:SEQ], ACT.Copy).then_inc(*A.done("y", l, ot))
                for i in range(2):
                    sc.wait_ge(*A.of("y", l, 6 + i))
                    act_(sq[:, 0, i * SEQ:(i + 1) * SEQ], yk[:, 6 + i, :], ACT.Square).then_inc(*A.done("csquare", l, i))
                sc.wait_ge(*T.of("csum", l))
                act_(rs[:, 0, :], banks[0], ACT.Sqrt, bias=sm("rms_eps", 1), scale=1.0 / HD).then_inc(*A.done("crms", l))
                rms_sums("f1", l, [V.of("x_out", "b1", l)])
                x_hi_out("f1", l, f"mlp_norm{l}")

                def evacuate(kind, j):
                    if kind == "down":
                        return
                    dst, c0 = (cg, 0) if kind == "gate" else (cv, 22)
                    sc.wait_ge(*T.of(kind, l, j))
                    if j >= 2:
                        sc.wait_ge(*V.of("hidden1", l, j - 2))
                        sc.wait_ge(*A.of("silu1", l, j - 2))
                    if j == 0:
                        sc.wait_ge(*T.of("unit", u0 + N_IN1 + N_PROJ + N_OUT - 1))
                    for c in range(2):
                        ch = c0 + 2 * j + c
                        act_(dst[:, j % 2, c, :], banks[4 + 2 * (j % 2) + (kind == "up")][:, c * SEQ:(c + 1) * SEQ],
                             ACT.Identity, scale=pr(f"conv_w{l}", 2 * 44 + ch), bias=pr(f"conv_b{l}", ch))\
                            .then_inc(*A.done("tap2", kind, l, j))
                    if kind == "up":
                        sc.wait_ge(*V.of("conv", "gate", l, j))
                        act_(act[:, j % 2, :], flat(cg[:, j % 2, :, :]), ACT.Silu).then_inc(*A.done("silu1", l, j))
                with_splits(u0 + N_IN1 + N_PROJ + N_OUT, evacuate)

            def swiglu():
                def evacuate(kind, j):
                    if kind == "gate":
                        sc.wait_ge(*T.of("dense_gate", j))
                        if j >= 2:
                            sc.wait_ge(*V.of("dense_hidden", j - 2))
                        act_(act[:, j % 2, :], banks[4 + 2 * (j % 2)], ACT.Silu).then_inc(*A.done("dense_silu", j))
                with_splits(FFN_0, evacuate)

            def layer_norm_sums(tag, l, ready):
                for tb in range(TB):
                    sc.wait_ge(*ready[tb])
                    if tb:
                        sc.wait_ge(*A.last())
                    act_(lnjunk, xr[:, tb, :], ACT.Copy, accum_out=sm("lnsum", 2)[:, tb:tb + 1])\
                        .then_inc(*A.done("lnsum", tag, l, tb))
                for tb in range(TB):
                    sc.wait_ge(*V.of("negmean", tag, l))
                    sc.wait_ge(*A.last())
                    act_(lnjunk, xr[:, tb, :], ACT.Square, bias=sm("negmean", 2)[:, tb:tb + 1],
                         accum_out=sm("lnsq", 2)[:, tb:tb + 1]).then_inc(*A.done("lnsq", tag, l, tb))

            def mixer(l, u0):
                xT_out("b2", l, None)

                def unit(n):
                    u = u0 + n
                    bank = banks[4 + n % 4]
                    bv = bank.rearrange("p (b n) -> p b n", b=2)
                    sc.wait_ge(*T.of("unit", u))
                    if n == 0 and l:
                        sc.wait_ge(*T.of("unit", FFN_0 + FFN - 1))
                    if n == 0 and l == 0:
                        sc.wait_ge(*V.of("conv", "up", DEPTH - 1, FJ - 1))
                    if n < 7:
                        for c in range(2):
                            act_(rkv[:, 2 * n + c, :], bank[:, c * SEQ:(c + 1) * SEQ], ACT.Identity,
                                 scale=sm(f"omu{l}", 14)[:, 2 * n + c:2 * n + c + 1]).then_inc(*A.done("unshift", l, n))
                    elif n == 8:
                        act_(conf[:, 2:4, :], bv, ACT.Sigmoid).then_inc(*A.done("in2", l, n))
                    elif n < 12:
                        dst = conf[:, 0:2, :] if n == 7 else short[:, 2 * (n - 9):2 * (n - 9) + 2, :]
                        act_(dst, bv, ACT.Copy).then_inc(*A.done("in2", l, n))
                    else:
                        act_(gk[:, 2 * (n - 12):2 * (n - 12) + 2, :], bv, ACT.Sigmoid).then_inc(*A.done("in2", l, n))
                sc.wait_ge(*V.of("omu", l))
                for n in range(7):
                    unit(n)
                left = list(range(7, N_IN2))

                def inject():
                    if left:
                        unit(left.pop(0))
                    if left and len(left) % 2:
                        unit(left.pop(0))
                sc.wait_ge(*V.of("shift", l, 6))
                act_(pg, pg, ACT.Sigmoid).then_inc(*A.done("pg", l))
                act_(wa[0:64, :], wa[0:64, :], ACT.Tanh).then_inc(*A.done("tanh", l))
                for x, dst, bias in ((0, t0, f"w0{l}"), (1, aa, f"a0{l}")):
                    sc.wait_ge(*T.of("lora", l, x))
                    for t in range(4):
                        act_(dst[:, t, :], banks[2 * x + t // 2][:, (t % 2) * SEQ:(t % 2 + 1) * SEQ], ACT.Sigmoid,
                             bias=pr(bias, t)).then_inc(*A.done("sig" if x == 0 else "aa", l))
                for t in range(4):
                    act_(t3[:, t, :], k_[:, t, :], ACT.Square, scale=pr(f"k_k{l}", t)).then_inc(*A.done("kksq", l))
                inject()
                sc.wait_ge(*V.of("kkms", l))
                act_(flat(t3), flat(t3), ACT.Sqrt).then_inc(*A.done("kknorm", l))
                sc.wait_ge(*V.of("cum", l))
                act_(flat(ep), flat(t1), ACT.Exp, scale=-KAPPA).then_inc(*A.done("ep", l))
                sc.wait_ge(*G.of("cumex", l))
                act_(flat(t2), flat(t2), ACT.Exp, scale=-KAPPA).then_inc(*A.done("ex", l))
                sc.wait_ge(*A.of("ep", l))
                act_(flat(t1), flat(t1), ACT.Exp, scale=KAPPA).then_inc(*A.done("en", l))
                inject()
                for n, x in enumerate((2, 2, 0, 0, 1, 1)):
                    sc.wait_ge(*T.of("tm", l, n))
                    act_(tm[:, x, n % 2, :], banks[2 + n % 2], ACT.Copy).then_inc(*A.done("tm", l, n))
                inject()
                for p in range(TB):
                    inject()
                    for lv in range(5):
                        for g in range(2):
                            sc.wait_ge(*T.of("lev", l, p, lv, g))
                            act_(flat(lev[:, 4 * g:4 * g + 4, :]), banks[2 * g], ACT.Copy)\
                                .then_inc(*A.done("lev", l, p, lv, g))
                        if lv % 2 == 1:
                            inject()
                    for cc in range(2):
                        c = 2 * p + cc
                        ch = slice(64 * cc, 64 * cc + 64)
                        sc.wait_ge(*T.of("x", l, c))
                        act_(xs[ch, :], banks[0][ch, :], ACT.Copy).then_inc(*A.done("xs", l, c))
                        sc.wait_ge(*T.of("o", l, c))
                        act_(rwo[ch, p, :], banks[2][ch, :], ACT.Copy).then_inc(*A.done("o", l, c))
                    inject()
                while left:
                    unit(left.pop(0))
                for i in range(2):
                    sc.wait_ge(*V.of("confcent", l))
                    act_(conf[:, i, :], ctmp[:, i, :], ACT.Square).then_inc(*A.done("confsq", l))
                sc.wait_ge(*T.of("confvar", l))
                act_(stmp[:, 0:SEQ], banks[3][:, 0:SEQ], ACT.Sqrt, bias=sm("ln_eps", 1)).then_inc(*A.done("confrms", l))
                sc.wait_ge(*T.of("rwoT", l))
                for t in range(2):
                    act_(yk[:, 2 * t:2 * t + 2, :], banks[t].rearrange("p (b n) -> p b n", b=2), ACT.Copy)\
                        .then_inc(*A.done("rwoT", l))
                sc.wait_ge(*V.of("confn", l))
                for i in range(2):
                    act_(yk[:, 4 + i, :], ctmp[:, i, :], ACT.Silu, scale=pr(f"conf_g{l}", i),
                         bias=pr(f"conf_lb{l}", i)).then_inc(*A.done("confy", l))
                layer_norm_sums("ln1", l, [V.of("mix", l, tb) for tb in range(TB)])
                (x_hi_out if l == 0 else xT_out)("f2", l, None)

            lnjunk = Z[:, 12288:12288 + D]
            for l in range(min(DEPTH, n_stages)):
                block1(l)
            if n_stages >= 3:
                mixer(0, MIX2_0)
                swiglu()
                layer_norm_sums("ln2", 0, [V.of("res2", 0, tb) for tb in range(TB)])
            if n_stages == 4:
                mixer(1, MIX2_1)
                sc.wait_ge(*V.of("negtop"))
                for tb in range(TB):
                    act_(sm("wexp", 16)[:, 8 * tb:8 * tb + 8], sm("logit", 16)[:, 8 * tb:8 * tb + 8], ACT.Exp,
                         bias=sm("negtop", 2)[:, tb:tb + 1]).then_inc(*A.done("wexp"))
                sc.wait_ge(*T.of("gather0"))
                for i in range(2):
                    act_(flat(xe_hi[:, 4 * i:4 * i + 4, :]), banks[2 + i], ACT.Copy).then_inc(*A.done("xe0", i))

                def turn(n, peeled):
                    where["turn"] = n
                    order = ffn_order()

                    def hT(j):
                        sc.wait_ge(*T.of("turned_hidden", j))
                        if j >= 2:
                            sc.wait_ge(*T.of("moe_down", j - 2))
                        elif not peeled:
                            sc.wait_ge(*T.before("moe_down", FJ - 1))
                        act_(hT_hi[:, j % 2, :], banks[6][:, 0:256], ACT.Copy).then_inc(*A.done("hT", j))
                    for i in range(FFN + 2):
                        if i < FFN:
                            sc.wait_ge(*moe_loaded(i, n))
                            if i >= SPLIT:
                                sc.wait_ge(*T.of("moe_unit", i - SPLIT))
                            elif not peeled:
                                sc.wait_ge(*T.before("moe_unit", i + FFN - SPLIT))
                            act_(part(w_hi, i), moe_slot(i), ACT.Copy).then_inc(*A.done("moe_hi", i))
                        kind, j = order[i - 2] if i >= 2 else ("none", 0)
                        if kind == "gate":
                            sc.wait_ge(*T.of("moe_gate", j))
                            if j >= 2:
                                sc.wait_ge(*V.of("moe_hidden", j - 2))
                            elif not peeled:
                                sc.wait_ge(*V.before("moe_hidden", FJ - 1))
                            act_(act_m[:, j % 2, :], banks[4][:, 0:256], ACT.Silu).then_inc(*A.done("moe_silu", j))
                            if j:
                                hT(j - 1)
                            if j == 2:
                                sc.wait_ge(*T.of("pickT"))
                                if not peeled:
                                    sc.wait_ge(*T.before("scattered"))
                                act_(pickT, banks[7][:, 0:256], ACT.Copy).then_inc(*A.done("pickT"))
                        if (kind, j) == ("down", FJ - 2):
                            sc.wait_ge(*T.of("gather"))
                            for x in range(2):
                                act_(flat(xe_hi[:, 4 * x:4 * x + 4, :]), banks[2 + x], ACT.Copy).then_inc(*A.done("xe", x))
                            hT(FJ - 1)
                    sc.wait_ge(*T.of("moe_down", FJ - 1))
                    act_(y_m[:, 0:512], banks[0], ACT.Copy).then_inc(*A.done("y"))
                A.enter()
                turn(0, True)
                A.again()
                load_turns(sc)
                with sc.Fori(1, where["turns"]) as n:
                    turn(n, False)
                A.leave()
                layer_norm_sums("ln2", 1, [V.of("res2", 1, tb) for tb in range(TB)])

        @block.vector
        def _(ve):
            v = nc.vector

            def own():
                ve.wait_ge(*V.last())

            def xT_out(tag, l, gain):
                for k in (2, 3, 6, 7):
                    ve.wait_ge(*T.of("turned", tag, l, k | 1))
                    src = banks[k // 2][:, (k % 2) * SEQ:(k % 2 + 1) * SEQ]
                    if gain:
                        v.tensor_scalar(xk[:, k, :], src, pr(gain, k), None, ALU.mult).then_inc(*V.done("xT", tag, l))
                    else:
                        v.tensor_copy(xk[:, k, :], src).then_inc(*V.done("xT", tag, l))

            def x_lo_out(tag, l, gain):
                for k in range(KT):
                    ve.wait_ge(*A.of("x_hi", tag, l, k | 1))
                    v.scalar_tensor_tensor(out=x_lo[:, k, :], in0=banks[k // 2][:, (k % 2) * SEQ:(k % 2 + 1) * SEQ],
                                           scalar=pr(gain, k) if gain else 1.0, in1=x_hi[:, k, :].bitcast(F32),
                                           op0=ALU.mult, op1=ALU.subtract).then_inc(*V.done("x_lo", tag, l))

            def with_splits(f0, evacuate):
                order = ffn_order()
                for n in range(FFN + 2):
                    if n < FFN:
                        u = f0 + n
                        ve.wait_ge(*A.of("hi", u))
                        if n >= SPLIT:
                            ve.wait_ge(*T.of("unit", u - SPLIT))
                        v.tensor_tensor(part(w_lo, n), slot(u), part(w_hi, n).bitcast(F32), ALU.subtract)\
                            .then_inc(*V.done("lo", u))
                    if n >= 2:
                        evacuate(*order[n - 2])

            def hidden_parts(h, j, key):
                own()
                if j >= 2:
                    ve.wait_ge(*T.of(*key[1]))
                v.tensor_copy(flat(h_hi[:, j % 2, :, :]), h).then_inc(*V.done("h_hi"))
                own()
                v.tensor_tensor(flat(h_lo[:, j % 2, :, :]), h, flat(h_hi[:, j % 2, :, :]).bitcast(F32), ALU.subtract)\
                    .then_inc(*V.done(*key[0]))

            def rms_apply(tag, l):
                ve.wait_ge(*A.of("ss", tag, l, 1))
                v.tensor_scalar(sm("ms", 2), sm(f"ss{tag}", 2), 1.0 / D, RMS_EPS, ALU.mult, ALU.add)\
                    .then_inc(*V.done("rms", tag, l))
                ve.wait_ge(*G.of("rstd", tag, l))
                for tb in range(TB):
                    v.tensor_scalar(wide[:, tb, :], xr[:, tb, :], sm("rstd", 2)[:, tb:tb + 1], None, ALU.mult)\
                        .then_inc(*V.done("normed", tag, l, tb))

            def residual(tag, l, last):
                ve.wait_ge(*last)
                for tb in range(TB):
                    for half in range(2):
                        d = xr[:, tb, half * 512:(half + 1) * 512]
                        v.tensor_tensor(d, d, banks[2 * tb + half], ALU.add).then_inc(*V.done("x_out", tag, l))

            def merge(blk, l):
                for c in range(4):
                    g = [flat(gk[:, 8 * b + 2 * c:8 * b + 2 * c + 2, :]) for b in range(3)]
                    for b in range(3):
                        n = 3 * c + b
                        ve.wait_ge(*T.of("branch", blk, l, n))
                        v.tensor_tensor(g[b], g[b], banks[4 + n % 4], ALU.mult).then_inc(*V.done("merged", blk, l, n))
                        own()
                        if b:
                            v.tensor_tensor(g[0], g[0], g[b], ALU.add).then_inc(*V.done("merged", blk, l, n))
                            own()

            def block1(l):
                u0 = l * LAYER1
                if l == 0:
                    v.memset(sm("rms_eps", 1), RMS_EPS).then_inc(*V.done("eps"))
                    v.memset(sm("ln_eps", 1), LN_EPS).then_inc(*V.done("eps"))
                    ve.wait_ge(s_par, 16)
                    ve.wait_ge(s_const, 16)
                    ve.wait_ge(s_x, 16)
                lam = pr(f"lam{l}", 0, 128)
                for i in range(2):
                    v.tensor_tensor(sm(f"lamprod{i}", 32), lam[:, 64 * i:64 * i + 32], lam[:, 64 * i + 32:64 * i + 64], ALU.mult)\
                        .then_inc(*V.done("lamprod", l))
                own()
                for i in range(2):
                    v.tensor_reduce(sm("lamsum", 2)[:, i:i + 1], sm(f"lamprod{i}", 32), AX.X, ALU.add)\
                        .then_inc(*V.done("lamsum", l))
                lam_init = 0.8 - 0.6 * float(np.exp(-0.3 * l))
                ve.wait_ge(*A.of("lamexp", l))
                v.scalar_tensor_tensor(out=sm("neglam", 1), in0=sm("lamexp", 2)[:, 1:2], scalar=-lam_init,
                                       in1=sm("lamexp", 2)[:, 0:1], op0=ALU.add, op1=ALU.subtract)\
                    .then_inc(*V.done("neglam", l))
                v.tensor_scalar(sm("negsink", 8), pr(f"sinks{l}", 0, 8), -1.0, None, ALU.mult).then_inc(*V.done("negsink", l))
                v.tensor_scalar(sm("sublnk", 1), pr(f"subln{l}", 0), 1.0 - lam_init, None, ALU.mult)\
                    .then_inc(*V.done("sublnk", l))
                rms_apply("b1", l)
                xT_out("b1", l, f"attn_norm{l}")
                def qk_norm(i):
                    c, m = QK_PAIRS[i]
                    w, dim = m * SEQ, HD if c < 9 else 32
                    b = i % 2
                    ve.wait_ge(*A.of("qrms", l, i))
                    v.reciprocal(rs[:, b, 0:w], rs[:, b, 0:w]).then_inc(*V.done("qrstd", l, i))
                    own()
                    ve.wait_ge(*A.of("in1", l, 8))
                    for j in range(m):
                        q = qk[:, (c + j) * SEQ:(c + j + 1) * SEQ]
                        v.scalar_tensor_tensor(out=q, in0=q, scalar=pr(f"q_gain{l}", c + j),
                                               in1=rs[:, b, j * SEQ:(j + 1) * SEQ], op0=ALU.mult, op1=ALU.mult)\
                            .then_inc(*V.done("qn", l, i))

                def qk_rot(i):
                    c, m = QK_PAIRS[i]
                    w, dim = m * SEQ, "64" if c < 9 else "32"
                    ve.wait_ge(*T.of("rotated", l, i))
                    if i >= 2:
                        ve.wait_ge(*G.of("roped", l, i - 2))
                    v.tensor_tensor(halves(rot[:, i % 2, 0:w]), halves(banks[2 + i % 2][:, 0:w]),
                                    grow(ct("sin" + dim), [P, m, SEQ], 1), ALU.mult)\
                        .then_inc(*V.done("rotsin", l, i))
                for i in range(len(QK_PAIRS)):
                    qk_norm(i)
                    if i:
                        qk_rot(i - 1)
                qk_rot(len(QK_PAIRS) - 1)

                def gate_recip(n):
                    ve.wait_ge(*G.of("gate1p", l, n))
                    g = flat(gk[:, 2 * n:2 * n + 2, :])
                    v.reciprocal(g, g).then_inc(*V.done("gate", l, n))
                for n in range(5):
                    gate_recip(n)
                pend = []
                for kind, n in SCHED:
                    if kind == "gate":
                        pend.append(n)
                        if len(pend) > 1:
                            gate_recip(pend.pop(0))
                        continue
                    br, h = JOBS[n][0], JOBS[n][1]
                    scale = 32 ** -0.5 if br[0] == "c" else HD ** -0.5
                    nm, rsm, se = sm(f"negmax{n % 2}", 2), sm(f"rowsum{n % 2}", 2), sm(f"sinkexp{n % 2}", 2)
                    if kind == "score":
                        mask = ct("window" if br == "b" else "causal")
                        own()
                        ve.wait_ge(*T.of("score", l, n))
                        if n >= 2:
                            ve.wait_ge(*A.of("exp", l, n - 2))
                            ve.wait_ge(*V.of("prob", l, n - 2))
                        for i, s in enumerate((slice(0, 128), slice(128, 384))):
                            v.tensor_tensor_reduce(out=msk[:, n % 2, s], in0=banks[n % 2][:, s], in1=mask[:, s], scale=1.0,
                                                   scalar=-3.0e38, op0=ALU.add, op1=ALU.max,
                                                   accum_out=sm("rowmax", 2)[:, i:i + 1]).then_inc(*V.done("masked", l, n))
                        own()
                        if br == "b":
                            v.tensor_scalar(nm, sm("rowmax", 2), -scale, sm("negsink", 8)[:, h:h + 1], ALU.mult, ALU.min)\
                                .then_inc(*V.done("negmax", l, n))
                        else:
                            v.tensor_scalar(nm, sm("rowmax", 2), -scale, None, ALU.mult).then_inc(*V.done("negmax", l, n))
                    elif kind == "norm":
                        ve.wait_ge(*A.of("exp", l, n))
                        if br == "b":
                            v.tensor_tensor(rsm, rsm, se, ALU.add).then_inc(*V.done("den", l, n))
                            own()
                        v.reciprocal(rsm, rsm).then_inc(*V.done("rden", l, n))
                        own()
                        if br == "c1":
                            v.tensor_scalar(rsm, rsm, sm("neglam", 1), None, ALU.mult).then_inc(*V.done("rlam", l, n))
                            own()
                        for i, s in enumerate((slice(0, 128), slice(128, 384))):
                            pb = prob[:, n % 3, s]
                            if br == "c1":
                                v.scalar_tensor_tensor(out=pb, in0=pb, scalar=rsm[:, i:i + 1],
                                                       in1=prob[:, (n - 1) % 3, s], op0=ALU.mult, op1=ALU.add)\
                                    .then_inc(*V.done("prob", l, n))
                            else:
                                v.tensor_scalar(pb, pb, rsm[:, i:i + 1], None, ALU.mult).then_inc(*V.done("prob", l, n))
                        own()
                for n in pend:
                    gate_recip(n)
                ve.wait_ge(*A.of("crms", l))
                v.reciprocal(rs[:, 0, :], rs[:, 0, :]).then_inc(*V.done("crstd", l))
                own()
                for i in range(2):
                    ve.wait_ge(*A.of("csquare", l, i))
                    v.scalar_tensor_tensor(out=yk[:, 6 + i, :], in0=yk[:, 6 + i, :], scalar=sm("sublnk", 1),
                                           in1=rs[:, 0, i * SEQ:(i + 1) * SEQ], op0=ALU.mult, op1=ALU.mult)\
                        .then_inc(*V.done("cnormed", l))
                merge("b1", l)
                residual("b1", l, T.of("unit", u0 + N_IN1 + N_PROJ + N_OUT - 1))
                rms_apply("f1", l)
                x_lo_out("f1", l, f"mlp_norm{l}")

                def evacuate(kind, j):
                    if kind == "down":
                        return
                    dst, c0 = (cg, 0) if kind == "gate" else (cv, 22)
                    ve.wait_ge(*A.of("tap2", kind, l, j))
                    bank = banks[4 + 2 * (j % 2) + (kind == "up")]
                    for tap in (1, 0):
                        lag = 2 - tap
                        for c in range(2):
                            d = dst[:, j % 2, c, lag:SEQ]
                            v.scalar_tensor_tensor(out=d, in0=bank[:, c * SEQ:(c + 1) * SEQ - lag],
                                                   scalar=pr(f"conv_w{l}", tap * 44 + c0 + 2 * j + c), in1=d,
                                                   op0=ALU.mult, op1=ALU.add).then_inc(*V.done("conv", kind, l, j))
                        own()
                    if kind == "up":
                        ve.wait_ge(*A.of("silu1", l, j))
                        h = flat(hid[:, j % 2, :, :])
                        v.tensor_tensor(h, act[:, j % 2, :], flat(cv[:, j % 2, :, :]), ALU.mult).then_inc(*V.done("h"))
                        hidden_parts(h, j, (("hidden1", l, j), ("down", l, j - 2)))
                with_splits(u0 + N_IN1 + N_PROJ + N_OUT, evacuate)
                residual("f1", l, T.of("down", l, FJ - 1))
                V.steps[("final_x", l)] = V.steps[("x_out", "f1", l)]

            def swiglu():
                def evacuate(kind, j):
                    if kind == "up":
                        ve.wait_ge(*A.of("dense_silu", j))
                        ve.wait_ge(*T.of("dense_up", j))
                        h = flat(hid[:, j % 2, :, :])
                        v.tensor_tensor(h, act[:, j % 2, :], banks[4 + 2 * (j % 2) + 1], ALU.mult).then_inc(*V.done("h"))
                        hidden_parts(h, j, (("dense_hidden", j), ("dense_down", j - 2)))
                with_splits(FFN_0, evacuate)

            def layer_norm(tag, l, out_key):
                ve.wait_ge(*A.of("lnsum", tag, l, 1))
                v.tensor_scalar(sm("negmean", 2), sm("lnsum", 2), -1.0 / D, None, ALU.mult).then_inc(*V.done("negmean", tag, l))
                ve.wait_ge(*A.of("lnsq", tag, l, 1))
                v.tensor_scalar(sm("ms", 2), sm("lnsq", 2), 1.0 / D, LN_EPS, ALU.mult, ALU.add)\
                    .then_inc(*V.done("lnvar", tag, l))
                ve.wait_ge(*G.of("lnrstd", tag, l))
                ve.wait_ge(s_norm_rows, 16 * (2 * l + (2 if tag == "ln2" else 1)))
                for tb in range(TB):
                    v.tensor_scalar(xr[:, tb, :], xr[:, tb, :], sm("negmean", 2)[:, tb:tb + 1],
                                    sm("rstd", 2)[:, tb:tb + 1], ALU.add, ALU.mult).then_inc(*V.done("lnn", tag, l))
                    own()
                    v.tensor_tensor(xr[:, tb, :], xr[:, tb, :], norm_rows[:, 0:D], ALU.mult)\
                        .then_inc(*V.done(out_key, l, tb))

            def mixer(l, u0):
                if l == 0:
                    for i in range(DEPTH):
                        v.tensor_scalar(sm(f"omu{i}", 14), pr(f"mu{i}", 0, 14), -1.0, 1.0, ALU.mult, ALU.add)\
                            .then_inc(*V.done("omu", i))
                        v.tensor_scalar(sm(f"oka{i}", 4), pr(f"k_a{i}", 0, 4), -1.0, 1.0, ALU.mult, ALU.add)\
                            .then_inc(*V.done("oka", i))
                own()
                for buf in (xs, us):
                    v.memset(buf, 0.0).then_inc(*V.done("zeroed"))
                xT_out("b2", l, None)
                for n in range(7):
                    ve.wait_ge(*A.of("unshift", l, n))
                    for c in range(2):
                        d = rkv[:, 2 * n + c, 1:SEQ]
                        v.scalar_tensor_tensor(out=d, in0=banks[4 + n % 4][:, c * SEQ:(c + 1) * SEQ - 1],
                                               scalar=pr(f"mu{l}", 2 * n + c), in1=d, op0=ALU.mult, op1=ALU.add)\
                            .then_inc(*V.done("shift", l, n))
                own()
                for t in range(4):
                    v.tensor_scalar(kk[:, t, :], k_[:, t, :], pr(f"k_k{l}", t), None, ALU.mult).then_inc(*V.done("kkr", l))
                ve.wait_ge(*A.of("sig", l))
                for t in range(4):
                    v.tensor_tensor_scan(t1[:, t, :], ct("reset"), t0[:, t, :], 0.0, ALU.mult, ALU.add)\
                        .then_inc(*V.done("cum", l))
                for i in range(2):
                    ve.wait_ge(*T.of("kksum", l, 1))
                    v.tensor_scalar(flat(t3)[:, i * 512:(i + 1) * 512], banks[i], 1e-24, None, ALU.max)\
                        .then_inc(*V.done("kkms", l))
                ve.wait_ge(*A.of("kknorm", l))
                v.reciprocal(flat(t3), flat(t3)).then_inc(*V.done("kkrn", l))
                own()
                v.tensor_tensor(flat(kk), flat(kk), flat(t3), ALU.mult).then_inc(*V.done("kk", l))
                own()
                ve.wait_ge(*A.of("ex", l))
                v.tensor_tensor(flat(a_), flat(kk), flat(t2), ALU.mult).then_inc(*V.done("at", l))
                v.tensor_tensor(flat(kk), flat(kk), flat(aa), ALU.mult).then_inc(*V.done("ka", l))
                own()
                ve.wait_ge(*A.of("en", l))
                v.scalar_tensor_tensor(out=flat(b_), in0=flat(kk), scalar=-1.0, in1=flat(t1), op0=ALU.mult, op1=ALU.mult)\
                    .then_inc(*V.done("bn", l))
                own()
                for t in range(4):
                    v.tensor_scalar(kk[:, t, :], aa[:, t, :], pr(f"k_a{l}", t), sm(f"oka{l}", 4)[:, t:t + 1],
                                    ALU.mult, ALU.add).then_inc(*V.done("kscale", l))
                own()
                v.tensor_tensor(flat(k_), flat(k_), flat(kk), ALU.mult).then_inc(*V.done("k2", l))
                own()
                ve.wait_ge(*G.of("cumex", l))
                for t in range(4):
                    v.scalar_tensor_tensor(out=t0[:, t, :], in0=r_[:, t, :], scalar=pr(f"r_k{l}", t), in1=k_[:, t, :],
                                           op0=ALU.mult, op1=ALU.mult).then_inc(*V.done("rk", l))
                own()
                v.tensor_tensor(flat(k_), flat(k_), flat(t1), ALU.mult).then_inc(*V.done("kt", l))
                v.tensor_tensor(flat(r_), flat(r_), flat(ep), ALU.mult).then_inc(*V.done("rt", l))
                v.tensor_copy(sm("ends", 16), flat(ep).rearrange("p (c s) -> p c s", s=CHUNK)[:, :, CHUNK - 1])\
                    .then_inc(*V.done("ends", l))
                ve.wait_ge(*T.of("bonus", l))
                v.tensor_copy(sm("bonus", 16), banks[0][:, 0:16]).then_inc(*V.done("bonus", l))
                ends = sm("ends", 16).rearrange("p (t c) -> p t c", t=4)

                def conf_some(k):
                    if not started:
                        started.append(1)
                        ve.wait_ge(*A.of("in2", l, 8))
                        v.tensor_tensor(conf[:, 0:2, :], conf[:, 0:2, :], conf[:, 2:4, :], ALU.mult)\
                            .then_inc(*V.done("confu", l))
                        own()
                        for i in range(2):
                            v.tensor_scalar(ctmp[:, i, :], conf[:, i, :], pr(f"conf_dw{l}", i * 31 + 30),
                                            pr(f"conf_b{l}", i), ALU.mult, ALU.add).then_inc(*V.done("conf30", l))
                        own()
                    for _ in range(k):
                        if not taps:
                            return
                        lag = taps.pop(0)
                        for i in range(2):
                            d = ctmp[:, i, lag:SEQ]
                            v.scalar_tensor_tensor(out=d, in0=conf[:, i, 0:SEQ - lag],
                                                   scalar=pr(f"conf_dw{l}", i * 31 + 30 - lag), in1=d,
                                                   op0=ALU.mult, op1=ALU.add).then_inc(*V.done("confconv", l))
                        own()
                started, taps = [], list(range(1, CONF_TAPS))
                for p in range(TB):
                    for h in range(8):
                        ve.wait_ge(*T.of("gram", l, p, h))
                        if h == 0 and p:
                            ve.wait_ge(*T.of("o", l, 1))
                        v.tensor_tensor(gram[:, 4 * (h % 2) + h // 2, :].rearrange("p (a n) -> p a n", a=2),
                                        banks[h % 2].rearrange("p (a n) -> p a n", a=2),
                                        grow(ct("chunk2"), [P, 2, 256], 1), ALU.mult)\
                            .then_inc(*V.done("gram", l, p, h))
                        if h >= 6:
                            g = h % 2
                            ve.wait_ge(*T.of("m", l, p, g))
                            if p == 0 and g == 0:
                                ve.wait_ge(*A.of("tm", l, 1))
                            v.tensor_tensor(tri[:, 4 * g:4 * g + 4, :], banks[2 + g].rearrange("p (h n) -> p h n", h=4),
                                            grow(ct("first"), [P, 4, P], 1), ALU.mult).then_inc(*V.done("first", l, p, g))
                    for lv in range(5):
                        for g in range(2):
                            ve.wait_ge(*T.of("inv", l, p, lv, g))
                            hs = slice(4 * g, 4 * g + 4)
                            if lv < 4:
                                v.tensor_tensor(flat(tri[:, hs, :]), flat(tri[:, hs, :]), banks[2 * g + 1],
                                                ALU.add).then_inc(*V.done("tri", l, p, lv, g))
                            v.tensor_tensor(flat(inv[:, hs, :]), flat(inv[:, hs, :]), banks[2 * g],
                                            ALU.add).then_inc(*V.done("inv", l, p, lv, g))
                            if p or lv >= 1:
                                conf_some(2)
                    for cc in range(2):
                        c = 2 * p + cc
                        ch = slice(64 * cc, 64 * cc + 64)
                        ve.wait_ge(*T.of("u", l, c))
                        v.tensor_copy(us[ch, :], banks[1][ch, :]).then_inc(*V.done("us", l, c))
                        ve.wait_ge(*T.of("s", l, c))
                        if c:
                            v.tensor_tensor(stmp, flat(state), banks[3], ALU.add).then_inc(*V.done("stmp", l, c))
                            own()
                            ve.wait_ge(*T.of("o", l, c))
                        src = stmp if c else banks[3]
                        for t in range(4):
                            v.scalar_tensor_tensor(out=state[:, t, :], in0=src[:, t * P:(t + 1) * P],
                                                   scalar=ends[:, t, c:c + 1], in1=ct("ones64"), op0=ALU.mult,
                                                   op1=ALU.mult).then_inc(*V.done("state", l, c))
                        own()
                conf_some(99)
                own()
                ve.wait_ge(*A.of("o", l, 3))
                og = rwo.rearrange("p b (h n) -> p (b h) n", n=HD)
                sqv = t0.rearrange("p t n -> p (t n)").rearrange("p (h n) -> p h n", n=HD)
                ve.wait_ge(*T.of("o", l, 3))
                v.tensor_reduce(sm("gsum", 16), og, AX.X, ALU.add).then_inc(*V.done("gsum", l))
                own()
                v.tensor_scalar(sm("gsum", 16), sm("gsum", 16), 1.0 / HD, None, ALU.mult).then_inc(*V.done("gmean", l))
                own()
                v.tensor_tensor(og, og, grow(sm("gsum", 16), [P, 16, HD], 2), ALU.subtract).then_inc(*V.done("gcent", l))
                own()
                v.tensor_tensor(sqv, og, og, ALU.mult).then_inc(*V.done("gsq", l))
                own()
                v.tensor_reduce(sm("gsum", 16), sqv, AX.X, ALU.add).then_inc(*V.done("gvar", l))
                own()
                v.tensor_scalar(sm("gvar", 16), sm("gsum", 16), 1.0 / HD, GN_EPS, ALU.mult, ALU.add).then_inc(*V.done("gms", l))
                tmv = tm[:, 2, :, :].rearrange("p b (h n) -> p (b h) n", n=HD)
                v.tensor_tensor(tmv, tmv, grow(sm("bonus", 16), [P, 16, HD], 2), ALU.mult).then_inc(*V.done("bv", l))
                ve.wait_ge(*G.of("grstd", l))
                v.tensor_tensor(og, og, grow(sm("gvar", 16), [P, 16, HD], 2), ALU.mult).then_inc(*V.done("gn", l))
                own()
                ve.wait_ge(s_group_rows, 16 * (l + 1))
                v.tensor_tensor(rwo, rwo, grow(group_rows[:, 0:512], [P, TB, 512], 1), ALU.mult).then_inc(*V.done("gg", l))
                own()
                v.tensor_tensor(rwo, rwo, grow(group_rows[:, 512:1024], [P, TB, 512], 1), ALU.add).then_inc(*V.done("gb", l))
                own()
                v.tensor_tensor(rwo, rwo, tm[:, 2, :, :], ALU.add).then_inc(*V.done("gbonus", l))
                own()
                ve.wait_ge(*T.of("outgate", l))
                for tb in range(TB):
                    v.tensor_tensor(rwo[:, tb, :], rwo[:, tb, :], banks[tb], ALU.mult).then_inc(*V.done("gated", l))
                ve.wait_ge(*A.of("in2", l, 11))
                v.tensor_tensor(short[:, 2:4, :], short[:, 2:4, :], short[:, 4:6, :], ALU.mult).then_inc(*V.done("shortu", l))
                own()
                for i in range(2):
                    v.tensor_scalar(short[:, 4 + i, :], short[:, 2 + i, :], pr(f"short_dw{l}", 3 * i + 2), None, ALU.mult)\
                        .then_inc(*V.done("short2", l))
                own()
                for lag in (1, 2):
                    for i in range(2):
                        d = short[:, 4 + i, lag:SEQ]
                        v.scalar_tensor_tensor(out=d, in0=short[:, 2 + i, 0:SEQ - lag],
                                               scalar=pr(f"short_dw{l}", 3 * i + 2 - lag), in1=d, op0=ALU.mult,
                                               op1=ALU.add).then_inc(*V.done("shortc", l))
                    own()
                v.tensor_tensor(yk[:, 6:8, :], short[:, 0:2, :], short[:, 4:6, :], ALU.mult).then_inc(*V.done("shorty", l))
                ve.wait_ge(*T.of("confmean", l))
                v.tensor_tensor(ctmp, ctmp, grow(banks[2][:, 0:SEQ], [P, 2, SEQ], 1), ALU.subtract)\
                    .then_inc(*V.done("confcent", l))
                ve.wait_ge(*T.of("confvar", l))
                ve.wait_ge(*A.of("confrms", l))
                v.reciprocal(stmp[:, 0:SEQ], stmp[:, 0:SEQ]).then_inc(*V.done("confrstd", l))
                own()
                ve.wait_ge(*A.of("confsq", l))
                v.tensor_tensor(ctmp, ctmp, grow(stmp[:, 0:SEQ], [P, 2, SEQ], 1), ALU.mult).then_inc(*V.done("confn", l))
                for n in range(N_IN2 - 4, N_IN2):
                    ve.wait_ge(*A.of("in2", l, n))
                merge("b2", l)
                ve.wait_ge(*T.of("unit", u0 + MIX2 - 1))
                for tb in range(TB):
                    for half in range(2):
                        d = xr[:, tb, half * 512:(half + 1) * 512]
                        v.scalar_tensor_tensor(out=d, in0=d, scalar=ALPHA, in1=banks[2 * tb + half], op0=ALU.mult,
                                               op1=ALU.add).then_inc(*V.done("mix", l, tb))
                own()
                layer_norm("ln1", l, "x1")
                (x_lo_out if l == 0 else xT_out)("f2", l, None)

            for l in range(min(DEPTH, n_stages)):
                block1(l)
            if n_stages >= 3:
                mixer(0, MIX2_0)
                swiglu()
                ve.wait_ge(*T.of("dense_down", FJ - 1))
                for tb in range(TB):
                    for half in range(2):
                        d = xr[:, tb, half * 512:(half + 1) * 512]
                        v.scalar_tensor_tensor(out=d, in0=d, scalar=ALPHA, in1=banks[2 * tb + half], op0=ALU.mult,
                                               op1=ALU.add).then_inc(*V.done("res2", 0, tb))
                own()
                layer_norm("ln2", 0, "x2")
            if n_stages == 4:
                mixer(1, MIX2_1)
                lg, wt = sm("logit", 16), sm("wexp", 16)
                gt_, eq_ = stmp[:, 0:64], stmp[:, 64:128]
                ve.wait_ge(*T.of("router"))
                v.tensor_copy(lg, banks[0][:, 0:16]).then_inc(*V.done("logit"))
                own()
                lv = lg.rearrange("p (b e) -> p b e", b=TB)
                v.tensor_reduce(sm("negtop", 2), lv, AX.X, ALU.max, negate=True).then_inc(*V.done("negtop"))
                for tb in range(TB):
                    fs = grow(lv[:, tb, :], [P, 8, 8], 1)
                    es = grow(lv[:, tb, :], [P, 8, 8], 2)
                    cmp_, eq = (m.rearrange("p (e f) -> p e f", e=8) for m in (gt_, eq_))
                    v.tensor_tensor(eq, fs, es, ALU.is_equal).then_inc(*V.done("eq"))
                    v.tensor_tensor(cmp_, fs, es, ALU.is_gt).then_inc(*V.done("gt"))
                    own()
                    v.tensor_tensor(eq_, eq_, ct("tie"), ALU.mult).then_inc(*V.done("tie"))
                    own()
                    v.tensor_tensor(gt_, gt_, eq_, ALU.add).then_inc(*V.done("rank"))
                    own()
                    v.tensor_reduce(sm("rank", 16)[:, 8 * tb:8 * tb + 8], cmp_, AX.X, ALU.add).then_inc(*V.done("rank"))
                    own()
                ve.wait_ge(*A.of("wexp"))
                sel, place, wgt = (sm(n, 48).rearrange("p (b c) -> p b c", b=TB) for n in ("sel", "place", "wgt"))
                for n in ("sel", "place", "wgt"):
                    v.memset(sm(n, 48), 0.0).then_inc(*V.done("empty"))
                own()
                rk = sm("rank", 16).rearrange("p (b e) -> p b e", b=TB)
                v.tensor_scalar(sel[:, :, 0:8], rk, 1.5, None, ALU.is_lt).then_inc(*V.done("selected"))
                own()
                wv = wt.rearrange("p (b e) -> p b e", b=TB)
                v.tensor_tensor(wv, wv, sel[:, :, 0:8], ALU.mult).then_inc(*V.done("wsel"))
                own()
                v.tensor_reduce(sm("wsum", 2), wv, AX.X, ALU.add).then_inc(*V.done("wsum"))
                own()
                v.reciprocal(sm("wsum", 2), sm("wsum", 2)).then_inc(*V.done("wrec"))
                own()
                v.tensor_tensor(wgt[:, :, 0:8], wv, grow(sm("wsum", 2), [P, TB, 8], 2), ALU.mult)\
                    .then_inc(*V.done("weights"))
                ve.wait_ge(*T.of("places"))
                v.tensor_copy(place[:, :, 0:8], banks[1][:, 0:16].rearrange("p (b e) -> p b e", b=TB))\
                    .then_inc(*V.done("place"))
                v.tensor_scalar(sm("full", 8), banks[1][:, 16:24], P + 0.5, None, ALU.is_gt).then_inc(*V.done("full"))
                own()

                def one_hot(dst, n, times, key):
                    for tb in range(TB):
                        at = bass.ds(n + 24 * tb, 1)
                        v.tensor_scalar(dst[:, tb, :], ct("slots"), sm("place", 48)[:, at], sm(times, 48)[:, at],
                                        ALU.is_equal, ALU.mult).then_inc(*V.done(key))
                ve.wait_ge(*V.of("place"))
                one_hot(pick, 0, "sel", "pick0")
                v.memset(gates[:, 4096:6144], 0.0).then_inc(*V.done("routed"))
                ve.wait_ge(*T.of("gather0"))

                def xe_low(ready, key):
                    for i in range(2):
                        ve.wait_ge(*A.of(ready, i))
                        v.tensor_tensor(flat(xe_lo[:, 4 * i:4 * i + 4, :]), banks[2 + i],
                                        flat(xe_hi[:, 4 * i:4 * i + 4, :]).bitcast(F32), ALU.subtract).then_inc(*V.done(key))
                xe_low("xe0", "xe0")
                v.tensor_tensor_scan(sm("nth", 8), ct("ones", 0, 8), sm("full", 8), 0.0, ALU.mult, ALU.add)\
                    .then_inc(*V.done("nth"))
                own()
                v.tensor_scalar(turn_cells[:, 0:1], sm("nth", 8)[0:1, 7:8], float(N_EXP), None, ALU.add)\
                    .then_inc(*V.done("cells"))
                for q in range(MORE):
                    v.scalar_tensor_tensor(out=sm("mine", 8), in0=sm("nth", 8), scalar=q + 1.0, in1=sm("full", 8),
                                           op0=ALU.is_equal, op1=ALU.mult).then_inc(*V.done("mine"))
                    own()
                    v.tensor_tensor(sm("which", 8), sm("mine", 8), ct("slots", 0, 8), ALU.mult).then_inc(*V.done("which"))
                    own()
                    v.tensor_reduce(sm("whom", 1), sm("which", 8), AX.X, ALU.add).then_inc(*V.done("whom"))
                    own()
                    v.tensor_copy(turn_cells[:, 1 + q:2 + q], sm("whom", 1)[0:1, :]).then_inc(*V.done("cells"))
                    for table, less in ((sel, 0.0), (place, -float(P)), (wgt, 0.0)):
                        for tb in range(TB):
                            v.tensor_tensor(sm("which", 8), sm("mine", 8), table[:, tb, 0:8], ALU.mult)\
                                .then_inc(*V.done("which"))
                            own()
                            v.tensor_reduce(sm("whom", 1), sm("which", 8), AX.X, ALU.add).then_inc(*V.done("whom"))
                            own()
                            v.tensor_scalar(table[:, tb, 8 + q:9 + q], sm("whom", 1), less, None, ALU.add)\
                                .then_inc(*V.done("column"))
                            own()
                V.same(("turns",), ("column",))

                def turn(n, peeled):
                    where["turn"] = n
                    order = ffn_order()
                    if not peeled:
                        ve.wait_ge(*T.before("pickT"))
                    one_hot(pickw, n, "wgt", "pickw")
                    ve.wait_ge(*(T.of("gather0") if peeled else T.before("gather")))
                    one_hot(pick, n + 1, "sel", "pick")

                    def hT(j):
                        ve.wait_ge(*A.of("hT", j))
                        v.tensor_tensor(hT_lo[:, j % 2, :], banks[6][:, 0:256], hT_hi[:, j % 2, :].bitcast(F32), ALU.subtract)\
                            .then_inc(*V.done("hT", j))
                    for i in range(FFN + 2):
                        if i < FFN:
                            ve.wait_ge(*A.of("moe_hi", i))
                            v.tensor_tensor(part(w_lo, i), moe_slot(i), part(w_hi, i).bitcast(F32), ALU.subtract)\
                                .then_inc(*V.done("moe_lo", i))
                        kind, j = order[i - 2] if i >= 2 else ("none", 0)
                        if kind == "gate" and j:
                            hT(j - 1)
                        if kind == "up":
                            ve.wait_ge(*A.of("moe_silu", j))
                            ve.wait_ge(*T.of("moe_up", j))
                            if j >= 2:
                                ve.wait_ge(*T.of("turned_hidden", j - 2))
                            elif not peeled:
                                ve.wait_ge(*T.before("turned_hidden", FJ - 1))
                            v.tensor_tensor(hid_m[:, j % 2, :], act_m[:, j % 2, :], banks[5][:, 0:256], ALU.mult)\
                                .then_inc(*V.done("moe_hidden", j))
                        if (kind, j) == ("down", FJ - 2):
                            xe_low("xe", "xe")
                            hT(FJ - 1)
                    ve.wait_ge(*T.of("moe_down", FJ - 1))
                    v.tensor_copy(y_m[:, 512:1024], banks[1]).then_inc(*V.done("y"))
                    ve.wait_ge(*T.of("scattered"))
                    for tb in range(TB):
                        for half in range(2):
                            d = moe_acc[:, tb, half * 512:(half + 1) * 512]
                            v.tensor_tensor(d, d, banks[2 + 4 * tb + half], ALU.add).then_inc(*V.done("acc"))
                    own()
                V.enter()
                turn(0, True)
                V.again()
                load_turns(ve)
                with ve.Fori(1, where["turns"]) as n:
                    turn(n, False)
                V.leave()
                for tb in range(TB):
                    v.scalar_tensor_tensor(out=xr[:, tb, :], in0=xr[:, tb, :], scalar=ALPHA, in1=moe_acc[:, tb, :],
                                           op0=ALU.mult, op1=ALU.add).then_inc(*V.done("res2", 1, tb))
                own()
                layer_norm("ln2", 1, "x2")
            V.steps[("final",)] = (V.kind, V.now - V.start)

        @block.gpsimd
        def _(po):
            g = nc.gpsimd

            def own():
                po.wait_ge(*G.last())

            def power(out, in_, key):
                n = in_.shape[-1]
                g.tensor_tensor(out, in_, mh.broadcast_to([P, n]), ALU.pow).then_inc(*key)

            def rms(tag, l):
                po.wait_ge(*V.of("rms", tag, l))
                power(sm("rstd", 2), sm("ms", 2), G.done("rstd", tag, l))

            def block1(l):
                rms("b1", l)

                def roped(i):
                    c, m = QK_PAIRS[i]
                    w, dim = m * SEQ, "64" if c < 9 else "32"
                    q = qk[:, c * SEQ:(c + m) * SEQ]
                    po.wait_ge(*T.of("rotated", l, i))
                    g.tensor_tensor(halves(q), halves(q), grow(ct("cos" + dim), [P, m, SEQ], 1), ALU.mult).then_inc(*G.done("cosq", l, i))
                    own()
                    po.wait_ge(*V.of("rotsin", l, i))
                    g.tensor_tensor(q, q, rot[:, i % 2, 0:w], ALU.add).then_inc(*G.done("roped", l, i))

                def gate(n):
                    po.wait_ge(*A.of("in1", l, 9 + n))
                    gv = flat(gk[:, 2 * n:2 * n + 2, :])
                    g.tensor_scalar(gv, gv, 1.0, None, ALU.add).then_inc(*G.done("gate1p", l, n))
                for i in range(len(QK_PAIRS)):
                    if i < 5:
                        gate(i)
                    if i:
                        roped(i - 1)
                roped(len(QK_PAIRS) - 1)
                for kind, n in SCHED:
                    if kind == "gate":
                        gate(n)
                rms("f1", l)

            def ln(tag, l, key):
                po.wait_ge(*V.of("lnvar", tag, l))
                power(sm("rstd", 2), sm("ms", 2), G.done("lnrstd", tag, l))
                for tb in range(TB):
                    po.wait_ge(*V.of(key, l, tb))
                    g.tensor_tensor(xr[:, tb, :], xr[:, tb, :], norm_rows[:, D:2 * D], ALU.add).then_inc(*G.done(key, l))

            def load_norm_rows(l, which):
                own()
                g.dma_start(norm_rows, rows_d[l, 2 * D * which:2 * D * (which + 1)].partition_broadcast(P))\
                    .then_inc(s_norm_rows, 16)

            def load_group_rows(l):
                g.dma_start(group_rows, rows_d[l, 4 * D:4 * D + 1024].partition_broadcast(P)).then_inc(s_group_rows, 16)

            def mixer(l, u0):
                po.wait_ge(*V.of("cum", l))
                g.tensor_tensor(flat(t2), flat(t1), flat(t0), ALU.subtract).then_inc(*G.done("cumex", l))
                for p in range(TB):
                    for gg in range(2):
                        hs = slice(4 * gg, 4 * gg + 4)
                        po.wait_ge(*V.of("first", l, p, gg))
                        po.wait_ge(*V.of("gram", l, p, 6 + gg))
                        if p:
                            po.wait_ge(*T.of("o", l, 1))
                        else:
                            po.wait_ge(*V.of("bonus", l))
                            po.wait_ge(*V.of("ends", l))
                        ident4 = grow(ct("ident"), [P, 4, P], 1)
                        g.tensor_tensor(tri[:, hs, :], tri[:, hs, :], ident4, ALU.add).then_inc(*G.done("tri1", l, p, gg))
                        g.tensor_tensor(inv[:, hs, :], gram[:, hs, 0:P], grow(ct("levels", 0, P), [P, 4, P], 1), ALU.mult)\
                            .then_inc(*G.done("inv1", l, p, gg))
                        own()
                        g.tensor_tensor(inv[:, hs, :], inv[:, hs, :], ident4, ALU.add).then_inc(*G.done("first", l, p, gg))
                    for lv in range(5):
                        for gg in range(2):
                            hs = slice(4 * gg, 4 * gg + 4)
                            if lv:
                                po.wait_ge(*T.of("lev", l, p, lv - 1, gg))
                            g.tensor_tensor(off[:, hs, :], gram[:, hs, 0:P],
                                            grow(ct("levels", (lv + 1) * P, P), [P, 4, P], 1), ALU.mult).then_inc(*G.done("off", l, p, lv, gg))
                po.wait_ge(*V.of("gms", l))
                power(sm("gvar", 16), sm("gvar", 16), G.done("grstd", l))
                ln("ln1", l, "x1")
                load_norm_rows(l, 1)

            g.memset(mh, -0.5).then_inc(*G.done("minus_half"))
            g.dma_start(norm_rows, rows_d[0, 0:2 * D].partition_broadcast(P)).then_inc(s_norm_rows, 16)
            load_group_rows(0)
            own()
            for l in range(min(DEPTH, n_stages)):
                block1(l)
            if n_stages >= 3:
                mixer(0, MIX2_0)
                po.wait_ge(*V.of("gb", 0))
                load_group_rows(1)
                ln("ln2", 0, "x2")
            if n_stages == 4:
                load_norm_rows(1, 0)
                mixer(1, MIX2_1)
                load_turns(po)
                ln("ln2", 1, "x2")
            G.steps[("final",)] = (G.kind, G.now - G.start)

    return {"matmul_done": T.steps, "scalar_done": A.steps, "vector_done": V.steps, "pool_done": G.steps}


def constants():
    f = np.float32
    c = {}
    i, j = np.meshgrid(np.arange(P), np.arange(P), indexing="ij")
    c["ident"] = (i == j).astype(f)
    c["ones64"] = (i // 64 == j // 64).astype(f)
    c["ones32"] = (i // 32 == j // 32).astype(f)
    c["mean256"] = np.full((P, P), 1.0 / 256, f)
    for dim in (64, 32):
        half = dim // 2
        rot = np.zeros((P, P), f)
        for m in range(P):
            if m % dim < half:
                rot[m + half, m] = -1.0
            else:
                rot[m - half, m] = 1.0
        c[f"rot{dim}"] = rot
        inv = (f(1.0) / np.power(f(10000.0), np.arange(0, dim, 2, dtype=f) / f(dim))).astype(f)
        ang = np.arange(SEQ, dtype=f)[None, :] * inv[np.arange(P) % half][:, None]
        c[f"cos{dim}"] = np.cos(ang).astype(f)
        c[f"sin{dim}"] = np.sin(ang).astype(f)
    causal = np.where(j <= i, 0.0, -BIG).astype(f)
    c["causal"] = np.concatenate([causal, np.zeros((P, P), f), causal], 1)
    c["window"] = np.concatenate([causal, np.where(j > i, 0.0, -BIG).astype(f), causal], 1)
    same = i // CHUNK == j // CHUNK
    strict, upto = (same & (i < j)).astype(f), (same & (i <= j)).astype(f)
    c["chunk2"] = np.concatenate([strict, upto], 1)
    c["earlier"] = (i < j).astype(f)
    c["slots"] = j.astype(f)
    c["ones"] = np.ones((P, P), f)

    def level(n, lo, hi):
        return ((lo // (2 * n) == hi // (2 * n)) & (lo % (2 * n) < n) & (hi % (2 * n) >= n)).astype(f)
    c["first"] = level(1, j, i)
    c["levels"] = np.concatenate([level(n, i, j) for n in (1, 2, 4, 8, 16, 32)], 1)
    c["heads2"] = (i[:, 0:2] // 64 == j[:, 0:2]).astype(f)
    c["reset"] = np.tile((np.arange(SEQ) % CHUNK != 0).astype(f), (P, 1))
    e, g = np.meshgrid(np.arange(8), np.arange(8), indexing="ij")
    c["tie"] = np.tile((g < e).astype(f).reshape(1, 64), (P, 1))
    return pack(CST, c)


def pack(names, arrays):
    out = np.zeros((P, names.size), np.float32)
    for name, (a, w) in names.at.items():
        out[:, a:a + w] = arrays[name]
    return out


def columns(v):
    return v.reshape(-1, P).T


def features_units(w):
    return w.reshape(KT, P, -1, 256).transpose(2, 1, 0, 3).reshape(-1, P, UNIT)


def rows_units(w):
    return w.reshape(-1, 2, P, D).transpose(0, 2, 1, 3).reshape(-1, P, UNIT)


HEAD_ORDER = [(h // 2) + 4 * (h % 2) for h in range(8)]


def lay_out(x):
    stream, par = np.empty((N_UNITS, P, UNIT), np.float32), {}
    at = [0]

    def put(u):
        stream[at[0]:at[0] + len(u)] = u
        at[0] += len(u)

    def put_ffn(gate, up, down):
        gate, up, down = features_units(gate), features_units(up), rows_units(down)
        for kind, j in ffn_order():
            put({"gate": gate, "up": up, "down": down}[kind][j:j + 1])

    for l in range(DEPTH):
        w = np.array(x["w_in"][l])
        w[:, 768:1280] = w[:, 768:1280].reshape(D, 8, HD)[:, HEAD_ORDER, :].reshape(D, 512)
        put(features_units(w))
        put(rows_units(x["w_pa"][l]))
        put(rows_units(x["w_pb"][l].reshape(8, HD, D)[HEAD_ORDER].reshape(512, D)))
        put(rows_units(x["w_pc"][l]))
        put(rows_units(x["w_out"][l]))
        put_ffn(x["w_up"][l][:, :FF], x["w_up"][l][:, FF:], x["w_down"][l])
        par[f"attn_norm{l}"] = columns(x["attn_norm"][l])
        par[f"mlp_norm{l}"] = columns(x["mlp_norm"][l])
        two = lambda n: np.tile(x[n][l], 2).reshape(P, 1)
        four = lambda n: np.tile(x[n][l], 4).reshape(P, 1)
        par[f"q_gain{l}"] = np.concatenate([two("qn_a")] * 2 + [two("kn_a")] * 2 + [two("qn_b")] * 4 + [two("kn_b")]
                                           + [four("qn_c")] * 2 + [four("kn_c")] * 2, 1)
        par[f"subln{l}"] = two("subln")
        par[f"sinks{l}"] = np.tile(x["sinks"][l].reshape(1, 8), (P, 1))
        lam = np.concatenate([x[n][l] for n in ("lam_q1", "lam_k1", "lam_q2", "lam_k2")])
        par[f"lam{l}"] = np.tile(lam.reshape(1, 128), (P, 1))
        par[f"conv_w{l}"] = x["conv_w"][l].reshape(3, 44, P).transpose(2, 0, 1).reshape(P, 132)
        par[f"conv_b{l}"] = columns(x["conv_b"][l])
    for l in range(DEPTH):
        put(features_units(x["w_in_2"][l]))
        for n in ("rwkv_w_o_2", "conf_w_o_2", "short_w_o_2", "w_out_2"):
            put(rows_units(x[n][l]))
        if l == 0:
            put_ffn(x["ffn_w_gate_2"][0], x["ffn_w_up_2"][0], x["ffn_w_down_2"][0])
        else:
            for e in range(N_EXP):
                put_ffn(x["moe_w_gate_2"][0, e], x["moe_w_up_2"][0, e], x["moe_w_down_2"][0, e])
        for name, n in (("mu", "rwkv_mu_2"), ("w0", "rwkv_w0_2"), ("a0", "rwkv_a0_2"), ("k_k", "rwkv_k_k_2"),
                        ("k_a", "rwkv_k_a_2"), ("r_k", "rwkv_r_k_2"), ("conf_b", "conf_dw_b_2"),
                        ("conf_g", "conf_ln_g_2"), ("conf_lb", "conf_ln_b_2")):
            par[f"{name}{l}"] = columns(x[n][l].reshape(-1))
        par[f"conf_dw{l}"] = x["conf_dw_2"][l].reshape(31, 2, P).transpose(2, 1, 0).reshape(P, 62)
        par[f"short_dw{l}"] = x["short_dw_2"][l].reshape(3, 2, P).transpose(2, 1, 0).reshape(P, 6)
        par[f"lora{l}"] = np.concatenate([x["rwkv_w2_2"][l], x["rwkv_a2_2"][l]], 0)
        par[f"g2{l}"] = x["rwkv_g2_2"][l]
    par["router"] = x["moe_router_2"][0].reshape(KT, P, N_EXP).transpose(1, 0, 2).reshape(P, KT * N_EXP)
    assert at[0] == N_UNITS
    rows = np.stack([np.concatenate([x[n][l] for n in ("ln1_g_2", "ln1_b_2", "ln2_g_2", "ln2_b_2", "rwkv_ln_g_2",
                                                       "rwkv_ln_b_2")]) for l in range(DEPTH)])
    return {"stream": stream, "par": pack(PAR, par), "cst": constants(), "rows": rows, "x": x["x"][0]}


N_STAGES = 4


def kernel(**inputs):
    import concourse.bacc as _bacc
    from concourse.bass_utils import run_bass_kernel_spmd as _run

    arrays = lay_out({n: np.asarray(a) for n, a in inputs.items()})
    known = {}
    for _ in range(2):
        nc = _bacc.Bacc("TRN2", target_bir_lowering=False, num_devices=1)
        d = {n: nc.dram_tensor(f"in_{n}", a.shape, F32, kind="ExternalInput").ap() for n, a in arrays.items()}
        out = nc.dram_tensor("out", (SEQ, D), F32, kind="ExternalOutput").ap()
        learned = known
        known = emit(nc, known, d["stream"], d["par"], d["cst"], d["rows"], d["x"], out, N_STAGES)
    assert known == learned
    r = _run(nc, [{f"in_{n}": a for n, a in arrays.items()}], core_ids=[0])
    return r.results[0]["out"].reshape(1, SEQ, D)
```

```python
from contextlib import ExitStack

import numpy as np

import concourse.bass as bass
from concourse import mybir

F32 = mybir.dt.float32
F32R = mybir.dt.float32r
ALU = mybir.AluOpType
ACT = mybir.ActivationFunctionType
AX = mybir.AxisListType

P = 128
SEQ = 256
TB = SEQ // P
D = 1024
KT = D // P
DEPTH = 2
FF = 2816
FJ = FF // 256
N_EXP = 8
MORE = 3
UNIT = 2048
HD = 64
N_QK = 13
CHUNK = 64
KAPPA = float(np.exp(-0.5))
ALPHA = (2.0 * DEPTH) ** 0.25
RMS_EPS = 1e-6
LN_EPS = 1e-5
GN_EPS = 64e-5
BIG = 1e30
CONF_TAPS = 31

N_IN1 = 21
N_PROJ = 4
N_OUT = 4
LAYER1 = N_IN1 + N_PROJ + N_OUT + 3 * FJ
N_IN2 = 24
MIX2 = N_IN2 + N_PROJ + N_OUT
FFN = 3 * FJ
MIX2_0 = DEPTH * LAYER1
FFN_0 = MIX2_0 + MIX2
MIX2_1 = FFN_0 + FFN
MOE_0 = MIX2_1 + MIX2
N_UNITS = MOE_0 + N_EXP * FFN
RING = 4
MOE_RING = 3
SCATTER = (3, 5)
POOL_SPLIT = 11
SPLIT = 3


def ffn_order():
    order = []
    for j in range(FJ):
        order += [("gate", j), ("up", j)]
        if j:
            order.append(("down", j - 1))
    return order + [("down", FJ - 1)]


BRANCHES = {"b1": [(c, b) for c in range(4) for b in (0, 1, 2)],
            "b2": [(0, 1), (0, 2), (1, 1), (1, 2), (0, 0), (1, 0)] + [(c, b) for c in (2, 3) for b in (1, 2, 0)]}
FFN_UNIT = {key: n for n, key in enumerate(ffn_order())}


class Names:

    def __init__(self):
        self.at, self.size = {}, 0

    def add(self, name, width):
        self.at[name] = (self.size, width)
        self.size += width


def param_names():
    n = Names()
    for l in range(DEPTH):
        for name, w in (("attn_norm", 8), ("mlp_norm", 8), ("q_gain", N_QK), ("subln", 1), ("sinks", 8), ("lam", 128),
                        ("conv_w", 3 * 44), ("conv_b", 44)):
            n.add(f"{name}{l}", w)
        for name, w in (("mu", 14), ("w0", 4), ("a0", 4), ("k_k", 4), ("k_a", 4), ("r_k", 4), ("conf_dw", 62),
                        ("conf_b", 2), ("conf_g", 2), ("conf_lb", 2), ("short_dw", 6), ("lora", 512), ("g2", 512)):
            n.add(f"{name}{l}", w)
    n.add("router", KT * N_EXP)
    return n


def const_names():
    n = Names()
    for name, w in (("ident", 128), ("ones64", 128), ("ones32", 128), ("rot64", 128), ("rot32", 128), ("mean256", 128),
                    ("causal", 384), ("window", 384), ("cos64", 256), ("sin64", 256), ("cos32", 256), ("sin32", 256),
                    ("chunk2", 256), ("earlier", 128), ("slots", 128), ("ones", 128), ("first", 128), ("levels", 6 * 128), ("heads2", 2), ("reset", 256), ("tie", 64)):
        n.add(name, w)
    return n


PAR = param_names()
CST = const_names()


class Steps:

    def __init__(self, sem, known, where):
        self.sem, self.known, self.where = sem, known, where
        self.now, self.steps, self.kind, self.start = 0, {}, "once", 0

    def done(self, *key):
        self.now += 1
        self.steps[key] = (self.kind, self.now - self.start)
        return self.sem, 1

    def _value(self, kind, n, lag=0):
        if kind == "once":
            return n
        base, per = self.known.get("base", 1), self.known.get("per", 1)
        if kind == "turn":
            return self.where["turn"] * per + (base - lag * per + n)
        return self.where["turns"] * per + (base + n)

    def of(self, *key):
        return self.sem, self._value(*(self.steps.get(key) or self.known.get(key, ("once", 1))))

    def before(self, *key):
        return self.sem, self._value(*self.known.get(key, ("turn", 1)), lag=1)

    def last(self):
        return self.sem, self._value(self.kind, self.now - self.start)

    def same(self, key, as_key):
        self.steps[key] = self.steps[as_key]

    def enter(self):
        self.kind, self.start = "turn", self.now
        self.steps["base"] = self.now

    def again(self):
        self.steps["per"] = self.now - self.start
        self.now = self.start

    def leave(self):
        self.kind, self.start = "after", self.now
        self.where["turn"] = self.where["turns"]


def emit(nc, known, stream, par_d, cst_d, rows_d, x_d, out_d, n_stages):
    ctx = ExitStack()
    with ctx:
        def sb(name, width):
            return ctx.enter_context(nc.sbuf_tensor(name, [P, -(-width // 8) * 8], F32))[:, 0:width]

        where = {"turn": None, "turns": None}

        def steps(name):
            return Steps(ctx.enter_context(nc.semaphore(name)), known.get(name, {}), where)

        ring = sb("ring", RING * UNIT)
        ring_at = nc.sbuf_base - 4 * RING * UNIT
        par = sb("par", PAR.size)
        cst = sb("cst", CST.size)
        norm_rows = sb("norm_rows", 2 * D)
        group_rows = sb("group_rows", 2 * 512)
        xres = sb("xres", TB * D)
        xT = sb("xT", KT * SEQ)
        xT_at = nc.sbuf_base - 4 * KT * SEQ
        gates = sb("gates", 24 * SEQ)
        yT = sb("yT", KT * SEQ)
        small = sb("small", 512)
        mh = sb("minus_half", 1)
        Z = sb("Z", 21504)
        z_at = nc.sbuf_base - 4 * 21504

        def rounded(name, at, width, base=None):
            return nc.alloc_sbuf_tensor_at(name, [P, width], F32R, offset=(z_at if base is None else base) + 4 * at)[:, :]

        w_hi, w_lo = rounded("w_hi", 0, SPLIT * UNIT), rounded("w_lo", SPLIT * UNIT, SPLIT * UNIT)
        x_hi, x_lo = (rounded(n, a, KT * SEQ).rearrange("p (k n) -> p k n", k=KT)
                      for n, a in (("x_hi", 13440), ("x_lo", 15488)))
        h_hi, h_lo = (rounded(n, a, 1024).rearrange("p (b c n) -> p b c n", b=2, c=2)
                      for n, a in (("h_hi", 17536), ("h_lo", 18560)))

        in_hi = rounded("in_hi", 17408, 2 * UNIT)
        ring_lo = rounded("ring_lo", 0, RING * UNIT, ring_at)
        x1_hi, x1_lo = (rounded(n, a, KT * SEQ, base).rearrange("p (k n) -> p k n", k=KT)
                        for n, a, base in (("x1_hi", 0, xT_at), ("x1_lo", 10368, None)))

        mix_hi = rounded("mix_hi", 6144, SPLIT * UNIT)
        def in_half(n):
            return in_hi[:, (n % 2) * UNIT:(n % 2 + 1) * UNIT]

        def part(w, n):
            return w[:, (n % SPLIT) * UNIT:(n % SPLIT + 1) * UNIT]
        banks = [ctx.enter_context(nc.psum_tensor(f"bank{i}", [P, 512], F32))[:, :] for i in range(8)]

        def pr(name, i=0, n=1):
            a, _ = PAR.at[name]
            return par[:, a + i:a + i + n]

        def ct(name, i=0, n=None):
            a, w = CST.at[name]
            return cst[:, a + i:a + (w if n is None else i + n)]

        small_at = {}

        def sm(name, width):
            if name not in small_at:
                used = sum(w for _, w in small_at.values())
                assert used + width <= 512
                small_at[name] = (used, width)
            a, w = small_at[name]
            return small[:, a:a + w]

        T = steps("matmul_done")
        A = steps("scalar_done")
        V = steps("vector_done")
        G = steps("pool_done")
        s_head = ctx.enter_context(nc.semaphore("head_loaded"))
        s_const = ctx.enter_context(nc.semaphore("const_loaded"))
        s_par = ctx.enter_context(nc.semaphore("par_loaded"))
        s_x = ctx.enter_context(nc.semaphore("x_loaded"))
        s_norm_rows = ctx.enter_context(nc.semaphore("norm_rows_loaded"))
        s_group_rows = ctx.enter_context(nc.semaphore("group_rows_loaded"))
        s_out = ctx.enter_context(nc.semaphore("out_stored"))
        s_slot = [ctx.enter_context(nc.semaphore(f"slot{i}_loaded")) for i in range(RING)]
        s_moe_slot = [ctx.enter_context(nc.semaphore(f"moe_slot{i}_loaded")) for i in range(MOE_RING)]
        block = ctx.enter_context(nc.Block())

        def slot(u):
            return ring[:, (u % RING) * UNIT:(u % RING + 1) * UNIT]

        def slot_lo(u):
            return ring_lo[:, (u % RING) * UNIT:(u % RING + 1) * UNIT]

        def loaded(u):
            return s_slot[u % RING], 16 * (u // RING + 1)

        def moe_slot(i):
            return slot(i % MOE_RING)

        def moe_loaded(i, e):
            per = FFN // MOE_RING
            return s_moe_slot[i % MOE_RING], e * (16 * per) + 16 * (i // MOE_RING + 1)

        def cols3(i):
            return slice(i * P, (i + 1) * P)

        QK_TILES = {0: 0, 1: 1, 2: 2, 3: 3, 6: 4, 7: 5, 8: 6, 9: 7, 10: 8, 12: 9, 13: 10, 14: 11, 15: 12}
        QK_PAIRS = [(0, 2), (2, 2), (4, 2), (6, 2), (8, 1), (9, 2), (11, 2)]

        JOBS = []
        for h in range(4):
            JOBS.append(("a", h, h // 2, 64 * (h % 2), h // 2, 2 + h // 2, 64 * (h % 2), 64, h * 64))
        for h in range(8):
            JOBS.append(("b", (h // 2) + 4 * (h % 2), 2 + h // 2, 64 * (h % 2), 4 + h // 2, 8, 64 * (h % 2), 64,
                         256 + 64 * (h % 2)))
        for h in range(4):
            for c in range(2):
                JOBS.append((f"c{c}", h, 6 + h // 2, 64 * (h % 2), 9 + h // 2, 11 + h // 2, 64 * (h % 2) + 32 * c, 32,
                             384 + h * 64))

        def attention_schedule():
            out, gate = [], 0
            for t in range(len(JOBS) + 3):
                if t < len(JOBS):
                    out.append(("score", t))
                if 1 <= t <= len(JOBS):
                    out.append(("norm", t - 1))
                if 2 <= t <= len(JOBS) + 1:
                    out.append(("turn", t - 2))
                if 3 <= t:
                    out.append(("value", t - 3))
                if t % 2 == 1 and gate < 7:
                    out.append(("gate", 5 + gate))
                    gate += 1
                elif gate and t % 2 == 0 and 9 + 5 + gate - 1 + 2 < N_IN1:
                    out.append(("split", 9 + 5 + gate - 1 + 2))
            assert gate == 7
            return out

        SCHED = attention_schedule()

        class Filler:

            def __init__(self, half, whole):
                self.half, self.whole, self.pos = half, whole, 0

            def __call__(self, halves):
                for _ in range(halves):
                    n = 7 + self.pos // 2
                    if n < N_IN2:
                        self.half(n, self.pos % 2)
                        if self.pos % 2:
                            self.whole(n)
                        self.pos += 1

            def next_unit(self):
                return 7 + (self.pos + 1) // 2

        START_FILL, GRAM_FILL, LEVEL_FILL, CHUNK_FILL = (6, 4, 4), 2, 1, 1

        qk = Z[:, 0:N_QK * SEQ]
        vtm = Z[:, 3328:3328 + TB * 640].rearrange("p (b n) -> p b n", b=TB)
        o = 3328 + TB * 640
        sq = Z[:, o:o + 1024].rearrange("p (b n) -> p b n", b=2)
        rs = Z[:, o + 1024:o + 2048].rearrange("p (b n) -> p b n", b=2)
        rot = Z[:, o + 2048:o + 3072].rearrange("p (b n) -> p b n", b=2)
        msk = Z[:, o + 3072:o + 3072 + 2 * 384].rearrange("p (b n) -> p b n", b=2)
        prob = Z[:, o + 3840:o + 3840 + 3 * 384].rearrange("p (b n) -> p b n", b=3)
        probT = Z[:, o + 4992:o + 4992 + 2 * 384].rearrange("p (b n) -> p b n", b=2)
        wide = Z[:, o + 5760:o + 5760 + 2 * D].rearrange("p (b n) -> p b n", b=TB)
        junk = Z[:, o + 5760 + 2 * D:o + 5760 + 3 * D]
        squares = Z[:, o + 5760 + 3 * D:o + 5760 + 3 * D + N_QK * SEQ]
        xr = xres.rearrange("p (b n) -> p b n", b=TB)
        xk = xT.rearrange("p (k n) -> p k n", k=KT)
        yk = yT.rearrange("p (k n) -> p k n", k=KT)
        gk = gates.rearrange("p (k n) -> p k n", k=24)

        hid = gates[:, 0:1024].rearrange("p (b c n) -> p b c n", b=2, c=2)
        act = gates[:, 1024:2048].rearrange("p (b n) -> p b n", b=2)
        cg = gates[:, 2048:3072].rearrange("p (b c n) -> p b c n", b=2, c=2)
        cv = gates[:, 3072:4096].rearrange("p (b c n) -> p b c n", b=2, c=2)
        act_m, hid_m = (gates[:, a:a + 512].rearrange("p (b n) -> p b n", b=2) for a in (0, 512))
        y_m = gates[:, 1536:2560]
        pick = gates[:, 2560:2816].rearrange("p (b n) -> p b n", b=TB)
        pickw = gates[:, 2816:3072].rearrange("p (b n) -> p b n", b=TB)
        pickT = gates[:, 3072:3328]
        moe_acc = gates[:, 4096:6144].rearrange("p (b n) -> p b n", b=TB)
        xe_hi, xe_lo = (rounded(n, a, KT * P).rearrange("p (k n) -> p k n", k=KT)
                        for n, a in (("xe_hi", 13440), ("xe_lo", 14464)))
        hT_hi, hT_lo = (rounded(n, a, 512).rearrange("p (b n) -> p b n", b=2) for n, a in (("hT_hi", 15488), ("hT_lo", 16000)))
        turn_cells = ctx.enter_context(nc.sbuf_tensor("turn_cells", [1, 2 + MORE], mybir.dt.int32))[:, :]

        rkv = Z[:, 0:3584].rearrange("p (t n) -> p t n", n=SEQ)
        r_, k_, v_ = rkv[:, 0:4, :], rkv[:, 4:8, :], rkv[:, 8:12, :]
        wa, pg = rkv[:, 12, :], rkv[:, 13, :]
        conf = Z[:, 3584:4608].rearrange("p (t n) -> p t n", n=SEQ)
        short = Z[:, 4608:6144].rearrange("p (t n) -> p t n", n=SEQ)
        a_ = Z[:, 6144:7168].rearrange("p (t n) -> p t n", n=SEQ)
        b_ = Z[:, 7168:8192].rearrange("p (t n) -> p t n", n=SEQ)
        tm = Z[:, 8192:11264].rearrange("p (x b n) -> p x b n", x=3, b=TB)
        rwo = Z[:, 11264:12288].rearrange("p (b n) -> p b n", b=TB)
        gram = Z[:, 12288:16384].rearrange("p (h n) -> p h n", h=8)
        inv = Z[:, 16384:17408].rearrange("p (h n) -> p h n", h=8)
        tri = v_.rearrange("p t n -> p (t n)").rearrange("p (h n) -> p h n", h=8)
        off = Z[:, 17408:18432].rearrange("p (h n) -> p h n", h=8)
        lev = Z[:, 18432:19456].rearrange("p (h n) -> p h n", h=8)
        xs = Z[:, 19456:19968]
        us = Z[:, 19968:20480]
        state = Z[:, 20480:20992].rearrange("p (t n) -> p t n", n=P)
        stmp = Z[:, 20992:21504]
        ctmp = yk[:, 4:6, :]
        lnx = Z[:, 17536:19584].rearrange("p (b n) -> p b n", b=TB)
        t0 = Z[:, 12288:13312].rearrange("p (t n) -> p t n", n=SEQ)
        t1 = Z[:, 13312:14336].rearrange("p (t n) -> p t n", n=SEQ)
        t2 = Z[:, 14336:15360].rearrange("p (t n) -> p t n", n=SEQ)
        t3 = Z[:, 15360:16384].rearrange("p (t n) -> p t n", n=SEQ)
        kk = Z[:, 16384:17408].rearrange("p (t n) -> p t n", n=SEQ)
        aa = Z[:, 17408:18432].rearrange("p (t n) -> p t n", n=SEQ)
        ep = Z[:, 18432:19456].rearrange("p (t n) -> p t n", n=SEQ)

        def flat(v):
            return v.rearrange("p a b -> p (a b)")

        def halves(v):
            return v.rearrange("p (b n) -> p b n", n=SEQ)

        def grow(v, shape, axis):
            return v.unsqueeze(axis).broadcast_to(shape)

        def load_turns(eng):
            eng.wait_ge(*V.of("turns"))
            where["turns"] = eng.value_load(turn_cells[0:1, 0:1], min_val=N_EXP, max_val=N_EXP + MORE)

        @block.sync
        def _(sp):
            sp.dma_start(xr, x_d.rearrange("(b p) n -> p b n", p=P)).then_inc(s_x, 16)
            heads = [(par, par_d, PAR.at["attn_norm0"][1], s_par), (cst, cst_d, CST.at["ident"][1], s_const)]
            for to, src, w, _ in heads:
                sp.dma_start(to[:, 0:w], src[:, 0:w]).then_inc(s_head, 16)
            n_main = {1: LAYER1, 2: 2 * LAYER1, 3: FFN_0 + FFN, 4: MOE_0}[n_stages]
            ffn_starts = [l * LAYER1 + N_IN1 + N_PROJ + N_OUT for l in range(DEPTH)] + [FFN_0]
            for u in range(n_main):
                if u >= RING:
                    split = any(f <= u - RING < f + FFN for f in ffn_starts)
                    sp.wait_ge(*(V.of("lo", u - RING) if split else T.of("unit", u - RING)))
                sp.dma_start(slot(u), stream[u]).then_inc(s_slot[u % RING], 16)
                if u == 1:
                    for to, src, w, sem in heads:
                        sp.dma_start(to[:, w:], src[:, w:]).then_inc(sem, 16)
            if n_stages == 4:
                def load(i, expert):
                    sp.dma_start(moe_slot(i), stream[expert * FFN + (MOE_0 + i)]).then_inc(s_moe_slot[i % MOE_RING], 16)

                def last_unit(i):
                    return max(u for u in range(MOE_0) if u % RING == i % MOE_RING)

                def turn(n, peeled, expert, next_expert):
                    where["turn"] = n
                    for i in range(2, FFN + 2):
                        if i < FFN:
                            if i - MOE_RING >= 2:
                                sp.wait_ge(*V.of("moe_lo", i - MOE_RING))
                            elif i == 2:
                                sp.wait_ge(*(T.of("unit", last_unit(2)) if peeled else V.before("moe_lo", FFN - 1)))
                            else:
                                sp.wait_ge(*(V.of("first_lo", i - MOE_RING) if peeled else V.before("moe_lo", i - MOE_RING)))
                            load(i, expert)
                        else:
                            sp.wait_ge(*V.of("moe_lo", i - MOE_RING))
                            load(i - FFN, next_expert)

                def further(n):
                    return sp.value_load(turn_cells[0:1, bass.ds(n - (N_EXP - 1), 1)], min_val=0, max_val=N_EXP - 1)
                for i in range(2):
                    sp.wait_ge(*T.of("unit", last_unit(i)))
                    load(i, 0)
                turn(0, True, 0, 1)
                with sp.Fori(1, N_EXP - 1) as n:
                    turn(n, False, n, n + 1)
                load_turns(sp)
                turn(N_EXP - 1, False, N_EXP - 1, sp.value_load(turn_cells[0:1, 1:2], min_val=0, max_val=N_EXP - 1))
                with sp.If(N_EXP < where["turns"]):
                    with sp.Fori(N_EXP, where["turns"]) as n:
                        turn(n, False, further(n), further(n + 1))
            sp.wait_ge(*V.of("final"))
            if n_stages >= 3:
                sp.wait_ge(*G.of("final"))
            sp.dma_start(out_d.rearrange("(b p) n -> p b n", p=P), xr).then_inc(s_out, 16)
            sp.wait_ge(s_out, 16)

        @block.tensor
        def _(pe):
            mm = nc.tensor.matmul

            def turn_wide(src, tag, l, ready):
                for k in range(KT):
                    for tb in range(TB):
                        if k == 0:
                            pe.wait_ge(*ready[tb])
                        t = nc.tensor.transpose(banks[k // 2][:, (k % 2) * SEQ + tb * P:(k % 2) * SEQ + (tb + 1) * P],
                                                src[:, tb, k * P:(k + 1) * P], ct("ident"))
                    t.then_inc(*T.done("turned", tag, l, k))

            def features(bank, w, l, halves=(0, 1)):
                wv = w.rearrange("p (k n) -> p k n", k=KT)
                for c in halves:
                    for k in range(KT):
                        r = mm(bank[:, c * SEQ:(c + 1) * SEQ], wv[:, k, c * P:(c + 1) * P], xk[:, k, :],
                               start=(k == 0), stop=(k == KT - 1))
                return r

            def rows(src, w, first, last):
                wv = w.rearrange("p (c n) -> p c n", c=2)
                for c in range(2):
                    for tb in range(TB):
                        for half in range(2):
                            r = mm(banks[2 * tb + half], src(c)[:, tb * P:(tb + 1) * P],
                                   wv[:, c, half * 512:(half + 1) * 512], start=(first and c == 0),
                                   stop=(last and c == 1))
                return r

            def features_split(bank, w, x):
                for c in range(2):
                    for k in range(KT):
                        at = slice(k * 256 + c * P, k * 256 + (c + 1) * P)
                        for a, b in ((0, 0), (0, 1), (1, 0)):
                            r = mm(bank[:, c * SEQ:(c + 1) * SEQ], w[a][:, at], x[b][:, k, :],
                                   start=(k == 0 and a == b), stop=(k == KT - 1 and a == 1))
                return r

            def tokens_split(bank, w, x):
                for tb in range(TB):
                    for k in range(KT):
                        for a, b in ((0, 0), (0, 1), (1, 0)):
                            r = mm(bank[:, tb * SEQ:(tb + 1) * SEQ], x[b][:, k, tb * P:(tb + 1) * P],
                                   w[a][:, k * 256:(k + 1) * 256], start=(k == 0 and a == b), stop=(k == KT - 1 and a == 1))
                return r

            def ffn_parts(n):
                return (part(w_hi, n), part(w_lo, n)), (x_hi, x_lo)

            def rows_split(j, n):
                for c in range(2):
                    for tb in range(TB):
                        for half in range(2):
                            for a, b in ((h_hi, w_hi), (h_lo, w_hi), (h_hi, w_lo)):
                                r = mm(banks[2 * tb + half], a[:, j % 2, c, tb * P:(tb + 1) * P],
                                       part(b, n)[:, c * D + half * 512:c * D + (half + 1) * 512],
                                       start=(j == 0 and c == 0 and a is h_hi and b is w_hi),
                                       stop=(j == FJ - 1 and c == 1 and b is w_lo))
                return r

            def project(l, blk, splits, u0, last_ready):
                for n in range(N_PROJ):
                    pe.wait_ge(*loaded(u0 + n))
                k_at = [0, splits[0], splits[0] + splits[1]]
                late = BRANCHES[blk][-1][1]
                for n, (c, b) in enumerate(BRANCHES[blk]):
                    bank = banks[4 + n % 4]
                    if n >= 4:
                        pe.wait_ge(*V.of("merged", blk, l, n - 4))
                    if b == late and c == 0:
                        last_ready()
                    for half in range(2):
                        for k in range(k_at[b], k_at[b] + splits[b]):
                            wv = slot(u0 + k // 2).rearrange("p (c n) -> p c n", c=2)
                            col = (2 * c + half) * P
                            r = mm(bank[:, half * SEQ:(half + 1) * SEQ], wv[:, k % 2, col:col + P], yk[:, k, :],
                                   start=(k == k_at[b]), stop=(k == k_at[b] + splits[b] - 1))
                    r.then_inc(*T.done("branch", blk, l, n))
                for n in range(N_PROJ):
                    T.steps[("unit", u0 + n)] = T.steps[("branch", blk, l, 11)]

            def project_out(l, blk, u0):
                for n in range(N_OUT):
                    u = u0 + n
                    pe.wait_ge(*loaded(u))
                    pe.wait_ge(*V.of("merged", blk, l, 11))
                    at = 8 * BRANCHES[blk][0][1] + 2 * n
                    rows(lambda c: gk[:, at + c, :], slot(u), n == 0, n == N_OUT - 1).then_inc(*T.done("unit", u))

            def block1(l):
                u0 = l * LAYER1
                if l == 0:
                    pe.wait_ge(s_head, 32)
                turn_wide(wide, "b1", l, [V.of("normed", "b1", l, tb) for tb in range(TB)])

                def unit(n):
                    u = u0 + n
                    pe.wait_ge(*(G if n >= POOL_SPLIT else V).of("lo", u))
                    if n == 0:
                        pe.wait_ge(*V.of("x_lo", "b1", l))
                    if n >= 4:
                        pe.wait_ge(*A.of("in1", l, n - 4))
                    product = tokens_split if n in (2, 8) else features_split
                    product(banks[4 + n % 4], (in_half(n), slot_lo(u)), (x1_hi, x1_lo)).then_inc(*T.done("unit", u))

                for n in range(9):
                    unit(n)
                    if n == 6:
                        pe.wait_ge(*A.of("in1", l, 5))
                        for tb in range(TB):
                            r = nc.tensor.transpose(banks[3][:, tb * P:(tb + 1) * P], msk[:, 0, tb * P:(tb + 1) * P], ct("ident"))
                        r.then_inc(*T.done("vb", l))
                if l == 0:
                    pe.wait_ge(s_const, 16)
                for i, (c, m) in enumerate(QK_PAIRS):
                    w = m * SEQ
                    ones = "ones64" if c < 9 else "ones32"
                    if i < 5:
                        unit(9 + i)
                    pe.wait_ge(*A.of("square", l, c + m - 1))
                    if i >= 2:
                        pe.wait_ge(*A.of("qrms", l, i - 2))
                    mm(banks[i % 2][:, 0:w], ct(ones), squares[:, c * SEQ:(c + m) * SEQ], start=True, stop=True)\
                        .then_inc(*T.done("sumsq", l, i))
                    if i >= 1:
                        rotate(l, i - 1)
                rotate(l, len(QK_PAIRS) - 1)

                for kind, n in SCHED:
                    if kind == "gate":
                        unit(9 + n)
                    elif kind == "score":
                        br, h, ot, ob, qt, kt, base, kk_, vc = JOBS[n]
                        if n == 0:
                            pe.wait_ge(*G.of("roped", l, len(QK_PAIRS) - 1))
                            pe.wait_ge(*V.of("qn", l, len(QK_PAIRS) - 1))
                            pe.wait_ge(*V.of("rotsin", l, len(QK_PAIRS) - 1))
                        if n >= 2:
                            pe.wait_ge(*V.of("masked", l, n - 2))
                        q = qk[base:base + kk_, qt * SEQ:(qt + 1) * SEQ]
                        k = qk[base:base + kk_, kt * SEQ:(kt + 1) * SEQ]
                        mm(banks[n % 2][:, 0:128], q[:, 0:128], k[:, 0:128], start=True, stop=True)
                        mm(banks[n % 2][:, 128:384], q[:, 128:256], k, start=True, stop=True)\
                            .then_inc(*T.done("score", l, n))
                    elif kind == "turn" and JOBS[n][0] != "c0":
                        pe.wait_ge(*V.of("prob", l, n))
                        if n >= 1:
                            m = n - 1 if JOBS[n - 1][0] != "c0" else n - 2
                            pe.wait_ge(*A.of("probT", l, m))
                        for i in range(3):
                            r = nc.tensor.transpose(banks[2][:, i * P:(i + 1) * P], prob[:, n % 3, cols3(i)], ct("ident"))
                        r.then_inc(*T.done("turnp", l, n))
                    elif kind == "value" and JOBS[n][0] != "c0":
                        br, h, ot, ob, qt, kt, base, kk_, vc = JOBS[n]
                        pe.wait_ge(*A.of("probT", l, n))
                        if ob == 0 and ot >= 1:
                            pe.wait_ge(*A.of("y", l, ot - 1))
                        dst = banks[3][ob:ob + HD, 0:SEQ]
                        mm(dst, vtm[:, 0, vc:vc + HD], probT[:, n % 2, 0:256], start=True, stop=False)
                        mm(dst[:, 128:256], vtm[:, 1, vc:vc + HD], probT[:, n % 2, 256:384], start=False, stop=True)\
                            .then_inc(*T.done("value", l, n))
                for i in range(2):
                    pe.wait_ge(*A.of("csquare", l, i))
                    if i == 0:
                        pe.wait_ge(*V.of("masked", l, len(JOBS) - 1))
                    r = mm(banks[0][:, i * SEQ:(i + 1) * SEQ], ct("ones64"), sq[:, 0, i * SEQ:(i + 1) * SEQ],
                           start=True, stop=True)
                r.then_inc(*T.done("csum", l))
                for i in range(3):
                    pe.wait_ge(*A.of("in1", l, N_IN1 - 1 - i))
                pe.wait_ge(*A.of("y", l, 5))
                project(l, "b1", (2, 4, 2), u0 + N_IN1, lambda: pe.wait_ge(*V.of("cnormed", l)))
                project_out(l, "b1", u0 + N_IN1 + N_PROJ)
                turn_wide(wide, "f1", l, [V.of("normed", "f1", l, tb) for tb in range(TB)])
                f0 = u0 + N_IN1 + N_PROJ + N_OUT
                for (kind, j), n in FFN_UNIT.items():
                    u = f0 + n
                    pe.wait_ge(*V.of("lo", u))
                    if n == 0:
                        pe.wait_ge(*V.of("x_lo", "f1", l))
                    if kind == "down":
                        pe.wait_ge(*V.of("hidden1", l, j))
                        r = rows_split(j, n)
                    else:
                        if j >= 2:
                            pe.wait_ge(*V.of("conv", kind, l, j - 2))
                        r = features_split(banks[4 + 2 * (j % 2) + (kind == "up")], *ffn_parts(n))
                    r.then_inc(*T.done("unit", u))
                    T.same((kind, l, j), ("unit", u))

            def rotate(l, i):
                c, m = QK_PAIRS[i]
                pe.wait_ge(*V.of("qn", l, i))
                if i >= 2:
                    pe.wait_ge(*V.of("rotsin", l, i - 2))
                mm(banks[2 + i % 2][:, 0:m * SEQ], ct("rot64" if c < 9 else "rot32"), qk[:, c * SEQ:(c + m) * SEQ],
                   start=True, stop=True).then_inc(*T.done("rotated", l, i))

            def swiglu():
                for (kind, j), n in FFN_UNIT.items():
                    u = FFN_0 + n
                    pe.wait_ge(*V.of("lo", u))
                    if n == 0:
                        pe.wait_ge(*V.of("x_lo", "f2", 0))
                    if kind == "down":
                        pe.wait_ge(*V.of("dense_hidden", j))
                        r = rows_split(j, n)
                    else:
                        if j >= 2:
                            pe.wait_ge(*V.of("dense_hidden", j - 2))
                        r = features_split(banks[4 + 2 * (j % 2) + (kind == "up")], *ffn_parts(n))
                    r.then_inc(*T.done("unit", u))
                    T.same(("dense_" + kind, j), ("unit", u))

            def rwkv(l, fill, conformer):
                tc = nc.tensor
                pe.wait_ge(*A.of("tanh", l))
                for x in range(2):
                    for t in range(4):
                        r = mm(banks[2 * x + t // 2][:, (t % 2) * SEQ:(t % 2 + 1) * SEQ],
                               pr(f"lora{l}", t * P, P)[64 * x:64 * x + 64, :], wa[64 * x:64 * x + 64, :],
                               start=True, stop=True)
                    r.then_inc(*T.done("lora", l, x))
                fill(START_FILL[0])
                pe.wait_ge(*A.of("kksq", l))
                pe.wait_ge(*A.of("aa", l))
                for i in range(2):
                    mm(banks[i], ct("ones64"), flat(t3)[:, i * 512:(i + 1) * 512], start=True, stop=True)\
                        .then_inc(*T.done("kksum", l, i))
                fill(START_FILL[1])
                n = 0
                for x, src, ready in ((2, v_, V.of("shift", l, 5)), (0, b_, V.of("bn", l)), (1, k_, V.of("kt", l))):
                    pe.wait_ge(*ready)
                    for tb in range(TB):
                        if n >= 2:
                            pe.wait_ge(*A.of("tm", l, n - 2))
                        elif n == 0:
                            pe.wait_ge(*V.of("kkms", l))
                        for t in range(4):
                            r = tc.transpose(banks[2 + n % 2][:, t * P:(t + 1) * P], src[:, t, tb * P:(tb + 1) * P],
                                             ct("ident"))
                        r.then_inc(*T.done("tm", l, n))
                        n += 1
                fill(START_FILL[2])
                pe.wait_ge(*V.of("rk", l))
                for tb in range(TB):
                    for t in range(4):
                        r = mm(banks[0][:, tb * 8 + 2 * t:tb * 8 + 2 * t + 2], t0[:, t, tb * P:(tb + 1) * P],
                               ct("heads2"), start=True, stop=True)
                r.then_inc(*T.done("bonus", l))
                pe.wait_ge(*V.of("bonus", l))
                pe.wait_ge(*V.of("rt", l))
                pe.wait_ge(*V.of("at", l))
                pe.wait_ge(*A.of("tm", l, 5))
                for p in range(TB):
                    cols = slice(p * P, (p + 1) * P)
                    for h in range(8):
                        bs, t = slice(64 * (h % 2), 64 * (h % 2) + 64), h // 2
                        if h >= 2:
                            pe.wait_ge(*V.of("gram", l, p, h - 2))
                        elif p:
                            pe.wait_ge(*A.of("o", l, 1) if h == 0 else V.of("state", l, 1))
                            pe.wait_ge(*V.of("us", l, 1))
                        bank = banks[h % 2]
                        mm(bank[:, 0:128], b_[bs, t, cols], a_[bs, t, cols], start=True, stop=True)
                        mm(bank[:, 128:256], b_[bs, t, cols], r_[bs, t, cols], start=True, stop=True)
                        mm(bank[:, 256:384], k_[bs, t, cols], a_[bs, t, cols], start=True, stop=True)
                        mm(bank[:, 384:512], k_[bs, t, cols], r_[bs, t, cols], start=True, stop=True)\
                            .then_inc(*T.done("gram", l, p, h))
                        r = mm(banks[2 + h % 2][:, t * P:(t + 1) * P], a_[bs, t, cols], b_[bs, t, cols],
                               start=True, stop=True)
                        if h >= 6:
                            r.then_inc(*T.done("m", l, p, h % 2))
                    fill(GRAM_FILL)
                    for lv in range(5):
                        for g in range(2):
                            hs = range(4 * g, 4 * g + 4)
                            if lv == 0:
                                pe.wait_ge(*G.of("first", l, p, g))
                                pe.wait_ge(*V.of("gram", l, p, 7))
                            else:
                                pe.wait_ge(*V.of("inv", l, p, lv - 1, g))
                            pe.wait_ge(*G.of("off", l, p, lv, g))
                            for h in hs:
                                r = mm(banks[2 * g][:, (h % 4) * P:(h % 4 + 1) * P], off[:, h, :], tri[:, h, :],
                                       start=True, stop=True)
                            r.then_inc(*T.done("lev", l, p, lv, g))
                        for g in range(2):
                            hs = range(4 * g, 4 * g + 4)
                            pe.wait_ge(*A.of("lev", l, p, lv, g))
                            if lv < 4:
                                for h in hs:
                                    mm(banks[2 * g + 1][:, (h % 4) * P:(h % 4 + 1) * P], inv[:, h, :], lev[:, h, :],
                                       start=True, stop=True)
                            for h in hs:
                                r = mm(banks[2 * g][:, (h % 4) * P:(h % 4 + 1) * P], lev[:, h, :], inv[:, h, :],
                                       start=True, stop=True)
                            r.then_inc(*T.done("inv", l, p, lv, g))
                        if p and lv in (2, 3):
                            conformer(lv - 2)
                        if p == 0 or lv != 2:
                            fill(LEVEL_FILL)
                    for cc in range(2):
                        c = 2 * p + cc
                        ch = slice(64 * cc, 64 * cc + 64)
                        tc_ = slice(c * 64, c * 64 + 64)
                        if c == 0 or cc == 0:
                            pe.wait_ge(*V.of("inv", l, p, 4, 0))
                            pe.wait_ge(*V.of("inv", l, p, 4, 1))
                        if c:
                            pe.wait_ge(*V.of("state", l, c - 1))
                            pe.wait_ge(*A.of("o", l, c - 1))
                        for t in range(4):
                            dst = banks[0][ch, t * P:(t + 1) * P]
                            if c:
                                mm(dst, a_[:, t, tc_], state[:, t, :], start=True, stop=False)
                            for x in range(2):
                                r = mm(dst[:, x * HD:(x + 1) * HD], gram[:, 4 * x + t, 256 + 64 * cc:320 + 64 * cc],
                                       tm[:, 2, p, t * P + x * HD:t * P + (x + 1) * HD], start=(c == 0), stop=(c == 0 or x == 1))
                        r.then_inc(*T.done("x", l, c))
                        fill(CHUNK_FILL)
                        pe.wait_ge(*A.of("xs", l, c))
                        for h in range(8):
                            r = mm(banks[1][ch, h * 64:h * 64 + 64], inv[:, 4 * (h % 2) + h // 2, ch],
                                   xs[:, h * 64:h * 64 + 64], start=True, stop=True)
                        r.then_inc(*T.done("u", l, c))
                        pe.wait_ge(*V.of("us", l, c))
                        for t in range(4):
                            dst, two = banks[3][:, t * P:(t + 1) * P], slice(t * P, (t + 1) * P)
                            mm(dst, tm[ch, 0, p, two], us[ch, two], start=True, stop=False)
                            r = mm(dst, tm[ch, 1, p, two], tm[ch, 2, p, two], start=False, stop=True)
                        r.then_inc(*T.done("s", l, c))
                        for t in range(4):
                            dst = banks[2][ch, t * P:(t + 1) * P]
                            if c:
                                mm(dst, r_[:, t, tc_], state[:, t, :], start=True, stop=False)
                            for x in range(2):
                                d, hv = dst[:, x * HD:(x + 1) * HD], slice(t * P + x * HD, t * P + (x + 1) * HD)
                                mm(d, gram[:, 4 * x + t, 128 + 64 * cc:192 + 64 * cc], us[:, hv], start=(c == 0), stop=False)
                                r = mm(d, gram[:, 4 * x + t, 384 + 64 * cc:448 + 64 * cc], tm[:, 2, p, hv],
                                       start=False, stop=(c == 0 or x == 1))
                        r.then_inc(*T.done("o", l, c))
                for tb in range(TB):
                    r = mm(banks[tb], pg[:, tb * P:(tb + 1) * P], pr(f"g2{l}", 0, 512), start=True, stop=True)
                r.then_inc(*T.done("outgate", l))

            def mixer(l, u0):
                ready = [V.of("final_x", DEPTH - 1) if l == 0 else V.of("x2", 0, tb) for tb in range(TB)]
                turn_wide(xr, "b2", l, ready)

                def half(n, c):
                    u = u0 + n
                    if c == 0:
                        pe.wait_ge(*loaded(u))
                        if n >= 4:
                            pe.wait_ge(*(V.of("shift", l, n - 4) if n - 4 < 7 else A.of("in2", l, n - 4)))
                    r = features(banks[4 + n % 4], slot(u), l, (c,))
                    if c:
                        r.then_inc(*T.done("unit", u))
                for n in range(7):
                    pe.wait_ge(*V.of("lo", u0 + n))
                    if n == 0:
                        pe.wait_ge(*V.of("x_lo", "b2", l))
                    if n >= 4:
                        pe.wait_ge(*V.of("shift", l, n - 4))
                    features_split(banks[4 + n % 4], (part(mix_hi, n), slot_lo(u0 + n)), (x_hi, x_lo))\
                        .then_inc(*T.done("unit", u0 + n))
                pe.wait_ge(*A.of("xT", "b2", l))
                pe.wait_ge(*V.of("xT", "b2", l))
                fill = Filler(half, lambda n: None)
                def conformer(step):
                    bank = banks[4 + fill.next_unit() % 4]
                    if step == 0:
                        pe.wait_ge(*V.of("confconv", l))
                        pe.wait_ge(*A.of("in2", l, fill.next_unit() - 4))
                    else:
                        pe.wait_ge(*A.of("confsq", l))
                    src = (ctmp, conf)[step]
                    for i in range(2):
                        r = mm(bank[:, step * SEQ:(step + 1) * SEQ], ct("mean256"), src[:, i, :], start=(i == 0),
                               stop=(i == 1))
                    r.then_inc(*T.done(("confmean", "confvar")[step], l))
                    if step:
                        pe.wait_ge(*A.of("confrms", l))
                rwkv(l, fill, conformer)
                fill(99)
                pe.wait_ge(*A.of("confy", l))
                pe.wait_ge(*V.of("shorty", l))
                for n in range(N_IN2 - 4, N_IN2):
                    pe.wait_ge(*A.of("in2", l, n))

                def turn_rwkv():
                    pe.wait_ge(*V.of("gated", l))
                    for t in range(4):
                        for tb in range(TB):
                            r = nc.tensor.transpose(banks[t // 2][:, (t % 2) * SEQ + tb * P:(t % 2) * SEQ + (tb + 1) * P],
                                                    rwo[:, tb, t * P:(t + 1) * P], ct("ident"))
                    r.then_inc(*T.done("rwoT", l))
                    pe.wait_ge(*A.of("rwoT", l))
                project(l, "b2", (4, 2, 2), u0 + N_IN2, turn_rwkv)
                project_out(l, "b2", u0 + N_IN2 + N_PROJ)
                turn_wide(xr, "f2", l, [V.of("x1", l, tb) for tb in range(TB)])

            for l in range(min(DEPTH, n_stages)):
                block1(l)
            if n_stages >= 3:
                mixer(0, MIX2_0)
                swiglu()
            if n_stages == 4:
                mixer(1, MIX2_1)
                pe.wait_ge(*A.of("xT", "f2", 1))
                pe.wait_ge(*V.of("xT", "f2", 1))
                for tb in range(TB):
                    for k in range(KT):
                        r = mm(banks[0][:, tb * 8:tb * 8 + 8], xk[:, k, tb * P:(tb + 1) * P],
                               pr("router", k * N_EXP, N_EXP), start=(k == 0), stop=(k == KT - 1))
                r.then_inc(*T.done("router"))
                sel = sm("sel", 48).rearrange("p (b c) -> p b c", b=TB)
                pe.wait_ge(*V.of("selected"))
                mm(banks[1][:, 0:8], ct("earlier"), sel[:, 0, 0:8], start=True, stop=True)
                mm(banks[1][:, 8:16], ct("earlier"), sel[:, 1, 0:8], start=True, stop=False)
                mm(banks[1][:, 8:16], ct("ones"), sel[:, 0, 0:8], start=False, stop=True)
                mm(banks[1][:, 16:24], ct("ones"), sel[:, 0, 0:8], start=True, stop=False)
                mm(banks[1][:, 16:24], ct("ones"), sel[:, 1, 0:8], start=False, stop=True).then_inc(*T.done("places"))

                def gather():
                    for k in range(KT):
                        for tb in range(TB):
                            r = mm(banks[2 + k // 4][:, (k % 4) * P:(k % 4 + 1) * P], xr[:, tb, k * P:(k + 1) * P],
                                   pick[:, tb, :], start=(tb == 0), stop=(tb == TB - 1))
                    return r
                pe.wait_ge(*V.of("pick0"))
                gather().then_inc(*T.done("gather0"))

                def scatter(tb, out):
                    for half in range(2):
                        r = mm(out[half], pickT[:, tb * P:(tb + 1) * P], y_m[:, half * 512:(half + 1) * 512],
                               start=True, stop=True)
                    return r

                def turn(n, peeled):
                    where["turn"] = n

                    def up(kind, j):
                        i = FFN_UNIT[(kind, j)]
                        if i >= 2:
                            pe.wait_ge(*V.of("moe_lo", i))
                        else:
                            pe.wait_ge(*(V.of("first_lo", i) if peeled else V.before("moe_lo", i)))
                        for k in range(KT):
                            for a, b in ((xe_hi, w_hi), (xe_lo, w_hi), (xe_hi, w_lo)):
                                r = mm(banks[4 + (kind == "up")][:, 0:256], a[:, k, :], part(b, i)[:, k * 256:(k + 1) * 256],
                                       start=(k == 0 and a is xe_hi and b is w_hi), stop=(k == KT - 1 and b is w_lo))
                        r.then_inc(*T.done("moe_unit", i))
                        T.same((f"moe_{kind}", j), ("moe_unit", i))

                    def turn_hidden(j):
                        pe.wait_ge(*V.of("moe_hidden", j))
                        if j:
                            pe.wait_ge(*V.of("hT", j - 1))
                        for c in range(2):
                            r = nc.tensor.transpose(banks[6][:, c * P:(c + 1) * P], hid_m[:, j % 2, c * P:(c + 1) * P],
                                                    ct("ident"))
                            if c == 0 and peeled and j in SCATTER:
                                r.then_inc(*T.done("scattered", SCATTER.index(j)))
                        r.then_inc(*T.done("turned_hidden", j))

                    def down(j):
                        i = FFN_UNIT[("down", j)]
                        pe.wait_ge(*V.of("moe_lo", i))
                        pe.wait_ge(*V.of("hT", j))
                        if j == 0:
                            pe.wait_ge(*A.of("y"))
                            pe.wait_ge(*V.of("y"))
                        for c in range(2):
                            for half in range(2):
                                for a, b in ((hT_hi, w_hi), (hT_lo, w_hi), (hT_hi, w_lo)):
                                    r = mm(banks[half], a[:, j % 2, c * P:(c + 1) * P],
                                           part(b, i)[:, c * D + half * 512:c * D + (half + 1) * 512],
                                           start=(j == 0 and c == 0 and a is hT_hi and b is w_hi),
                                           stop=(j == FJ - 1 and c == 1 and b is w_lo))
                        r.then_inc(*T.done("moe_unit", i))
                        T.same(("moe_down", j), ("moe_unit", i))

                    for j in range(FJ):
                        if j == 0:
                            pe.wait_ge(*(V.of("xe0") if peeled else V.before("xe")))
                        else:
                            pe.wait_ge(*A.of("moe_silu", j - 1))
                        up("gate", j)
                        if j - 1 in SCATTER and not peeled:
                            tb = SCATTER.index(j - 1)
                            pe.wait_ge(*(V.of("acc", 0) if tb else A.before("pickT")))
                            scatter(tb, banks[2:4]).then_inc(*T.done("scattered", tb))
                        if j:
                            turn_hidden(j - 1)
                        up("up", j)
                        if j:
                            down(j - 1)
                        if j == 8:
                            pe.wait_ge(*V.of("pickw"))
                            for tb in range(TB):
                                r = nc.tensor.transpose(banks[7][:, tb * P:(tb + 1) * P], pickw[:, tb, :], ct("ident"))
                            r.then_inc(*T.done("pickT"))
                    pe.wait_ge(*V.of("pick"))
                    pe.wait_ge(*V.of("acc", 1))
                    gather().then_inc(*T.done("gather"))
                    turn_hidden(FJ - 1)
                    down(FJ - 1)
                T.enter()
                turn(0, True)
                T.again()
                load_turns(pe)
                with pe.Fori(1, where["turns"]) as n:
                    turn(n, False)
                T.leave()
                pe.wait_ge(*A.before("pickT"))
                pe.wait_ge(*A.of("last_y"))
                pe.wait_ge(*V.of("last_y"))
                for tb in range(TB):
                    scatter(tb, banks[2 + 4 * tb:4 + 4 * tb]).then_inc(*T.done("last_scattered", tb))

        @block.scalar
        def _(sc):
            act_ = nc.scalar.activation

            def xT_out(tag, l, gain):
                for k in (0, 1, 4, 5):
                    sc.wait_ge(*T.of("turned", tag, l, k | 1))
                    src = banks[k // 2][:, (k % 2) * SEQ:(k % 2 + 1) * SEQ]
                    act_(xk[:, k, :], src, ACT.Copy, scale=pr(gain, k) if gain else 1.0)\
                        .then_inc(*A.done("xT", tag, l))

            def x_hi_out(tag, l, gain, dst=x_hi):
                for k in range(KT):
                    sc.wait_ge(*T.of("turned", tag, l, k | 1))
                    act_(dst[:, k, :], banks[k // 2][:, (k % 2) * SEQ:(k % 2 + 1) * SEQ], ACT.Copy,
                         scale=pr(gain, k) if gain else 1.0).then_inc(*A.done("x_hi", tag, l, k))

            def ffn_split(f0, n):
                sc.wait_ge(*loaded(f0 + n))
                if n >= SPLIT:
                    sc.wait_ge(*T.of("unit", f0 + n - SPLIT))
                act_(part(w_hi, n), slot(f0 + n), ACT.Copy).then_inc(*A.done("hi", f0 + n))

            def with_splits(f0, evacuate):
                for n, step in enumerate(ffn_order()):
                    if n + 2 < FFN:
                        ffn_split(f0, n + 2)
                    evacuate(*step)

            def rms_sums(tag, l, ready):
                for tb in range(TB):
                    for s in ready:
                        sc.wait_ge(*s)
                    act_(junk, xr[:, tb, :], ACT.Square, accum_out=sm(f"ss{tag}", 2)[:, tb:tb + 1])\
                        .then_inc(*A.done("ss", tag, l, tb))
                    sc.wait_ge(*A.last())

            def block1(l):
                u0 = l * LAYER1
                if l == 0:
                    sc.wait_ge(s_x, 16)
                rms_sums("b1", l, [] if l == 0 else [V.of("x_out", "f1", l - 1)])

                def split(n):
                    if n < N_IN1:
                        sc.wait_ge(*loaded(u0 + n))
                        if n >= 2:
                            sc.wait_ge(*T.of("unit", u0 + n - 2))
                        act_(in_half(n), slot(u0 + n), ACT.Copy).then_inc(*A.done("hi", u0 + n))
                split(0)
                if l == 0:
                    sc.wait_ge(s_head, 32)
                x_hi_out("b1", l, f"attn_norm{l}", x1_hi)
                split(1)
                sc.wait_ge(*V.of("lamsum", l))
                act_(sm("lamexp", 2), sm("lamsum", 2), ACT.Exp).then_inc(*A.done("lamexp", l))

                def unit(n):
                    u = u0 + n
                    bank = banks[4 + n % 4]
                    sc.wait_ge(*T.of("unit", u))
                    if n == 0 and l:
                        sc.wait_ge(*V.of("merged", "b1", l - 1, 11))
                    if n in (2, 8):
                        c = 0 if n == 2 else 384
                        act_(vtm[:, :, c:c + 256], bank.rearrange("p (b n) -> p b n", b=TB), ACT.Copy)\
                            .then_inc(*A.done("in1", l, n))
                    elif n == 5:
                        act_(qk[:, 8 * SEQ:9 * SEQ], bank[:, 0:SEQ], ACT.Copy).then_inc(*A.done("q8", l))
                        act_(squares[:, 8 * SEQ:9 * SEQ], bank[:, 0:SEQ], ACT.Square).then_inc(*A.done("square", l, 8))
                        act_(msk[:, 0, 0:SEQ], bank[:, SEQ:2 * SEQ], ACT.Copy).then_inc(*A.done("in1", l, n))
                    elif n < 9:
                        c = QK_TILES[2 * n]
                        act_(squares[:, c * SEQ:(c + 2) * SEQ], bank, ACT.Square).then_inc(*A.done("square", l, c + 1))
                        act_(qk[:, c * SEQ:(c + 2) * SEQ], bank, ACT.Copy).then_inc(*A.done("in1", l, n))
                    else:
                        func, scale = (ACT.Copy, 1.0) if n < 14 else (ACT.Exp, -1.0)
                        act_(gk[:, 2 * (n - 9):2 * (n - 9) + 2, :], bank.rearrange("p (b n) -> p b n", b=2), func,
                             scale=scale).then_inc(*A.done("in1", l, n))

                for n in range(9):
                    split(n + 2)
                    unit(n)
                    if n == 7:
                        sc.wait_ge(*T.of("vb", l))
                        act_(vtm[:, :, 256:384], banks[3][:, 0:SEQ].rearrange("p (b n) -> p b n", b=TB), ACT.Copy)\
                            .then_inc(*A.done("vb", l))
                for i, (c, m) in enumerate(QK_PAIRS):
                    if i < 5:
                        split(11 + i)
                        unit(9 + i)
                    if i >= 2:
                        sc.wait_ge(*V.of("qn", l, i - 2))
                    sc.wait_ge(*T.of("sumsq", l, i))
                    act_(rs[:, i % 2, 0:m * SEQ], banks[i % 2][:, 0:m * SEQ], ACT.Sqrt, bias=sm("rms_eps", 1),
                         scale=1.0 / (HD if c < 9 else 32)).then_inc(*A.done("qrms", l, i))
                sc.wait_ge(*A.of("in1", l, 13))
                for n in range(5):
                    gv = flat(gk[:, 2 * n:2 * n + 2, :])
                    act_(gv, gv, ACT.Exp, scale=-1.0).then_inc(*A.done("gexp", l, n))
                for kind, n in SCHED:
                    if kind == "gate":
                        unit(9 + n)
                    if kind == "split":
                        split(n)
                    if kind in ("gate", "split"):
                        continue
                    br = JOBS[n][0]
                    scale = 32 ** -0.5 if br[0] == "c" else HD ** -0.5
                    if kind == "score":
                        sc.wait_ge(*V.of("negmax", l, n))
                        if n >= 3:
                            if JOBS[n - 3][0] != "c0":
                                sc.wait_ge(*T.of("turnp", l, n - 3))
                            else:
                                sc.wait_ge(*V.of("prob", l, n - 2))
                        for i, s in enumerate((slice(0, 128), slice(128, 384))):
                            act_(prob[:, n % 3, s], msk[:, n % 2, s], ACT.Exp, bias=sm(f"negmax{n % 2}", 2)[:, i:i + 1],
                                 scale=scale, accum_out=sm(f"rowsum{n % 2}", 2)[:, i:i + 1])\
                                .then_inc(*A.done("exp", l, n))
                        if br == "b":
                            act_(sm(f"sinkexp{n % 2}", 2), sm(f"negmax{n % 2}", 2), ACT.Exp,
                                 bias=pr(f"sinks{l}", JOBS[n][1])).then_inc(*A.done("exp", l, n))
                    elif kind == "turn" and br != "c0":
                        sc.wait_ge(*T.of("turnp", l, n))
                        m = [i for i in range(n - 1) if JOBS[i][0] != "c0" and i % 2 == n % 2]
                        if m:
                            sc.wait_ge(*T.of("value", l, m[-1]))
                        act_(probT[:, n % 2, :], banks[2][:, 0:384], ACT.Copy).then_inc(*A.done("probT", l, n))
                    elif kind == "value" and br != "c0" and JOBS[n][3] == 64:
                        ot = JOBS[n][2]
                        sc.wait_ge(*T.of("value", l, n))
                        if ot == 0:
                            sc.wait_ge(*T.of("rotated", l, len(QK_PAIRS) - 1))
                            sc.wait_ge(*T.of("sumsq", l, len(QK_PAIRS) - 1))
                        act_(yk[:, ot, :], banks[3][:, 0:SEQ], ACT.Copy).then_inc(*A.done("y", l, ot))
                for i in range(2):
                    sc.wait_ge(*A.of("y", l, 6 + i))
                    act_(sq[:, 0, i * SEQ:(i + 1) * SEQ], yk[:, 6 + i, :], ACT.Square).then_inc(*A.done("csquare", l, i))
                sc.wait_ge(*T.of("csum", l))
                act_(rs[:, 0, :], banks[0], ACT.Sqrt, bias=sm("rms_eps", 1), scale=1.0 / HD).then_inc(*A.done("crms", l))
                for n in range(2):
                    ffn_split(u0 + N_IN1 + N_PROJ + N_OUT, n)
                rms_sums("f1", l, [V.of("x_out", "b1", l)])
                x_hi_out("f1", l, f"mlp_norm{l}")

                def evacuate(kind, j):
                    if kind == "down":
                        return
                    dst, c0 = (cg, 0) if kind == "gate" else (cv, 22)
                    sc.wait_ge(*T.of(kind, l, j))
                    if j >= 2:
                        sc.wait_ge(*V.of("hidden1", l, j - 2))
                        sc.wait_ge(*A.of("silu1", l, j - 2))
                    if j == 0:
                        sc.wait_ge(*T.of("unit", u0 + N_IN1 + N_PROJ + N_OUT - 1))
                    for c in range(2):
                        ch = c0 + 2 * j + c
                        act_(dst[:, j % 2, c, :], banks[4 + 2 * (j % 2) + (kind == "up")][:, c * SEQ:(c + 1) * SEQ],
                             ACT.Identity, scale=pr(f"conv_w{l}", 2 * 44 + ch), bias=pr(f"conv_b{l}", ch))\
                            .then_inc(*A.done("tap2", kind, l, j))
                    if kind == "up":
                        sc.wait_ge(*V.of("conv", "gate", l, j))
                        act_(act[:, j % 2, :], flat(cg[:, j % 2, :, :]), ACT.Silu).then_inc(*A.done("silu1", l, j))
                with_splits(u0 + N_IN1 + N_PROJ + N_OUT, evacuate)

            def swiglu():
                def evacuate(kind, j):
                    if kind == "gate":
                        sc.wait_ge(*T.of("dense_gate", j))
                        if j >= 2:
                            sc.wait_ge(*V.of("dense_hidden", j - 2))
                        act_(act[:, j % 2, :], banks[4 + 2 * (j % 2)], ACT.Silu).then_inc(*A.done("dense_silu", j))
                with_splits(FFN_0, evacuate)

            def layer_norm_sums(tag, l, ready):
                for tb in range(TB):
                    sc.wait_ge(*ready[tb])
                    if tb:
                        sc.wait_ge(*A.last())
                    act_(lnjunk, xr[:, tb, :], ACT.Copy, accum_out=sm("lnsum", 2)[:, tb:tb + 1])\
                        .then_inc(*A.done("lnsum", tag, l, tb))
                for tb in range(TB):
                    sc.wait_ge(*V.of("negmean", tag, l))
                    sc.wait_ge(*A.last())
                    act_(lnjunk, xr[:, tb, :], ACT.Square, bias=sm("negmean", 2)[:, tb:tb + 1],
                         accum_out=sm("lnsq", 2)[:, tb:tb + 1]).then_inc(*A.done("lnsq", tag, l, tb))

            def mixer(l, u0):
                def split(n):
                    sc.wait_ge(*loaded(u0 + n))
                    if n >= SPLIT:
                        sc.wait_ge(*T.of("unit", u0 + n - SPLIT))
                    act_(part(mix_hi, n), slot(u0 + n), ACT.Copy).then_inc(*A.done("hi", u0 + n))
                if l == 0:
                    sc.wait_ge(*T.of("unit", MIX2_0 - 1))
                for n in range(2):
                    split(n)
                x_hi_out("b2", l, None)
                sc.wait_ge(*V.of("x_lo", "b2", l))
                xT_out("b2", l, None)

                def unit(n):
                    u = u0 + n
                    bank = banks[4 + n % 4]
                    bv = bank.rearrange("p (b n) -> p b n", b=2)
                    sc.wait_ge(*T.of("unit", u))
                    if n == 0 and l:
                        sc.wait_ge(*T.of("unit", FFN_0 + FFN - 1))
                    if n == 0 and l == 0:
                        sc.wait_ge(*V.of("conv", "up", DEPTH - 1, FJ - 1))
                    if n < 7:
                        for c in range(2):
                            act_(rkv[:, 2 * n + c, :], bank[:, c * SEQ:(c + 1) * SEQ], ACT.Identity,
                                 scale=sm(f"omu{l}", 14)[:, 2 * n + c:2 * n + c + 1]).then_inc(*A.done("unshift", l, n))
                    elif n == 8:
                        act_(conf[:, 2:4, :], bv, ACT.Sigmoid).then_inc(*A.done("in2", l, n))
                    elif n < 12:
                        dst = conf[:, 0:2, :] if n == 7 else short[:, 2 * (n - 9):2 * (n - 9) + 2, :]
                        act_(dst, bv, ACT.Copy).then_inc(*A.done("in2", l, n))
                    else:
                        act_(gk[:, 2 * (n - 12):2 * (n - 12) + 2, :], bv, ACT.Sigmoid).then_inc(*A.done("in2", l, n))
                sc.wait_ge(*V.of("omu", l))
                for n in range(7):
                    if n + 2 < 7:
                        split(n + 2)
                    unit(n)
                fill = Filler(lambda n, c: None, unit)
                sc.wait_ge(*V.of("shift", l, 6))
                act_(pg, pg, ACT.Sigmoid).then_inc(*A.done("pg", l))
                act_(wa[0:64, :], wa[0:64, :], ACT.Tanh).then_inc(*A.done("tanh", l))
                for x, dst, bias in ((0, t0, f"w0{l}"), (1, aa, f"a0{l}")):
                    sc.wait_ge(*T.of("lora", l, x))
                    for t in range(4):
                        act_(dst[:, t, :], banks[2 * x + t // 2][:, (t % 2) * SEQ:(t % 2 + 1) * SEQ], ACT.Sigmoid,
                             bias=pr(bias, t)).then_inc(*A.done("sig" if x == 0 else "aa", l))
                for t in range(4):
                    act_(t3[:, t, :], k_[:, t, :], ACT.Square, scale=pr(f"k_k{l}", t)).then_inc(*A.done("kksq", l))
                fill(START_FILL[0])
                sc.wait_ge(*V.of("kkms", l))
                act_(flat(t3), flat(t3), ACT.Sqrt).then_inc(*A.done("kknorm", l))
                sc.wait_ge(*V.of("cum", l))
                act_(flat(ep), flat(t1), ACT.Exp, scale=-KAPPA).then_inc(*A.done("ep", l))
                sc.wait_ge(*G.of("cumex", l))
                act_(flat(t2), flat(t2), ACT.Exp, scale=-KAPPA).then_inc(*A.done("ex", l))
                sc.wait_ge(*A.of("ep", l))
                act_(flat(t1), flat(t1), ACT.Exp, scale=KAPPA).then_inc(*A.done("en", l))
                fill(START_FILL[1])
                for n, x in enumerate((2, 2, 0, 0, 1, 1)):
                    sc.wait_ge(*T.of("tm", l, n))
                    act_(tm[:, x, n % 2, :], banks[2 + n % 2], ACT.Copy).then_inc(*A.done("tm", l, n))
                fill(START_FILL[2])
                for p in range(TB):
                    fill(GRAM_FILL)
                    for lv in range(5):
                        for g in range(2):
                            sc.wait_ge(*T.of("lev", l, p, lv, g))
                            act_(flat(lev[:, 4 * g:4 * g + 4, :]), banks[2 * g], ACT.Copy)\
                                .then_inc(*A.done("lev", l, p, lv, g))
                        if p and lv == 2:
                            sc.wait_ge(*V.of("confcent", l))
                            act_(conf[:, 0:2, :], ctmp, ACT.Square).then_inc(*A.done("confsq", l))
                        if p and lv == 3:
                            sc.wait_ge(*T.of("confvar", l))
                            act_(stmp[:, 0:SEQ], banks[4 + fill.next_unit() % 4][:, SEQ:2 * SEQ], ACT.Sqrt, bias=sm("ln_eps", 1))\
                                .then_inc(*A.done("confrms", l))
                        if p == 0 or lv != 2:
                            fill(LEVEL_FILL)
                    for cc in range(2):
                        c = 2 * p + cc
                        ch = slice(64 * cc, 64 * cc + 64)
                        sc.wait_ge(*T.of("x", l, c))
                        act_(xs[ch, :], banks[0][ch, :], ACT.Copy).then_inc(*A.done("xs", l, c))
                        fill(CHUNK_FILL)
                        sc.wait_ge(*T.of("o", l, c))
                        act_(rwo[ch, p, :], banks[2][ch, :], ACT.Copy).then_inc(*A.done("o", l, c))
                fill(99)
                sc.wait_ge(*V.of("confn", l))
                for i in range(2):
                    act_(yk[:, 4 + i, :], ctmp[:, i, :], ACT.Silu, scale=pr(f"conf_g{l}", i),
                         bias=pr(f"conf_lb{l}", i)).then_inc(*A.done("confy", l))
                sc.wait_ge(*T.of("rwoT", l))
                for t in range(2):
                    act_(yk[:, 2 * t:2 * t + 2, :], banks[t].rearrange("p (b n) -> p b n", b=2), ACT.Copy)\
                        .then_inc(*A.done("rwoT", l))
                if l == 0:
                    sc.wait_ge(*V.of("gated", l))
                    for n in range(2):
                        ffn_split(FFN_0, n)
                layer_norm_sums("ln1", l, [V.of("mix", l, tb) for tb in range(TB)])
                (x_hi_out if l == 0 else xT_out)("f2", l, None)

            lnjunk = Z[:, 12288:12288 + D]
            for l in range(min(DEPTH, n_stages)):
                block1(l)
            if n_stages >= 3:
                mixer(0, MIX2_0)
                swiglu()
                layer_norm_sums("ln2", 0, [V.of("res2", 0, tb) for tb in range(TB)])
            if n_stages == 4:
                mixer(1, MIX2_1)
                for i in range(2):
                    sc.wait_ge(*moe_loaded(i, 0))
                    act_(part(w_hi, i), moe_slot(i), ACT.Copy).then_inc(*A.done("first_hi", i))
                sc.wait_ge(*V.of("negtop"))
                for tb in range(TB):
                    act_(sm("wexp", 16)[:, 8 * tb:8 * tb + 8], sm("logit", 16)[:, 8 * tb:8 * tb + 8], ACT.Exp,
                         bias=sm("negtop", 2)[:, tb:tb + 1]).then_inc(*A.done("wexp"))
                sc.wait_ge(*T.of("gather0"))
                for i in range(2):
                    act_(flat(xe_hi[:, 4 * i:4 * i + 4, :]), banks[2 + i], ACT.Copy).then_inc(*A.done("xe0", i))

                def turn(n, peeled):
                    where["turn"] = n
                    order = ffn_order()

                    def hT(j):
                        sc.wait_ge(*T.of("turned_hidden", j))
                        if j >= 2:
                            sc.wait_ge(*T.of("moe_down", j - 2))
                        elif not peeled:
                            sc.wait_ge(*T.before("moe_down", FJ - 1))
                        act_(hT_hi[:, j % 2, :], banks[6][:, 0:256], ACT.Copy).then_inc(*A.done("hT", j))
                    if peeled:
                        act_(y_m[:, 0:1], ct("ones", 0, 1), ACT.Copy).then_inc(*A.done("y"))
                    else:
                        sc.wait_ge(*T.before("scattered", 1))
                        sc.wait_ge(*T.before("moe_down", FJ - 1))
                        act_(y_m[:, 0:512], banks[0], ACT.Copy).then_inc(*A.done("y"))
                    for i in range(2, FFN + 2):
                        sc.wait_ge(*(moe_loaded(i, n) if i < FFN else moe_loaded(i - FFN, n + 1)))
                        if i >= SPLIT:
                            sc.wait_ge(*T.of("moe_unit", i - SPLIT))
                        elif not peeled:
                            sc.wait_ge(*T.before("moe_unit", i + FFN - SPLIT))
                        at = i % FFN
                        act_(part(w_hi, at), moe_slot(at), ACT.Copy).then_inc(*A.done("moe_hi", at))
                        kind, j = order[i - 2]
                        if kind == "gate":
                            sc.wait_ge(*T.of("moe_gate", j))
                            if j >= 2:
                                sc.wait_ge(*V.of("moe_hidden", j - 2))
                            elif not peeled:
                                sc.wait_ge(*V.before("moe_hidden", FJ - 1))
                            act_(act_m[:, j % 2, :], banks[4][:, 0:256], ACT.Silu).then_inc(*A.done("moe_silu", j))
                            if j:
                                hT(j - 1)
                            if j == 9:
                                sc.wait_ge(*T.of("pickT"))
                                sc.wait_ge(*T.of("scattered", 1))
                                act_(pickT, banks[7][:, 0:256], ACT.Copy).then_inc(*A.done("pickT"))
                        if (kind, j) == ("down", FJ - 2):
                            sc.wait_ge(*T.of("gather"))
                            for x in range(2):
                                act_(flat(xe_hi[:, 4 * x:4 * x + 4, :]), banks[2 + x], ACT.Copy).then_inc(*A.done("xe", x))
                            hT(FJ - 1)
                A.enter()
                turn(0, True)
                A.again()
                load_turns(sc)
                with sc.Fori(1, where["turns"]) as n:
                    turn(n, False)
                A.leave()
                sc.wait_ge(*T.before("moe_down", FJ - 1))
                act_(y_m[:, 0:512], banks[0], ACT.Copy).then_inc(*A.done("last_y"))
                layer_norm_sums("ln2", 1, [V.of("res2", 1, tb) for tb in range(TB)])

        @block.vector
        def _(ve):
            v = nc.vector

            def own():
                ve.wait_ge(*V.last())

            def xT_out(tag, l, gain):
                for k in (2, 3, 6, 7):
                    ve.wait_ge(*T.of("turned", tag, l, k | 1))
                    src = banks[k // 2][:, (k % 2) * SEQ:(k % 2 + 1) * SEQ]
                    if gain:
                        v.tensor_scalar(xk[:, k, :], src, pr(gain, k), None, ALU.mult).then_inc(*V.done("xT", tag, l))
                    else:
                        v.tensor_copy(xk[:, k, :], src).then_inc(*V.done("xT", tag, l))

            def x_lo_out(tag, l, gain, hi=x_hi, lo=x_lo):
                for k in range(KT):
                    ve.wait_ge(*A.of("x_hi", tag, l, k | 1))
                    v.scalar_tensor_tensor(out=lo[:, k, :], in0=banks[k // 2][:, (k % 2) * SEQ:(k % 2 + 1) * SEQ],
                                           scalar=pr(gain, k) if gain else 1.0, in1=hi[:, k, :].bitcast(F32),
                                           op0=ALU.mult, op1=ALU.subtract).then_inc(*V.done("x_lo", tag, l))

            def ffn_split(f0, n):
                ve.wait_ge(*A.of("hi", f0 + n))
                if n >= SPLIT:
                    ve.wait_ge(*T.of("unit", f0 + n - SPLIT))
                v.tensor_tensor(part(w_lo, n), slot(f0 + n), part(w_hi, n).bitcast(F32), ALU.subtract)\
                    .then_inc(*V.done("lo", f0 + n))

            def with_splits(f0, evacuate):
                for n, step in enumerate(ffn_order()):
                    if n + 2 < FFN:
                        ffn_split(f0, n + 2)
                    evacuate(*step)

            def hidden_parts(h, j, key):
                own()
                if j >= 2:
                    ve.wait_ge(*T.of(*key[1]))
                v.tensor_copy(flat(h_hi[:, j % 2, :, :]), h).then_inc(*V.done("h_hi"))
                own()
                v.tensor_tensor(flat(h_lo[:, j % 2, :, :]), h, flat(h_hi[:, j % 2, :, :]).bitcast(F32), ALU.subtract)\
                    .then_inc(*V.done(*key[0]))

            def rms_apply(tag, l):
                ve.wait_ge(*A.of("ss", tag, l, 1))
                v.tensor_scalar(sm("ms", 2), sm(f"ss{tag}", 2), 1.0 / D, RMS_EPS, ALU.mult, ALU.add)\
                    .then_inc(*V.done("rms", tag, l))
                ve.wait_ge(*G.of("rstd", tag, l))
                for tb in range(TB):
                    v.tensor_scalar(wide[:, tb, :], xr[:, tb, :], sm("rstd", 2)[:, tb:tb + 1], None, ALU.mult)\
                        .then_inc(*V.done("normed", tag, l, tb))

            def residual(tag, l, last):
                ve.wait_ge(*last)
                for tb in range(TB):
                    for half in range(2):
                        d = xr[:, tb, half * 512:(half + 1) * 512]
                        v.tensor_tensor(d, d, banks[2 * tb + half], ALU.add).then_inc(*V.done("x_out", tag, l))

            def merge(blk, l):
                first = BRANCHES[blk][0][1]
                for n, (c, b) in enumerate(BRANCHES[blk]):
                    into, g = (flat(gk[:, 8 * x + 2 * c:8 * x + 2 * c + 2, :]) for x in (first, b))
                    ve.wait_ge(*T.of("branch", blk, l, n))
                    v.tensor_tensor(g, g, banks[4 + n % 4], ALU.mult).then_inc(*V.done("merged", blk, l, n))
                    own()
                    if b != first:
                        v.tensor_tensor(into, into, g, ALU.add).then_inc(*V.done("merged", blk, l, n))
                        own()

            def block1(l):
                u0 = l * LAYER1
                if l == 0:
                    v.memset(sm("rms_eps", 1), RMS_EPS).then_inc(*V.done("eps"))
                    v.memset(sm("ln_eps", 1), LN_EPS).then_inc(*V.done("eps"))
                    ve.wait_ge(s_head, 32)
                    ve.wait_ge(s_x, 16)
                rms_apply("b1", l)

                def split(n):
                    if n < N_IN1:
                        u = u0 + n
                        ve.wait_ge(*A.of("hi", u))
                        v.tensor_tensor(slot_lo(u), slot(u), in_half(n).bitcast(F32), ALU.subtract).then_inc(*V.done("lo", u))
                split(0)
                ve.wait_ge(*T.of("turned", "b1", l, KT - 1))
                x_lo_out("b1", l, f"attn_norm{l}", x1_hi, x1_lo)
                if l == 0:
                    ve.wait_ge(s_par, 16)
                    ve.wait_ge(s_const, 16)
                lam = pr(f"lam{l}", 0, 128)
                for i in range(2):
                    v.tensor_tensor(sm(f"lamprod{i}", 32), lam[:, 64 * i:64 * i + 32], lam[:, 64 * i + 32:64 * i + 64], ALU.mult)\
                        .then_inc(*V.done("lamprod", l))
                own()
                for i in range(2):
                    v.tensor_reduce(sm("lamsum", 2)[:, i:i + 1], sm(f"lamprod{i}", 32), AX.X, ALU.add)\
                        .then_inc(*V.done("lamsum", l))
                split(1)
                lam_init = 0.8 - 0.6 * float(np.exp(-0.3 * l))
                ve.wait_ge(*A.of("lamexp", l))
                v.scalar_tensor_tensor(out=sm("neglam", 1), in0=sm("lamexp", 2)[:, 1:2], scalar=-lam_init,
                                       in1=sm("lamexp", 2)[:, 0:1], op0=ALU.add, op1=ALU.subtract)\
                    .then_inc(*V.done("neglam", l))
                v.tensor_scalar(sm("negsink", 8), pr(f"sinks{l}", 0, 8), -1.0, None, ALU.mult).then_inc(*V.done("negsink", l))
                v.tensor_scalar(sm("sublnk", 1), pr(f"subln{l}", 0), 1.0 - lam_init, None, ALU.mult)\
                    .then_inc(*V.done("sublnk", l))
                for n in range(2, POOL_SPLIT):
                    split(n)
                def qk_norm(i):
                    c, m = QK_PAIRS[i]
                    w, dim = m * SEQ, HD if c < 9 else 32
                    b = i % 2
                    ve.wait_ge(*A.of("qrms", l, i))
                    v.reciprocal(rs[:, b, 0:w], rs[:, b, 0:w]).then_inc(*V.done("qrstd", l, i))
                    own()
                    ve.wait_ge(*A.of("in1", l, 8))
                    for j in range(m):
                        q = qk[:, (c + j) * SEQ:(c + j + 1) * SEQ]
                        v.scalar_tensor_tensor(out=q, in0=q, scalar=pr(f"q_gain{l}", c + j),
                                               in1=rs[:, b, j * SEQ:(j + 1) * SEQ], op0=ALU.mult, op1=ALU.mult)\
                            .then_inc(*V.done("qn", l, i))

                def qk_rot(i):
                    c, m = QK_PAIRS[i]
                    w, dim = m * SEQ, "64" if c < 9 else "32"
                    ve.wait_ge(*T.of("rotated", l, i))
                    if i >= 2:
                        ve.wait_ge(*G.of("roped", l, i - 2))
                    v.tensor_tensor(halves(rot[:, i % 2, 0:w]), halves(banks[2 + i % 2][:, 0:w]),
                                    grow(ct("sin" + dim), [P, m, SEQ], 1), ALU.mult)\
                        .then_inc(*V.done("rotsin", l, i))
                for i in range(len(QK_PAIRS)):
                    qk_norm(i)
                    if i:
                        qk_rot(i - 1)
                qk_rot(len(QK_PAIRS) - 1)

                def gate_recip(n):
                    ve.wait_ge(*G.of("gate1p", l, n))
                    g = flat(gk[:, 2 * n:2 * n + 2, :])
                    v.reciprocal(g, g).then_inc(*V.done("gate", l, n))
                pend = list(range(5))
                for kind, n in SCHED:
                    if kind == "gate":
                        pend.append(n)
                    if kind in ("gate", "split"):
                        if len(pend) > 1:
                            gate_recip(pend.pop(0))
                        continue
                    br, h = JOBS[n][0], JOBS[n][1]
                    scale = 32 ** -0.5 if br[0] == "c" else HD ** -0.5
                    nm, rsm, se = sm(f"negmax{n % 2}", 2), sm(f"rowsum{n % 2}", 2), sm(f"sinkexp{n % 2}", 2)
                    if kind == "score":
                        mask = ct("window" if br == "b" else "causal")
                        own()
                        ve.wait_ge(*T.of("score", l, n))
                        if n >= 2:
                            ve.wait_ge(*A.of("exp", l, n - 2))
                            ve.wait_ge(*V.of("prob", l, n - 2))
                        for i, s in enumerate((slice(0, 128), slice(128, 384))):
                            v.tensor_tensor_reduce(out=msk[:, n % 2, s], in0=banks[n % 2][:, s], in1=mask[:, s], scale=1.0,
                                                   scalar=-3.0e38, op0=ALU.add, op1=ALU.max,
                                                   accum_out=sm("rowmax", 2)[:, i:i + 1]).then_inc(*V.done("masked", l, n))
                        own()
                        if br == "b":
                            v.tensor_scalar(nm, sm("rowmax", 2), -scale, sm("negsink", 8)[:, h:h + 1], ALU.mult, ALU.min)\
                                .then_inc(*V.done("negmax", l, n))
                        else:
                            v.tensor_scalar(nm, sm("rowmax", 2), -scale, None, ALU.mult).then_inc(*V.done("negmax", l, n))
                    elif kind == "norm":
                        ve.wait_ge(*A.of("exp", l, n))
                        if br == "b":
                            v.tensor_tensor(rsm, rsm, se, ALU.add).then_inc(*V.done("den", l, n))
                            own()
                        v.reciprocal(rsm, rsm).then_inc(*V.done("rden", l, n))
                        own()
                        if br == "c1":
                            v.tensor_scalar(rsm, rsm, sm("neglam", 1), None, ALU.mult).then_inc(*V.done("rlam", l, n))
                            own()
                        for i, s in enumerate((slice(0, 128), slice(128, 384))):
                            pb = prob[:, n % 3, s]
                            if br == "c1":
                                v.scalar_tensor_tensor(out=pb, in0=pb, scalar=rsm[:, i:i + 1],
                                                       in1=prob[:, (n - 1) % 3, s], op0=ALU.mult, op1=ALU.add)\
                                    .then_inc(*V.done("prob", l, n))
                            else:
                                v.tensor_scalar(pb, pb, rsm[:, i:i + 1], None, ALU.mult).then_inc(*V.done("prob", l, n))
                        own()
                for n in pend:
                    gate_recip(n)
                ve.wait_ge(*A.of("crms", l))
                v.reciprocal(rs[:, 0, :], rs[:, 0, :]).then_inc(*V.done("crstd", l))
                own()
                for i in range(2):
                    ve.wait_ge(*A.of("csquare", l, i))
                    v.scalar_tensor_tensor(out=yk[:, 6 + i, :], in0=yk[:, 6 + i, :], scalar=sm("sublnk", 1),
                                           in1=rs[:, 0, i * SEQ:(i + 1) * SEQ], op0=ALU.mult, op1=ALU.mult)\
                        .then_inc(*V.done("cnormed", l))
                merge("b1", l)
                for n in range(2):
                    ffn_split(u0 + N_IN1 + N_PROJ + N_OUT, n)
                residual("b1", l, T.of("unit", u0 + N_IN1 + N_PROJ + N_OUT - 1))
                rms_apply("f1", l)
                x_lo_out("f1", l, f"mlp_norm{l}")

                def evacuate(kind, j):
                    if kind == "down":
                        return
                    dst, c0 = (cg, 0) if kind == "gate" else (cv, 22)
                    ve.wait_ge(*A.of("tap2", kind, l, j))
                    bank = banks[4 + 2 * (j % 2) + (kind == "up")]
                    for tap in (1, 0):
                        lag = 2 - tap
                        for c in range(2):
                            d = dst[:, j % 2, c, lag:SEQ]
                            v.scalar_tensor_tensor(out=d, in0=bank[:, c * SEQ:(c + 1) * SEQ - lag],
                                                   scalar=pr(f"conv_w{l}", tap * 44 + c0 + 2 * j + c), in1=d,
                                                   op0=ALU.mult, op1=ALU.add).then_inc(*V.done("conv", kind, l, j))
                        own()
                    if kind == "up":
                        ve.wait_ge(*A.of("silu1", l, j))
                        h = flat(hid[:, j % 2, :, :])
                        v.tensor_tensor(h, act[:, j % 2, :], flat(cv[:, j % 2, :, :]), ALU.mult).then_inc(*V.done("h"))
                        hidden_parts(h, j, (("hidden1", l, j), ("down", l, j - 2)))
                with_splits(u0 + N_IN1 + N_PROJ + N_OUT, evacuate)
                residual("f1", l, T.of("down", l, FJ - 1))
                V.steps[("final_x", l)] = V.steps[("x_out", "f1", l)]

            def swiglu():
                def evacuate(kind, j):
                    if kind == "up":
                        ve.wait_ge(*A.of("dense_silu", j))
                        ve.wait_ge(*T.of("dense_up", j))
                        h = flat(hid[:, j % 2, :, :])
                        v.tensor_tensor(h, act[:, j % 2, :], banks[4 + 2 * (j % 2) + 1], ALU.mult).then_inc(*V.done("h"))
                        hidden_parts(h, j, (("dense_hidden", j), ("dense_down", j - 2)))
                with_splits(FFN_0, evacuate)

            def layer_norm(tag, l, out_key):
                ve.wait_ge(*A.of("lnsum", tag, l, 1))
                v.tensor_scalar(sm("negmean", 2), sm("lnsum", 2), -1.0 / D, None, ALU.mult).then_inc(*V.done("negmean", tag, l))
                ve.wait_ge(s_norm_rows, 16 * (2 * l + (2 if tag == "ln2" else 1)))
                own()
                for tb in range(TB):
                    v.scalar_tensor_tensor(out=lnx[:, tb, :], in0=xr[:, tb, :], scalar=sm("negmean", 2)[:, tb:tb + 1],
                                           in1=norm_rows[:, 0:D], op0=ALU.add, op1=ALU.mult).then_inc(*V.done("lnx", tag, l))
                ve.wait_ge(*A.of("lnsq", tag, l, 1))
                v.tensor_scalar(sm("ms", 2), sm("lnsq", 2), 1.0 / D, LN_EPS, ALU.mult, ALU.add)\
                    .then_inc(*V.done("lnvar", tag, l))
                ve.wait_ge(*G.of("lnrstd", tag, l))
                own()
                for tb in range(TB):
                    v.scalar_tensor_tensor(out=xr[:, tb, :], in0=lnx[:, tb, :], scalar=sm("rstd", 2)[:, tb:tb + 1],
                                           in1=norm_rows[:, D:2 * D], op0=ALU.mult, op1=ALU.add)\
                        .then_inc(*V.done(out_key, l, tb))

            def mixer(l, u0):
                if l == 0:
                    for i in range(DEPTH):
                        v.tensor_scalar(sm(f"omu{i}", 14), pr(f"mu{i}", 0, 14), -1.0, 1.0, ALU.mult, ALU.add)\
                            .then_inc(*V.done("omu", i))
                        v.tensor_scalar(sm(f"oka{i}", 4), pr(f"k_a{i}", 0, 4), -1.0, 1.0, ALU.mult, ALU.add)\
                            .then_inc(*V.done("oka", i))

                def split(n):
                    u = u0 + n
                    ve.wait_ge(*A.of("hi", u))
                    v.tensor_tensor(slot_lo(u), slot(u), part(mix_hi, n).bitcast(F32), ALU.subtract).then_inc(*V.done("lo", u))
                own()
                for buf in (xs, us):
                    v.memset(buf, 0.0).then_inc(*V.done("zeroed"))
                split(0)
                x_lo_out("b2", l, None)
                xT_out("b2", l, None)
                split(1)
                for n in range(7):
                    if n + 2 < 7:
                        split(n + 2)
                    ve.wait_ge(*A.of("unshift", l, n))
                    for c in range(2):
                        d = rkv[:, 2 * n + c, 1:SEQ]
                        v.scalar_tensor_tensor(out=d, in0=banks[4 + n % 4][:, c * SEQ:(c + 1) * SEQ - 1],
                                               scalar=pr(f"mu{l}", 2 * n + c), in1=d, op0=ALU.mult, op1=ALU.add)\
                            .then_inc(*V.done("shift", l, n))
                own()
                for t in range(4):
                    v.tensor_scalar(kk[:, t, :], k_[:, t, :], pr(f"k_k{l}", t), None, ALU.mult).then_inc(*V.done("kkr", l))
                ve.wait_ge(*A.of("sig", l))
                for t in range(4):
                    v.tensor_tensor_scan(t1[:, t, :], ct("reset"), t0[:, t, :], 0.0, ALU.mult, ALU.add)\
                        .then_inc(*V.done("cum", l))
                for i in range(2):
                    ve.wait_ge(*T.of("kksum", l, 1))
                    v.tensor_scalar(flat(t3)[:, i * 512:(i + 1) * 512], banks[i], 1e-24, None, ALU.max)\
                        .then_inc(*V.done("kkms", l))
                ve.wait_ge(*A.of("kknorm", l))
                v.reciprocal(flat(t3), flat(t3)).then_inc(*V.done("kkrn", l))
                own()
                v.tensor_tensor(flat(kk), flat(kk), flat(t3), ALU.mult).then_inc(*V.done("kk", l))
                own()
                ve.wait_ge(*A.of("ex", l))
                v.tensor_tensor(flat(a_), flat(kk), flat(t2), ALU.mult).then_inc(*V.done("at", l))
                v.tensor_tensor(flat(kk), flat(kk), flat(aa), ALU.mult).then_inc(*V.done("ka", l))
                own()
                ve.wait_ge(*A.of("en", l))
                v.scalar_tensor_tensor(out=flat(b_), in0=flat(kk), scalar=-1.0, in1=flat(t1), op0=ALU.mult, op1=ALU.mult)\
                    .then_inc(*V.done("bn", l))
                own()
                for t in range(4):
                    v.tensor_scalar(kk[:, t, :], aa[:, t, :], pr(f"k_a{l}", t), sm(f"oka{l}", 4)[:, t:t + 1],
                                    ALU.mult, ALU.add).then_inc(*V.done("kscale", l))
                own()
                v.tensor_tensor(flat(k_), flat(k_), flat(kk), ALU.mult).then_inc(*V.done("k2", l))
                own()
                ve.wait_ge(*G.of("cumex", l))
                for t in range(4):
                    v.scalar_tensor_tensor(out=t0[:, t, :], in0=r_[:, t, :], scalar=pr(f"r_k{l}", t), in1=k_[:, t, :],
                                           op0=ALU.mult, op1=ALU.mult).then_inc(*V.done("rk", l))
                own()
                v.tensor_tensor(flat(k_), flat(k_), flat(t1), ALU.mult).then_inc(*V.done("kt", l))
                v.tensor_tensor(flat(r_), flat(r_), flat(ep), ALU.mult).then_inc(*V.done("rt", l))
                v.tensor_copy(sm("ends", 16), flat(ep).rearrange("p (c s) -> p c s", s=CHUNK)[:, :, CHUNK - 1])\
                    .then_inc(*V.done("ends", l))
                ve.wait_ge(*T.of("bonus", l))
                v.tensor_copy(sm("bonus", 16), banks[0][:, 0:16]).then_inc(*V.done("bonus", l))
                ends = sm("ends", 16).rearrange("p (t c) -> p t c", t=4)

                def conf_some(k):
                    if not started:
                        started.append(1)
                        ve.wait_ge(*A.of("in2", l, 8))
                        v.tensor_tensor(conf[:, 0:2, :], conf[:, 0:2, :], conf[:, 2:4, :], ALU.mult)\
                            .then_inc(*V.done("confu", l))
                        own()
                        for i in range(2):
                            v.tensor_scalar(ctmp[:, i, :], conf[:, i, :], pr(f"conf_dw{l}", i * 31 + 30),
                                            pr(f"conf_b{l}", i), ALU.mult, ALU.add).then_inc(*V.done("conf30", l))
                        own()
                    for _ in range(k):
                        if not taps:
                            return
                        lag = taps.pop(0)
                        for i in range(2):
                            d = ctmp[:, i, lag:SEQ]
                            v.scalar_tensor_tensor(out=d, in0=conf[:, i, 0:SEQ - lag],
                                                   scalar=pr(f"conf_dw{l}", i * 31 + 30 - lag), in1=d,
                                                   op0=ALU.mult, op1=ALU.add).then_inc(*V.done("confconv", l))
                        own()
                started, taps = [], list(range(1, CONF_TAPS))
                before = Filler(lambda n, c: None, lambda n: None)
                before(sum(START_FILL) + 2 * GRAM_FILL + 7 * LEVEL_FILL + 2 * CHUNK_FILL)
                conf_bank = banks[4 + before.next_unit() % 4]

                def heads_of(t, tb):
                    return t[:, tb, :].rearrange("p (h n) -> p h n", n=HD)

                def group_norm_start(tb):
                    og, sqv = heads_of(rwo, tb), stmp.rearrange("p (h n) -> p h n", n=HD)
                    mean, var, bonus = (sm(n, 16)[:, 8 * tb:8 * tb + 8] for n in ("gsum", "gvar", "bonus"))
                    own()
                    ve.wait_ge(*A.of("o", l, 2 * tb + 1))
                    v.tensor_reduce(mean, og, AX.X, ALU.add).then_inc(*V.done("gsum", l))
                    own()
                    v.tensor_scalar(mean, mean, 1.0 / HD, None, ALU.mult).then_inc(*V.done("gmean", l))
                    own()
                    v.tensor_tensor(og, og, grow(mean, [P, 8, HD], 2), ALU.subtract).then_inc(*V.done("gcent", l))
                    own()
                    v.tensor_tensor(sqv, og, og, ALU.mult).then_inc(*V.done("gsq", l))
                    own()
                    v.tensor_reduce(mean, sqv, AX.X, ALU.add).then_inc(*V.done("gvar", l))
                    own()
                    v.tensor_scalar(var, mean, 1.0 / HD, GN_EPS, ALU.mult, ALU.add).then_inc(*V.done("gms", l, tb))
                    ve.wait_ge(*T.of("o", l, 2 * tb + 1))
                    tmv = heads_of(tm[:, 2, :, :], tb)
                    v.tensor_tensor(tmv, tmv, grow(bonus, [P, 8, HD], 2), ALU.mult).then_inc(*V.done("bv", l))

                def group_norm_end(tb):
                    o, og = rwo[:, tb, :], heads_of(rwo, tb)
                    ve.wait_ge(*G.of("grstd", l, tb))
                    v.tensor_tensor(og, og, grow(sm("gvar", 16)[:, 8 * tb:8 * tb + 8], [P, 8, HD], 2), ALU.mult)\
                        .then_inc(*V.done("gn", l))
                    own()
                    ve.wait_ge(s_group_rows, 16 * (l + 1))
                    v.tensor_tensor(o, o, group_rows[:, 0:512], ALU.mult).then_inc(*V.done("gg", l))
                    own()
                    v.tensor_tensor(o, o, group_rows[:, 512:1024], ALU.add).then_inc(*V.done("gb", l))
                    own()
                    v.tensor_tensor(o, o, tm[:, 2, tb, :], ALU.add).then_inc(*V.done("gbonus", l))
                    own()

                def short_conv():
                    ve.wait_ge(*A.of("in2", l, 11))
                    v.tensor_tensor(short[:, 2:4, :], short[:, 2:4, :], short[:, 4:6, :], ALU.mult).then_inc(*V.done("shortu", l))
                    own()
                    for i in range(2):
                        v.tensor_scalar(short[:, 4 + i, :], short[:, 2 + i, :], pr(f"short_dw{l}", 3 * i + 2), None, ALU.mult)\
                            .then_inc(*V.done("short2", l))
                    own()
                    for lag in (1, 2):
                        for i in range(2):
                            d = short[:, 4 + i, lag:SEQ]
                            v.scalar_tensor_tensor(out=d, in0=short[:, 2 + i, 0:SEQ - lag],
                                                   scalar=pr(f"short_dw{l}", 3 * i + 2 - lag), in1=d, op0=ALU.mult,
                                                   op1=ALU.add).then_inc(*V.done("shortc", l))
                        own()
                    v.tensor_tensor(yk[:, 6:8, :], short[:, 0:2, :], short[:, 4:6, :], ALU.mult).then_inc(*V.done("shorty", l))
                for p in range(TB):
                    for h in range(8):
                        ve.wait_ge(*T.of("gram", l, p, h))
                        if h == 0 and p:
                            ve.wait_ge(*T.of("o", l, 1))
                        v.tensor_tensor(gram[:, 4 * (h % 2) + h // 2, :].rearrange("p (a n) -> p a n", a=2),
                                        banks[h % 2].rearrange("p (a n) -> p a n", a=2),
                                        grow(ct("chunk2"), [P, 2, 256], 1), ALU.mult)\
                            .then_inc(*V.done("gram", l, p, h))
                        if h >= 6:
                            g = h % 2
                            ve.wait_ge(*T.of("m", l, p, g))
                            if p == 0 and g == 0:
                                ve.wait_ge(*A.of("tm", l, 1))
                            v.tensor_tensor(tri[:, 4 * g:4 * g + 4, :], banks[2 + g].rearrange("p (h n) -> p h n", h=4),
                                            grow(ct("first"), [P, 4, P], 1), ALU.mult).then_inc(*V.done("first", l, p, g))
                    for lv in range(5):
                        for g in range(2):
                            ve.wait_ge(*T.of("inv", l, p, lv, g))
                            hs = slice(4 * g, 4 * g + 4)
                            if lv < 4:
                                v.tensor_tensor(flat(tri[:, hs, :]), flat(tri[:, hs, :]), banks[2 * g + 1],
                                                ALU.add).then_inc(*V.done("tri", l, p, lv, g))
                            v.tensor_tensor(flat(inv[:, hs, :]), flat(inv[:, hs, :]), banks[2 * g],
                                            ALU.add).then_inc(*V.done("inv", l, p, lv, g))
                            if p == 0 and lv >= 1:
                                conf_some(3)
                            if p and lv < 2:
                                conf_some(2)
                        if p == 1:
                            if lv == 0:
                                group_norm_start(0)
                            if lv == 1:
                                conf_some(99)
                                group_norm_end(0)
                            if lv == 2:
                                ve.wait_ge(*T.of("confmean", l))
                                v.tensor_tensor(ctmp, ctmp, grow(conf_bank[:, 0:SEQ], [P, 2, SEQ], 1), ALU.subtract)\
                                    .then_inc(*V.done("confcent", l))
                                short_conv()
                            if lv == 3:
                                ve.wait_ge(*T.of("confvar", l))
                                ve.wait_ge(*A.of("confrms", l))
                                v.reciprocal(stmp[:, 0:SEQ], stmp[:, 0:SEQ]).then_inc(*V.done("confrstd", l))
                                own()
                                v.tensor_tensor(ctmp, ctmp, grow(stmp[:, 0:SEQ], [P, 2, SEQ], 1), ALU.mult)\
                                    .then_inc(*V.done("confn", l))
                    for cc in range(2):
                        c = 2 * p + cc
                        ch = slice(64 * cc, 64 * cc + 64)
                        ve.wait_ge(*T.of("u", l, c))
                        v.tensor_copy(us[ch, :], banks[1][ch, :]).then_inc(*V.done("us", l, c))
                        ve.wait_ge(*T.of("s", l, c))
                        if c:
                            v.tensor_tensor(stmp, flat(state), banks[3], ALU.add).then_inc(*V.done("stmp", l, c))
                            own()
                            ve.wait_ge(*T.of("o", l, c))
                        src = stmp if c else banks[3]
                        for t in range(4):
                            v.scalar_tensor_tensor(out=state[:, t, :], in0=src[:, t * P:(t + 1) * P],
                                                   scalar=ends[:, t, c:c + 1], in1=ct("ones64"), op0=ALU.mult,
                                                   op1=ALU.mult).then_inc(*V.done("state", l, c))
                        own()
                group_norm_start(1)
                group_norm_end(1)
                ve.wait_ge(*T.of("outgate", l))
                for tb in range(TB):
                    v.tensor_tensor(rwo[:, tb, :], rwo[:, tb, :], banks[tb], ALU.mult).then_inc(*V.done("gated", l))
                for n in range(N_IN2 - 4, N_IN2):
                    ve.wait_ge(*A.of("in2", l, n))
                merge("b2", l)
                if l == 0:
                    for n in range(2):
                        ffn_split(FFN_0, n)
                ve.wait_ge(*T.of("unit", u0 + MIX2 - 1))
                for tb in range(TB):
                    for half in range(2):
                        d = xr[:, tb, half * 512:(half + 1) * 512]
                        v.scalar_tensor_tensor(out=d, in0=d, scalar=ALPHA, in1=banks[2 * tb + half], op0=ALU.mult,
                                               op1=ALU.add).then_inc(*V.done("mix", l, tb))
                own()
                layer_norm("ln1", l, "x1")
                (x_lo_out if l == 0 else xT_out)("f2", l, None)

            for l in range(min(DEPTH, n_stages)):
                block1(l)
            if n_stages >= 3:
                mixer(0, MIX2_0)
                swiglu()
                ve.wait_ge(*T.of("dense_down", FJ - 1))
                for tb in range(TB):
                    for half in range(2):
                        d = xr[:, tb, half * 512:(half + 1) * 512]
                        v.scalar_tensor_tensor(out=d, in0=d, scalar=ALPHA, in1=banks[2 * tb + half], op0=ALU.mult,
                                               op1=ALU.add).then_inc(*V.done("res2", 0, tb))
                own()
                layer_norm("ln2", 0, "x2")
            if n_stages == 4:
                mixer(1, MIX2_1)
                for i in range(2):
                    ve.wait_ge(*A.of("first_hi", i))
                    v.tensor_tensor(part(w_lo, i), moe_slot(i), part(w_hi, i).bitcast(F32), ALU.subtract)\
                        .then_inc(*V.done("first_lo", i))
                lg, wt = sm("logit", 16), sm("wexp", 16)
                gt_, eq_ = stmp[:, 0:64], stmp[:, 64:128]
                ve.wait_ge(*T.of("router"))
                v.tensor_copy(lg, banks[0][:, 0:16]).then_inc(*V.done("logit"))
                own()
                lv = lg.rearrange("p (b e) -> p b e", b=TB)
                v.tensor_reduce(sm("negtop", 2), lv, AX.X, ALU.max, negate=True).then_inc(*V.done("negtop"))
                for tb in range(TB):
                    fs = grow(lv[:, tb, :], [P, 8, 8], 1)
                    es = grow(lv[:, tb, :], [P, 8, 8], 2)
                    cmp_, eq = (m.rearrange("p (e f) -> p e f", e=8) for m in (gt_, eq_))
                    v.tensor_tensor(eq, fs, es, ALU.is_equal).then_inc(*V.done("eq"))
                    v.tensor_tensor(cmp_, fs, es, ALU.is_gt).then_inc(*V.done("gt"))
                    own()
                    v.tensor_tensor(eq_, eq_, ct("tie"), ALU.mult).then_inc(*V.done("tie"))
                    own()
                    v.tensor_tensor(gt_, gt_, eq_, ALU.add).then_inc(*V.done("rank"))
                    own()
                    v.tensor_reduce(sm("rank", 16)[:, 8 * tb:8 * tb + 8], cmp_, AX.X, ALU.add).then_inc(*V.done("rank"))
                    own()
                ve.wait_ge(*A.of("wexp"))
                sel, place, wgt = (sm(n, 48).rearrange("p (b c) -> p b c", b=TB) for n in ("sel", "place", "wgt"))
                for n in ("sel", "place", "wgt"):
                    v.memset(sm(n, 48), 0.0).then_inc(*V.done("empty"))
                own()
                rk = sm("rank", 16).rearrange("p (b e) -> p b e", b=TB)
                v.tensor_scalar(sel[:, :, 0:8], rk, 1.5, None, ALU.is_lt).then_inc(*V.done("selected"))
                own()
                wv = wt.rearrange("p (b e) -> p b e", b=TB)
                v.tensor_tensor(wv, wv, sel[:, :, 0:8], ALU.mult).then_inc(*V.done("wsel"))
                own()
                v.tensor_reduce(sm("wsum", 2), wv, AX.X, ALU.add).then_inc(*V.done("wsum"))
                own()
                v.reciprocal(sm("wsum", 2), sm("wsum", 2)).then_inc(*V.done("wrec"))
                own()
                v.tensor_tensor(wgt[:, :, 0:8], wv, grow(sm("wsum", 2), [P, TB, 8], 2), ALU.mult)\
                    .then_inc(*V.done("weights"))
                ve.wait_ge(*T.of("places"))
                v.tensor_copy(place[:, :, 0:8], banks[1][:, 0:16].rearrange("p (b e) -> p b e", b=TB))\
                    .then_inc(*V.done("place"))
                v.tensor_scalar(sm("full", 8), banks[1][:, 16:24], P + 0.5, None, ALU.is_gt).then_inc(*V.done("full"))
                own()

                def one_hot(dst, n, times, key):
                    for tb in range(TB):
                        at = bass.ds(n + 24 * tb, 1)
                        v.tensor_scalar(dst[:, tb, :], ct("slots"), sm("place", 48)[:, at], sm(times, 48)[:, at],
                                        ALU.is_equal, ALU.mult).then_inc(*V.done(key))
                ve.wait_ge(*V.of("place"))
                one_hot(pick, 0, "sel", "pick0")
                ve.wait_ge(*T.of("gather0"))

                def xe_low(ready, key):
                    for i in range(2):
                        ve.wait_ge(*A.of(ready, i))
                        v.tensor_tensor(flat(xe_lo[:, 4 * i:4 * i + 4, :]), banks[2 + i],
                                        flat(xe_hi[:, 4 * i:4 * i + 4, :]).bitcast(F32), ALU.subtract).then_inc(*V.done(key))
                xe_low("xe0", "xe0")
                v.tensor_tensor_scan(sm("nth", 8), ct("ones", 0, 8), sm("full", 8), 0.0, ALU.mult, ALU.add)\
                    .then_inc(*V.done("nth"))
                own()
                v.tensor_scalar(turn_cells[:, 0:1], sm("nth", 8)[0:1, 7:8], float(N_EXP), None, ALU.add)\
                    .then_inc(*V.done("cells"))
                v.tensor_scalar(turn_cells[:, 1 + MORE:2 + MORE], sm("nth", 8)[0:1, 7:8], 0.0, None, ALU.mult)\
                    .then_inc(*V.done("cells"))
                for q in range(MORE):
                    v.scalar_tensor_tensor(out=sm("mine", 8), in0=sm("nth", 8), scalar=q + 1.0, in1=sm("full", 8),
                                           op0=ALU.is_equal, op1=ALU.mult).then_inc(*V.done("mine"))
                    own()
                    v.tensor_tensor(sm("which", 8), sm("mine", 8), ct("slots", 0, 8), ALU.mult).then_inc(*V.done("which"))
                    own()
                    v.tensor_reduce(sm("whom", 1), sm("which", 8), AX.X, ALU.add).then_inc(*V.done("whom"))
                    own()
                    v.tensor_copy(turn_cells[:, 1 + q:2 + q], sm("whom", 1)[0:1, :]).then_inc(*V.done("cells"))
                    for table, less in ((sel, 0.0), (place, -float(P)), (wgt, 0.0)):
                        for tb in range(TB):
                            v.tensor_tensor(sm("which", 8), sm("mine", 8), table[:, tb, 0:8], ALU.mult)\
                                .then_inc(*V.done("which"))
                            own()
                            v.tensor_reduce(sm("whom", 1), sm("which", 8), AX.X, ALU.add).then_inc(*V.done("whom"))
                            own()
                            v.tensor_scalar(table[:, tb, 8 + q:9 + q], sm("whom", 1), less, None, ALU.add)\
                                .then_inc(*V.done("column"))
                            own()
                V.same(("turns",), ("column",))

                def turn(n, peeled):
                    where["turn"] = n
                    order = ffn_order()

                    def accumulate(tb):
                        ve.wait_ge(*T.of("scattered", tb))
                        for half in range(2):
                            d = moe_acc[:, tb, half * 512:(half + 1) * 512]
                            if peeled:
                                v.memset(d, 0.0).then_inc(*V.done("acc", tb))
                            else:
                                v.tensor_tensor(d, d, banks[2 + half], ALU.add).then_inc(*V.done("acc", tb))

                    def hT(j):
                        ve.wait_ge(*A.of("hT", j))
                        v.tensor_tensor(hT_lo[:, j % 2, :], banks[6][:, 0:256], hT_hi[:, j % 2, :].bitcast(F32), ALU.subtract)\
                            .then_inc(*V.done("hT", j))
                    if peeled:
                        v.memset(y_m[:, 512:513], 0.0).then_inc(*V.done("y"))
                    else:
                        ve.wait_ge(*T.before("moe_down", FJ - 1))
                        v.tensor_copy(y_m[:, 512:1024], banks[1]).then_inc(*V.done("y"))
                    for i in range(2, FFN + 2):
                        at = i % FFN
                        ve.wait_ge(*A.of("moe_hi", at))
                        v.tensor_tensor(part(w_lo, at), moe_slot(at), part(w_hi, at).bitcast(F32), ALU.subtract)\
                            .then_inc(*V.done("moe_lo", at))
                        kind, j = order[i - 2]
                        if kind == "gate" and j:
                            hT(j - 1)
                            if j - 1 in SCATTER:
                                accumulate(SCATTER.index(j - 1))
                            if j == 7:
                                if not peeled:
                                    ve.wait_ge(*T.before("pickT"))
                                one_hot(pickw, n, "wgt", "pickw")
                                ve.wait_ge(*(T.of("gather0") if peeled else T.before("gather")))
                                one_hot(pick, n + 1, "sel", "pick")
                        if kind == "up":
                            ve.wait_ge(*A.of("moe_silu", j))
                            ve.wait_ge(*T.of("moe_up", j))
                            if j >= 2:
                                ve.wait_ge(*T.of("turned_hidden", j - 2))
                            elif not peeled:
                                ve.wait_ge(*T.before("turned_hidden", FJ - 1))
                            v.tensor_tensor(hid_m[:, j % 2, :], act_m[:, j % 2, :], banks[5][:, 0:256], ALU.mult)\
                                .then_inc(*V.done("moe_hidden", j))
                        if (kind, j) == ("down", FJ - 2):
                            xe_low("xe", "xe")
                            hT(FJ - 1)
                V.enter()
                turn(0, True)
                V.again()
                load_turns(ve)
                with ve.Fori(1, where["turns"]) as n:
                    turn(n, False)
                V.leave()
                ve.wait_ge(*T.before("moe_down", FJ - 1))
                v.tensor_copy(y_m[:, 512:1024], banks[1]).then_inc(*V.done("last_y"))
                for tb in range(TB):
                    ve.wait_ge(*T.of("last_scattered", tb))
                    for half in range(2):
                        d = moe_acc[:, tb, half * 512:(half + 1) * 512]
                        v.tensor_tensor(d, d, banks[2 + 4 * tb + half], ALU.add).then_inc(*V.done("last_acc", tb))
                own()
                for tb in range(TB):
                    v.scalar_tensor_tensor(out=xr[:, tb, :], in0=xr[:, tb, :], scalar=ALPHA, in1=moe_acc[:, tb, :],
                                           op0=ALU.mult, op1=ALU.add).then_inc(*V.done("res2", 1, tb))
                own()
                layer_norm("ln2", 1, "x2")
            V.steps[("final",)] = (V.kind, V.now - V.start)

        @block.gpsimd
        def _(po):
            g = nc.gpsimd

            def own():
                po.wait_ge(*G.last())

            def power(out, in_, key):
                n = in_.shape[-1]
                g.tensor_tensor(out, in_, mh.broadcast_to([P, n]), ALU.pow).then_inc(*key)

            def rms(tag, l):
                po.wait_ge(*V.of("rms", tag, l))
                power(sm("rstd", 2), sm("ms", 2), G.done("rstd", tag, l))

            def block1(l):
                rms("b1", l)

                def roped(i):
                    c, m = QK_PAIRS[i]
                    w, dim = m * SEQ, "64" if c < 9 else "32"
                    q = qk[:, c * SEQ:(c + m) * SEQ]
                    po.wait_ge(*T.of("rotated", l, i))
                    g.tensor_tensor(halves(q), halves(q), grow(ct("cos" + dim), [P, m, SEQ], 1), ALU.mult).then_inc(*G.done("cosq", l, i))
                    own()
                    po.wait_ge(*V.of("rotsin", l, i))
                    g.tensor_tensor(q, q, rot[:, i % 2, 0:w], ALU.add).then_inc(*G.done("roped", l, i))

                def gate(n):
                    po.wait_ge(*(A.of("gexp", l, n) if n < 5 else A.of("in1", l, 9 + n)))
                    gv = flat(gk[:, 2 * n:2 * n + 2, :])
                    g.tensor_scalar(gv, gv, 1.0, None, ALU.add).then_inc(*G.done("gate1p", l, n))

                def split(n):
                    u = l * LAYER1 + n
                    po.wait_ge(*A.of("hi", u))
                    g.tensor_tensor(slot_lo(u), slot(u), in_half(n).bitcast(F32), ALU.subtract).then_inc(*G.done("lo", u))
                for i in range(len(QK_PAIRS)):
                    if i < 5:
                        split(11 + i)
                    if i:
                        roped(i - 1)
                roped(len(QK_PAIRS) - 1)
                for n in range(5):
                    gate(n)
                for kind, n in SCHED:
                    if kind == "gate":
                        gate(n)
                    if kind == "split":
                        split(n)
                rms("f1", l)

            def ln(tag, l, key):
                po.wait_ge(*V.of("lnvar", tag, l))
                power(sm("rstd", 2), sm("ms", 2), G.done("lnrstd", tag, l))
                po.wait_ge(*V.of(key, l, TB - 1))

            def load_norm_rows(l, which):
                own()
                g.dma_start(norm_rows, rows_d[l, 2 * D * which:2 * D * (which + 1)].partition_broadcast(P))\
                    .then_inc(s_norm_rows, 16)

            def load_group_rows(l):
                g.dma_start(group_rows, rows_d[l, 4 * D:4 * D + 1024].partition_broadcast(P)).then_inc(s_group_rows, 16)

            def mixer(l, u0):
                def group_rstd(tb):
                    po.wait_ge(*V.of("gms", l, tb))
                    var = sm("gvar", 16)[:, 8 * tb:8 * tb + 8]
                    power(var, var, G.done("grstd", l, tb))
                po.wait_ge(*V.of("cum", l))
                g.tensor_tensor(flat(t2), flat(t1), flat(t0), ALU.subtract).then_inc(*G.done("cumex", l))
                for p in range(TB):
                    for gg in range(2):
                        hs = slice(4 * gg, 4 * gg + 4)
                        po.wait_ge(*V.of("first", l, p, gg))
                        po.wait_ge(*V.of("gram", l, p, 6 + gg))
                        if p:
                            po.wait_ge(*T.of("o", l, 1))
                        else:
                            po.wait_ge(*V.of("bonus", l))
                            po.wait_ge(*V.of("ends", l))
                        ident4 = grow(ct("ident"), [P, 4, P], 1)
                        g.tensor_tensor(tri[:, hs, :], tri[:, hs, :], ident4, ALU.add).then_inc(*G.done("tri1", l, p, gg))
                        g.tensor_tensor(inv[:, hs, :], gram[:, hs, 0:P], grow(ct("levels", 0, P), [P, 4, P], 1), ALU.mult)\
                            .then_inc(*G.done("inv1", l, p, gg))
                        own()
                        g.tensor_tensor(inv[:, hs, :], inv[:, hs, :], ident4, ALU.add).then_inc(*G.done("first", l, p, gg))
                    for lv in range(5):
                        for gg in range(2):
                            hs = slice(4 * gg, 4 * gg + 4)
                            if lv:
                                po.wait_ge(*T.of("lev", l, p, lv - 1, gg))
                            g.tensor_tensor(off[:, hs, :], gram[:, hs, 0:P],
                                            grow(ct("levels", (lv + 1) * P, P), [P, 4, P], 1), ALU.mult).then_inc(*G.done("off", l, p, lv, gg))
                        if p and lv == 1:
                            group_rstd(0)
                group_rstd(1)
                ln("ln1", l, "x1")
                load_norm_rows(l, 1)

            g.memset(mh, -0.5).then_inc(*G.done("minus_half"))
            g.dma_start(norm_rows, rows_d[0, 0:2 * D].partition_broadcast(P)).then_inc(s_norm_rows, 16)
            load_group_rows(0)
            own()
            for l in range(min(DEPTH, n_stages)):
                block1(l)
            if n_stages >= 3:
                mixer(0, MIX2_0)
                po.wait_ge(*V.of("gb", 0))
                load_group_rows(1)
                ln("ln2", 0, "x2")
            if n_stages == 4:
                load_norm_rows(1, 0)
                mixer(1, MIX2_1)
                load_turns(po)
                ln("ln2", 1, "x2")
            G.steps[("final",)] = (G.kind, G.now - G.start)

    return {"matmul_done": T.steps, "scalar_done": A.steps, "vector_done": V.steps, "pool_done": G.steps}


def constants():
    f = np.float32
    c = {}
    i, j = np.meshgrid(np.arange(P), np.arange(P), indexing="ij")
    c["ident"] = (i == j).astype(f)
    c["ones64"] = (i // 64 == j // 64).astype(f)
    c["ones32"] = (i // 32 == j // 32).astype(f)
    c["mean256"] = np.full((P, P), 1.0 / 256, f)
    for dim in (64, 32):
        half = dim // 2
        rot = np.zeros((P, P), f)
        for m in range(P):
            if m % dim < half:
                rot[m + half, m] = -1.0
            else:
                rot[m - half, m] = 1.0
        c[f"rot{dim}"] = rot
        inv = (f(1.0) / np.power(f(10000.0), np.arange(0, dim, 2, dtype=f) / f(dim))).astype(f)
        ang = np.arange(SEQ, dtype=f)[None, :] * inv[np.arange(P) % half][:, None]
        c[f"cos{dim}"] = np.cos(ang).astype(f)
        c[f"sin{dim}"] = np.sin(ang).astype(f)
    causal = np.where(j <= i, 0.0, -BIG).astype(f)
    c["causal"] = np.concatenate([causal, np.zeros((P, P), f), causal], 1)
    c["window"] = np.concatenate([causal, np.where(j > i, 0.0, -BIG).astype(f), causal], 1)
    same = i // CHUNK == j // CHUNK
    strict, upto = (same & (i < j)).astype(f), (same & (i <= j)).astype(f)
    c["chunk2"] = np.concatenate([strict, upto], 1)
    c["earlier"] = (i < j).astype(f)
    c["slots"] = j.astype(f)
    c["ones"] = np.ones((P, P), f)

    def level(n, lo, hi):
        return ((lo // (2 * n) == hi // (2 * n)) & (lo % (2 * n) < n) & (hi % (2 * n) >= n)).astype(f)
    c["first"] = level(1, j, i)
    c["levels"] = np.concatenate([level(n, i, j) for n in (1, 2, 4, 8, 16, 32)], 1)
    c["heads2"] = (i[:, 0:2] // 64 == j[:, 0:2]).astype(f)
    c["reset"] = np.tile((np.arange(SEQ) % CHUNK != 0).astype(f), (P, 1))
    e, g = np.meshgrid(np.arange(8), np.arange(8), indexing="ij")
    c["tie"] = np.tile((g < e).astype(f).reshape(1, 64), (P, 1))
    return pack(CST, c)


def pack(names, arrays):
    out = np.zeros((P, names.size), np.float32)
    for name, (a, w) in names.at.items():
        out[:, a:a + w] = arrays[name]
    return out


def columns(v):
    return v.reshape(-1, P).T


def features_units(w):
    return w.reshape(KT, P, -1, 256).transpose(2, 1, 0, 3).reshape(-1, P, UNIT)


def rows_units(w):
    return w.reshape(-1, 2, P, D).transpose(0, 2, 1, 3).reshape(-1, P, UNIT)


HEAD_ORDER = [(h // 2) + 4 * (h % 2) for h in range(8)]


def lay_out(x):
    stream, par = np.empty((N_UNITS, P, UNIT), np.float32), {}
    at = [0]

    def put(u):
        stream[at[0]:at[0] + len(u)] = u
        at[0] += len(u)

    def put_ffn(gate, up, down):
        gate, up, down = features_units(gate), features_units(up), rows_units(down)
        for kind, j in ffn_order():
            put({"gate": gate, "up": up, "down": down}[kind][j:j + 1])

    for l in range(DEPTH):
        w = np.array(x["w_in"][l])
        w[:, 768:1280] = w[:, 768:1280].reshape(D, 8, HD)[:, HEAD_ORDER, :].reshape(D, 512)
        put(features_units(w))
        put(rows_units(x["w_pa"][l]))
        put(rows_units(x["w_pb"][l].reshape(8, HD, D)[HEAD_ORDER].reshape(512, D)))
        put(rows_units(x["w_pc"][l]))
        put(rows_units(x["w_out"][l]))
        put_ffn(x["w_up"][l][:, :FF], x["w_up"][l][:, FF:], x["w_down"][l])
        par[f"attn_norm{l}"] = columns(x["attn_norm"][l])
        par[f"mlp_norm{l}"] = columns(x["mlp_norm"][l])
        two = lambda n: np.tile(x[n][l], 2).reshape(P, 1)
        four = lambda n: np.tile(x[n][l], 4).reshape(P, 1)
        par[f"q_gain{l}"] = np.concatenate([two("qn_a")] * 2 + [two("kn_a")] * 2 + [two("qn_b")] * 4 + [two("kn_b")]
                                           + [four("qn_c")] * 2 + [four("kn_c")] * 2, 1)
        par[f"subln{l}"] = two("subln")
        par[f"sinks{l}"] = np.tile(x["sinks"][l].reshape(1, 8), (P, 1))
        lam = np.concatenate([x[n][l] for n in ("lam_q1", "lam_k1", "lam_q2", "lam_k2")])
        par[f"lam{l}"] = np.tile(lam.reshape(1, 128), (P, 1))
        par[f"conv_w{l}"] = x["conv_w"][l].reshape(3, 44, P).transpose(2, 0, 1).reshape(P, 132)
        par[f"conv_b{l}"] = columns(x["conv_b"][l])
    for l in range(DEPTH):
        put(features_units(x["w_in_2"][l]))
        for n in ("rwkv_w_o_2", "conf_w_o_2", "short_w_o_2", "w_out_2"):
            put(rows_units(x[n][l]))
        if l == 0:
            put_ffn(x["ffn_w_gate_2"][0], x["ffn_w_up_2"][0], x["ffn_w_down_2"][0])
        else:
            for e in range(N_EXP):
                put_ffn(x["moe_w_gate_2"][0, e], x["moe_w_up_2"][0, e], x["moe_w_down_2"][0, e])
        for name, n in (("mu", "rwkv_mu_2"), ("w0", "rwkv_w0_2"), ("a0", "rwkv_a0_2"), ("k_k", "rwkv_k_k_2"),
                        ("k_a", "rwkv_k_a_2"), ("r_k", "rwkv_r_k_2"), ("conf_b", "conf_dw_b_2"),
                        ("conf_g", "conf_ln_g_2"), ("conf_lb", "conf_ln_b_2")):
            par[f"{name}{l}"] = columns(x[n][l].reshape(-1))
        par[f"conf_dw{l}"] = x["conf_dw_2"][l].reshape(31, 2, P).transpose(2, 1, 0).reshape(P, 62)
        par[f"short_dw{l}"] = x["short_dw_2"][l].reshape(3, 2, P).transpose(2, 1, 0).reshape(P, 6)
        par[f"lora{l}"] = np.concatenate([x["rwkv_w2_2"][l], x["rwkv_a2_2"][l]], 0)
        par[f"g2{l}"] = x["rwkv_g2_2"][l]
    par["router"] = x["moe_router_2"][0].reshape(KT, P, N_EXP).transpose(1, 0, 2).reshape(P, KT * N_EXP)
    assert at[0] == N_UNITS
    rows = np.stack([np.concatenate([x[n][l] for n in ("ln1_g_2", "ln1_b_2", "ln2_g_2", "ln2_b_2", "rwkv_ln_g_2",
                                                       "rwkv_ln_b_2")]) for l in range(DEPTH)])
    return {"stream": stream, "par": pack(PAR, par), "cst": constants(), "rows": rows, "x": x["x"][0]}


N_STAGES = 4


def kernel(**inputs):
    import concourse.bacc as _bacc
    from concourse.bass_utils import run_bass_kernel_spmd as _run

    arrays = lay_out({n: np.asarray(a) for n, a in inputs.items()})
    known = {}
    for _ in range(2):
        nc = _bacc.Bacc("TRN2", target_bir_lowering=False, num_devices=1)
        d = {n: nc.dram_tensor(f"in_{n}", a.shape, F32, kind="ExternalInput").ap() for n, a in arrays.items()}
        out = nc.dram_tensor("out", (SEQ, D), F32, kind="ExternalOutput").ap()
        learned = known
        known = emit(nc, known, d["stream"], d["par"], d["cst"], d["rows"], d["x"], out, N_STAGES)
    assert known == learned
    r = _run(nc, [{f"in_{n}": a for n, a in arrays.items()}], core_ids=[0])
    return r.results[0]["out"].reshape(1, SEQ, D)
```
